# Optimizing a Trainium2 kernel written in Bass

```python
import jax, jax.numpy as jnp
from jax import lax
import numpy as np
import math

D_MODEL = 1024
BATCH = 1
SEQ = 256
DEPTH = 2

CHUNK = 64
N_LEFT_CHUNKS = 8
BAND = (N_LEFT_CHUNKS + 1) * CHUNK
HEAD_DIM = 64
N_HEADS_A = 8
N_HEADS_B = 8
A_W = N_HEADS_A * HEAD_DIM
B_W = N_HEADS_B * HEAD_DIM
MIX_W = A_W + B_W
REL_CLIP = 256
Q_BLOCK = 128
LRU_WIDTH = D_MODEL
LRU_BLOCKS = 4
LRU_BLOCK_W = LRU_WIDTH // LRU_BLOCKS
CONV_WIDTH = 4
LRU_C = 8.0
D_FF = -(-(8 * D_MODEL) // (3 * 256)) * 256
RMS_EPS = 1e-6
N_ATTN_LAYERS = (DEPTH + 1) // 2
N_REC_LAYERS = DEPTH // 2


def rmsnorm(x, g):
    xf = x.astype(jnp.float32)
    y = xf * lax.rsqrt(jnp.mean(xf * xf, axis=-1, keepdims=True) + RMS_EPS)
    return (y * g.astype(jnp.float32)).astype(x.dtype)

def chunked_relpos_attention(q, k, v, rel_bias):
    b, s, h, dh = q.shape
    nc = s // CHUNK
    qc = q.reshape(b, nc, CHUNK, h, dh)

    def gather_band(t):
        tc = t.reshape(b, nc, CHUNK, h, dh)
        tp = jnp.pad(tc, ((0, 0), (N_LEFT_CHUNKS, 0), (0, 0), (0, 0), (0, 0)))
        return jnp.concatenate([tp[:, j:j + nc] for j in range(N_LEFT_CHUNKS + 1)], axis=2)

    kb, vb = gather_band(k), gather_band(v)
    scores = jnp.einsum('bcqhd,bckhd->bhcqk', qc, kb).astype(jnp.float32) * (dh ** -0.5)
    qpos = N_LEFT_CHUNKS * CHUNK + jnp.arange(CHUNK)
    kpos = jnp.arange(BAND)
    rel = jnp.clip(qpos[:, None] - kpos[None, :], -REL_CLIP, REL_CLIP) + REL_CLIP
    bias = rel_bias[:, rel].astype(jnp.float32)
    key_chunk = jnp.arange(nc)[:, None] - N_LEFT_CHUNKS + (kpos // CHUNK)[None, :]
    valid = key_chunk >= 0
    scores = scores + bias[None, :, None, :, :]
    scores = jnp.where(valid[None, None, :, None, :], scores, -jnp.inf)
    p = jax.nn.softmax(scores, axis=-1).astype(v.dtype)
    o = jnp.einsum('bhcqk,bckhd->bcqhd', p, vb)
    return o.reshape(b, s, h * dh)

def stick_breaking_attention(q, k, v):
    b, s, h, dh = q.shape
    nb = s // Q_BLOCK
    scale = dh ** -0.5
    kpos = jnp.arange(s)
    q_blocks = q.reshape(b, nb, Q_BLOCK, h, dh).transpose(1, 0, 2, 3, 4)

    def one_block(args):
        q_blk, blk = args
        z = jnp.einsum('bqhd,bkhd->bhqk', q_blk, k).astype(jnp.float32) * scale
        qpos = blk * Q_BLOCK + jnp.arange(Q_BLOCK)
        causal = kpos[None, :] < qpos[:, None]
        log_beta = jax.nn.log_sigmoid(z)
        log_1m_beta = jnp.where(causal, jax.nn.log_sigmoid(-z), 0.0)
        after = lax.cumsum(log_1m_beta, axis=3, reverse=True) - log_1m_beta
        w = jnp.where(causal, jnp.exp(log_beta + after), 0.0).astype(v.dtype)
        return jnp.einsum('bhqk,bkhd->bqhd', w, v)

    o = lax.map(one_block, (q_blocks, jnp.arange(nb)))
    return o.transpose(1, 0, 2, 3, 4).reshape(b, s, h * dh)

def attention_mixer(h, w_in, rel_bias, w_out):
    b, s, _ = h.shape
    proj = h @ w_in
    part_a, part_b = proj[..., :3 * A_W], proj[..., 3 * A_W:]
    qa, ka, va = [t.reshape(b, s, N_HEADS_A, HEAD_DIM) for t in jnp.split(part_a, 3, axis=-1)]
    qs, ks, vs = [t.reshape(b, s, N_HEADS_B, HEAD_DIM) for t in jnp.split(part_b, 3, axis=-1)]
    out_a = chunked_relpos_attention(qa, ka, va, rel_bias)
    out_b = stick_breaking_attention(qs, ks, vs)
    return jnp.concatenate([out_a, out_b], axis=-1) @ w_out

def recurrent_mixer(h, w_in, conv_w, conv_b, w_a, b_a, w_i, b_i, lam, w_out):
    b, s, _ = h.shape
    proj = h @ w_in
    gate, xr = jnp.split(proj, 2, axis=-1)
    gate = jax.nn.gelu(gate, approximate=True)
    xc = lax.conv_general_dilated(
        xr, conv_w, window_strides=(1,), padding=[(CONV_WIDTH - 1, 0)],
        dimension_numbers=('NWC', 'WIO', 'NWC'), feature_group_count=LRU_WIDTH) + conv_b
    xg = xc.reshape(b, s, LRU_BLOCKS, LRU_BLOCK_W)
    r = jax.nn.sigmoid(jnp.einsum('bsni,nij->bsnj', xg, w_a) + b_a).reshape(b, s, LRU_WIDTH)
    i = jax.nn.sigmoid(jnp.einsum('bsni,nij->bsnj', xg, w_i) + b_i).reshape(b, s, LRU_WIDTH)
    log_a = -LRU_C * r.astype(jnp.float32) * jax.nn.softplus(-lam.astype(jnp.float32))
    a = jnp.exp(log_a)
    mult = jnp.sqrt(-jnp.expm1(2.0 * log_a))
    u = mult * (i * xc).astype(jnp.float32)

    def combine(left, right):
        a1, b1 = left
        a2, b2 = right
        return a1 * a2, a2 * b1 + b2

    _, hs = lax.associative_scan(combine, (a, u), axis=1)
    return (hs.astype(h.dtype) * gate) @ w_out

def swiglu(h, w_gate, w_up, w_down):
    return (jax.nn.silu(h @ w_gate) * (h @ w_up)) @ w_down

def first_inputs(seed: int = 0) -> dict:
    key = jax.random.key(seed)
    ks = jax.random.split(key, 24)
    f32 = jnp.float32

    def nrm(k, shape, fan_in):
        return jax.random.normal(k, shape, f32) * (fan_in ** -0.5)

    def gain(k, shape):
        return 1.0 + 0.05 * jax.random.normal(k, shape, f32)

    u = jax.random.uniform(ks[12], (N_REC_LAYERS, LRU_WIDTH), f32, 0.9, 0.999)
    base = u ** (1.0 / LRU_C)
    lam = jnp.log(base) - jnp.log1p(-base)
    return {
        'x': jax.random.normal(ks[0], (BATCH, SEQ, D_MODEL), f32),
        'attn_w_in': nrm(ks[1], (N_ATTN_LAYERS, D_MODEL, 3 * MIX_W), D_MODEL),
        'attn_rel_bias': 0.2 * jax.random.normal(ks[2], (N_ATTN_LAYERS, N_HEADS_A, 2 * REL_CLIP + 1), f32),
        'attn_w_out': nrm(ks[3], (N_ATTN_LAYERS, MIX_W, D_MODEL), MIX_W),
        'rg_w_in': nrm(ks[4], (N_REC_LAYERS, D_MODEL, 2 * LRU_WIDTH), D_MODEL),
        'rg_conv_w': nrm(ks[5], (N_REC_LAYERS, CONV_WIDTH, 1, LRU_WIDTH), CONV_WIDTH),
        'rg_conv_b': 0.01 * jax.random.normal(ks[6], (N_REC_LAYERS, LRU_WIDTH), f32),
        'rg_w_a': nrm(ks[7], (N_REC_LAYERS, LRU_BLOCKS, LRU_BLOCK_W, LRU_BLOCK_W), LRU_BLOCK_W),
        'rg_b_a': 0.01 * jax.random.normal(ks[8], (N_REC_LAYERS, LRU_BLOCKS, LRU_BLOCK_W), f32),
        'rg_w_i': nrm(ks[9], (N_REC_LAYERS, LRU_BLOCKS, LRU_BLOCK_W, LRU_BLOCK_W), LRU_BLOCK_W),
        'rg_b_i': 0.01 * jax.random.normal(ks[10], (N_REC_LAYERS, LRU_BLOCKS, LRU_BLOCK_W), f32),
        'rg_lambda': lam,
        'rg_w_out': nrm(ks[11], (N_REC_LAYERS, LRU_WIDTH, D_MODEL), LRU_WIDTH),
        'norm_mix_pre': gain(ks[13], (DEPTH, D_MODEL)),
        'norm_mix_post': gain(ks[14], (DEPTH, D_MODEL)),
        'norm_ffn_pre': gain(ks[15], (DEPTH, D_MODEL)),
        'norm_ffn_post': gain(ks[16], (DEPTH, D_MODEL)),
        'ffn_w_gate': nrm(ks[17], (DEPTH, D_MODEL, D_FF), D_MODEL),
        'ffn_w_up': nrm(ks[18], (DEPTH, D_MODEL, D_FF), D_MODEL),
        'ffn_w_down': nrm(ks[19], (DEPTH, D_FF, D_MODEL), D_FF),
    }

def first_block(x, attn_w_in, attn_rel_bias, attn_w_out, rg_w_in, rg_conv_w, rg_conv_b,
              rg_w_a, rg_b_a, rg_w_i, rg_b_i, rg_lambda, rg_w_out,
              norm_mix_pre, norm_mix_post, norm_ffn_pre, norm_ffn_post,
              ffn_w_gate, ffn_w_up, ffn_w_down):
    for layer in range(DEPTH):
        j = layer // 2
        h = rmsnorm(x, norm_mix_pre[layer])
        if layer % 2 == 0:
            m = attention_mixer(h, attn_w_in[j], attn_rel_bias[j], attn_w_out[j])
        else:
            m = recurrent_mixer(h, rg_w_in[j], rg_conv_w[j], rg_conv_b[j], rg_w_a[j], rg_b_a[j],
                                rg_w_i[j], rg_b_i[j], rg_lambda[j], rg_w_out[j])
        x = x + rmsnorm(m, norm_mix_post[layer])
        h = rmsnorm(x, norm_ffn_pre[layer])
        f = swiglu(h, ffn_w_gate[layer], ffn_w_up[layer], ffn_w_down[layer])
        x = x + rmsnorm(f, norm_ffn_post[layer])
    return x


N_ATTN_HEADS = D_MODEL // HEAD_DIM
N_DIFF_HEADS = N_ATTN_HEADS // 4
DIL_GROUPS = ((128, 1), (512, 4), (2048, 16))
HEADS_PER_DIL = (N_ATTN_HEADS - N_DIFF_HEADS) // len(DIL_GROUPS)
N_DIL_HEADS = HEADS_PER_DIL * len(DIL_GROUPS)
DIL_WIDTH = N_DIL_HEADS * HEAD_DIM
DIFF_QK_DIM = HEAD_DIM // 2
DIFF_QK_WIDTH = N_DIFF_HEADS * 2 * DIFF_QK_DIM
DIFF_V_WIDTH = N_DIFF_HEADS * HEAD_DIM
ATTN_IN_WIDTH = 3 * DIL_WIDTH + 2 * DIFF_QK_WIDTH + DIFF_V_WIDTH
ATTN_SPLITS = [DIL_WIDTH, 2 * DIL_WIDTH, 3 * DIL_WIDTH,
               3 * DIL_WIDTH + DIFF_QK_WIDTH, 3 * DIL_WIDTH + 2 * DIFF_QK_WIDTH]
BLOCK = 128
HGRN_HEADS = 8
HGRN_EXPAND = 128
HGRN_FORGET_DIM = HGRN_HEADS * HGRN_EXPAND
HGRN_VDIM = D_MODEL // HGRN_HEADS
HGRN_CHUNK = 64
HGRN_IN_WIDTH = 2 * HGRN_FORGET_DIM + 2 * D_MODEL
D_FF_2 = 2816
N_EXPERTS = 8
TOP_K = 2
D_FF_EXPERT = 3584
N_EVEN = (DEPTH + 1) // 2
N_ODD = DEPTH // 2
EPS = 1e-6
NEG_INF = -1e30
F32 = jnp.float32


def rms_norm(x, gain):
    xf = x.astype(F32)
    y = xf * lax.rsqrt(jnp.mean(xf * xf, axis=-1, keepdims=True) + EPS)
    return (y * gain.astype(F32)).astype(x.dtype)

def alibi_slopes(n):
    return 2.0 ** (-8.0 * (jnp.arange(n, dtype=F32) + 1.0) / n)

def dilated_window_attention(q, k, v, slopes, window, dilation):
    B, S, H, Dh = q.shape
    span = window // dilation
    assert span <= BLOCK
    n_blk = -(-S // (dilation * BLOCK))
    Lp = n_blk * dilation * BLOCK

    def to_classes(t):
        t = jnp.pad(t, ((0, 0), (0, Lp - S), (0, 0), (0, 0)))
        t = t.reshape(B, Lp // dilation, dilation, H, Dh).transpose(0, 2, 1, 3, 4)
        return t.reshape(B, dilation, n_blk, BLOCK, H, Dh)

    def with_prev(t):
        prev = jnp.pad(t[:, :, :-1], ((0, 0), (0, 0), (1, 0), (0, 0), (0, 0), (0, 0)))
        return jnp.concatenate([prev, t], axis=3)

    qc = to_classes(q)
    kb = with_prev(to_classes(k))
    vb = with_prev(to_classes(v))
    step = jnp.arange(BLOCK)[:, None] + BLOCK - jnp.arange(2 * BLOCK)[None, :]
    not_before_start = (jnp.arange(n_blk)[:, None, None] > 0) | (jnp.arange(2 * BLOCK)[None, None, :] >= BLOCK)
    valid = (step >= 0) & (step <= span) & not_before_start
    bias = -slopes[:, None, None] * (step * dilation).astype(F32)
    s = jnp.einsum('brnqhd,brnkhd->brnhqk', qc, kb).astype(F32) * (Dh ** -0.5) + bias
    s = jnp.where(valid[None, None, :, None], s, NEG_INF)
    lse = jax.nn.logsumexp(s, axis=-1)
    p = jnp.exp(s - lse[..., None])
    o = jnp.einsum('brnhqk,brnkhd->brnqhd', p, vb.astype(F32))

    def from_classes(t):
        X = t.shape[-1]
        t = t.reshape(B, dilation, Lp // dilation, H, X).transpose(0, 2, 1, 3, 4)
        return t.reshape(B, Lp, H, X)[:, :S]

    lse_pos = from_classes(jnp.swapaxes(lse, -1, -2)[..., None])[..., 0]
    return from_classes(o), lse_pos

def differential_attention(q1, q2, k1, k2, v, slopes, lam):
    B, S, H, dk = q1.shape
    n_blk = S // BLOCK
    scale = dk ** -0.5
    kpos = jnp.arange(S)
    vf = v.astype(F32)

    def one_block(args):
        qb1, qb2, blk = args
        dist = (blk * BLOCK + jnp.arange(BLOCK))[:, None] - kpos[None, :]
        causal = dist >= 0
        bias = -slopes[:, None, None] * dist.astype(F32)

        def probs(qb, kk):
            s = jnp.einsum('bqhd,bkhd->bhqk', qb, kk).astype(F32) * scale + bias
            return jax.nn.softmax(jnp.where(causal, s, NEG_INF), axis=-1)

        a = probs(qb1, k1) - lam * probs(qb2, k2)
        return jnp.einsum('bhqk,bkhd->bqhd', a, vf)

    to_blocks = lambda t: t.reshape(B, n_blk, BLOCK, H, dk).transpose(1, 0, 2, 3, 4)
    out = lax.map(one_block, (to_blocks(q1), to_blocks(q2), jnp.arange(n_blk)))
    return out.transpose(1, 0, 2, 3, 4).reshape(B, S, H, 2 * dk)

def dilated_diff_mixer(u, w_in, dil_q_gain, dil_k_gain, diff_q_gain, diff_k_gain,
                       lam_q1, lam_k1, lam_q2, lam_k2, diff_out_gain, w_out, layer):
    B, S, _ = u.shape
    dq, dk, dv, fq, fk, fv = jnp.split(u @ w_in, ATTN_SPLITS, axis=-1)
    slopes = alibi_slopes(N_ATTN_HEADS)
    dq = rms_norm(dq.reshape(B, S, N_DIL_HEADS, HEAD_DIM), dil_q_gain)
    dk = rms_norm(dk.reshape(B, S, N_DIL_HEADS, HEAD_DIM), dil_k_gain)
    dv = dv.reshape(B, S, N_DIL_HEADS, HEAD_DIM)
    outs, lses = [], []
    for g, (window, dilation) in enumerate(DIL_GROUPS):
        hs = slice(g * HEADS_PER_DIL, (g + 1) * HEADS_PER_DIL)
        o, lse = dilated_window_attention(dq[:, :, hs], dk[:, :, hs], dv[:, :, hs], slopes[hs], window, dilation)
        outs.append(o)
        lses.append(lse)
    alpha = jax.nn.softmax(jnp.stack(lses), axis=0)
    dil_out = jnp.concatenate([alpha[g][..., None] * outs[g] for g in range(len(DIL_GROUPS))], axis=2)
    fq = rms_norm(fq.reshape(B, S, N_DIFF_HEADS, 2, DIFF_QK_DIM), diff_q_gain)
    fk = rms_norm(fk.reshape(B, S, N_DIFF_HEADS, 2, DIFF_QK_DIM), diff_k_gain)
    fv = fv.reshape(B, S, N_DIFF_HEADS, HEAD_DIM)
    lam_init = 0.8 - 0.6 * math.exp(-0.3 * layer)
    lam = (jnp.exp(jnp.sum(lam_q1.astype(F32) * lam_k1.astype(F32)))
           - jnp.exp(jnp.sum(lam_q2.astype(F32) * lam_k2.astype(F32))) + lam_init)
    diff = differential_attention(fq[..., 0, :], fq[..., 1, :], fk[..., 0, :], fk[..., 1, :],
                                  fv, slopes[N_DIL_HEADS:], lam)
    diff = rms_norm(diff, diff_out_gain) * (1.0 - lam_init)
    mixed = jnp.concatenate([dil_out, diff], axis=2).reshape(B, S, D_MODEL).astype(u.dtype)
    return mixed @ w_out

def chunk_gated_recurrence(q, k, v, log_f):
    B, S, H, K = q.shape
    V = v.shape[-1]
    C = HGRN_CHUNK
    n = S // C
    rs = lambda t: t.reshape(B, n, C, H, t.shape[-1]).transpose(1, 0, 3, 2, 4)
    q, k, v, lf = rs(q), rs(k), rs(v), rs(log_f)
    b = jnp.cumsum(lf, axis=-2)
    b_last = b[..., -1:, :]
    b_mid = b[..., C // 2:C // 2 + 1, :]
    scores = jnp.einsum('nbhtk,nbhsk->nbhts', q * jnp.exp(b - b_mid), k * jnp.exp(b_mid - b))
    causal = jnp.tril(jnp.ones((C, C), dtype=bool))
    o_intra = jnp.einsum('nbhts,nbhsv->nbhtv', jnp.where(causal, scores, 0.0), v)
    q_inter = q * jnp.exp(b)
    k_state = k * jnp.exp(b_last - b)
    chunk_decay = jnp.exp(b_last[..., 0, :])

    def step(state, xs):
        qi, ks, vc, dec = xs
        o = jnp.einsum('bhtk,bhkv->bhtv', qi, state)
        state = dec[..., None] * state + jnp.einsum('bhsk,bhsv->bhkv', ks, vc)
        return state, o

    _, o_inter = lax.scan(step, jnp.zeros((B, H, K, V), F32), (q_inter, k_state, v, chunk_decay))
    o = o_intra + o_inter
    return o.transpose(1, 0, 3, 2, 4).reshape(B, S, H, V)

def hgrn2_mixer(u, w_in, lb_logits, out_gain, w_out, layer):
    B, S, _ = u.shape
    q, f_logit, i, g = jnp.split(u @ w_in, [HGRN_FORGET_DIM, 2 * HGRN_FORGET_DIM,
                                            2 * HGRN_FORGET_DIM + D_MODEL], axis=-1)
    sm = jax.nn.softmax(lb_logits.astype(F32), axis=0)
    lb = (jnp.cumsum(sm, axis=0) - sm[0])[layer]
    fl = f_logit.astype(F32)
    log_f = jnp.logaddexp(jnp.log(lb), jnp.log1p(-lb) + jax.nn.log_sigmoid(fl))
    k = (1.0 - lb) * jax.nn.sigmoid(-fl)
    q = jax.nn.silu(q.astype(F32))
    heads = lambda t, d: t.reshape(B, S, HGRN_HEADS, d)
    o = chunk_gated_recurrence(heads(q, HGRN_EXPAND), heads(k, HGRN_EXPAND),
                               heads(i.astype(F32), HGRN_VDIM), heads(log_f, HGRN_EXPAND))
    o = rms_norm(o, out_gain) * jax.nn.sigmoid(heads(g.astype(F32), HGRN_VDIM))
    return o.reshape(B, S, D_MODEL).astype(u.dtype) @ w_out

def swiglu_2(u, w_gate, w_up, w_down):
    return (jax.nn.silu(u @ w_gate) * (u @ w_up)) @ w_down

def moe_swiglu(u, w_router, w_gate, w_up, w_down):
    B, S, D = u.shape
    t = u.reshape(B * S, D)
    logits = (t @ w_router).astype(F32)
    top_vals, top_idx = lax.top_k(logits, TOP_K)
    top_w = jax.nn.softmax(top_vals, axis=-1)
    gates = jnp.sum(jax.nn.one_hot(top_idx, N_EXPERTS, dtype=F32) * top_w[..., None], axis=1)
    out = jnp.zeros((B * S, D), F32)
    for e in range(N_EXPERTS):
        y = swiglu_2(t, w_gate[e], w_up[e], w_down[e]).astype(F32)
        out = out + gates[:, e:e + 1] * y
    return out.reshape(B, S, D).astype(u.dtype)

def second_inputs(seed: int = 0) -> dict:
    key = jax.random.key(seed)
    ks = iter(jax.random.split(key, 40))
    nrm = lambda shape, scale: jax.random.normal(next(ks), shape, F32) * scale
    gain = lambda shape: 1.0 + nrm(shape, 0.02)
    D, E, O = D_MODEL, N_EVEN, N_ODD
    return {
        "x": nrm((BATCH, SEQ, D), 1.0),
        "attn_norm": gain((E, D)),
        "attn_w_in": nrm((E, D, ATTN_IN_WIDTH), D ** -0.5),
        "dil_q_gain": gain((E, HEAD_DIM)),
        "dil_k_gain": gain((E, HEAD_DIM)),
        "diff_q_gain": gain((E, DIFF_QK_DIM)),
        "diff_k_gain": gain((E, DIFF_QK_DIM)),
        "diff_lambda_q1": nrm((E, DIFF_QK_DIM), 0.1),
        "diff_lambda_k1": nrm((E, DIFF_QK_DIM), 0.1),
        "diff_lambda_q2": nrm((E, DIFF_QK_DIM), 0.1),
        "diff_lambda_k2": nrm((E, DIFF_QK_DIM), 0.1),
        "diff_out_gain": gain((E, HEAD_DIM)),
        "attn_w_out": nrm((E, D, D), D ** -0.5),
        "ffn_norm": gain((E, D)),
        "ffn_w_gate": nrm((E, D, D_FF_2), D ** -0.5),
        "ffn_w_up": nrm((E, D, D_FF_2), D ** -0.5),
        "ffn_w_down": nrm((E, D_FF_2, D), D_FF_2 ** -0.5),
        "hgrn_norm": gain((O, D)),
        "hgrn_w_in": nrm((O, D, HGRN_IN_WIDTH), D ** -0.5),
        "hgrn_lb_logits": nrm((DEPTH, HGRN_FORGET_DIM), 0.5),
        "hgrn_out_gain": gain((O, HGRN_VDIM)),
        "hgrn_w_out": nrm((O, D, D), D ** -0.5),
        "moe_norm": gain((O, D)),
        "moe_w_router": nrm((O, D, N_EXPERTS), D ** -0.5),
        "moe_w_gate": nrm((O, N_EXPERTS, D, D_FF_EXPERT), D ** -0.5),
        "moe_w_up": nrm((O, N_EXPERTS, D, D_FF_EXPERT), D ** -0.5),
        "moe_w_down": nrm((O, N_EXPERTS, D_FF_EXPERT, D), D_FF_EXPERT ** -0.5),
    }

def second_block(x, attn_norm, attn_w_in, dil_q_gain, dil_k_gain, diff_q_gain, diff_k_gain,
              diff_lambda_q1, diff_lambda_k1, diff_lambda_q2, diff_lambda_k2, diff_out_gain,
              attn_w_out, ffn_norm, ffn_w_gate, ffn_w_up, ffn_w_down,
              hgrn_norm, hgrn_w_in, hgrn_lb_logits, hgrn_out_gain, hgrn_w_out,
              moe_norm, moe_w_router, moe_w_gate, moe_w_up, moe_w_down):
    h = x
    for layer in range(DEPTH):
        j = layer // 2
        if layer % 2 == 0:
            h = h + dilated_diff_mixer(rms_norm(h, attn_norm[j]), attn_w_in[j], dil_q_gain[j], dil_k_gain[j],
                                       diff_q_gain[j], diff_k_gain[j], diff_lambda_q1[j], diff_lambda_k1[j],
                                       diff_lambda_q2[j], diff_lambda_k2[j], diff_out_gain[j],
                                       attn_w_out[j], layer).astype(h.dtype)
            h = h + swiglu_2(rms_norm(h, ffn_norm[j]), ffn_w_gate[j], ffn_w_up[j], ffn_w_down[j]).astype(h.dtype)
        else:
            h = h + hgrn2_mixer(rms_norm(h, hgrn_norm[j]), hgrn_w_in[j], hgrn_lb_logits,
                                hgrn_out_gain[j], hgrn_w_out[j], layer).astype(h.dtype)
            h = h + moe_swiglu(rms_norm(h, moe_norm[j]), moe_w_router[j], moe_w_gate[j],
                               moe_w_up[j], moe_w_down[j]).astype(h.dtype)
    return h


def setup_inputs(seed=0):
    out = dict(first_inputs(seed))
    for name, value in second_inputs(seed + 1).items():
        if name != "x":
            out[name + "_2"] = value
    return out


def reference(
    x, attn_w_in, attn_rel_bias, attn_w_out, rg_w_in, rg_conv_w, rg_conv_b, rg_w_a, rg_b_a,
    rg_w_i, rg_b_i, rg_lambda, rg_w_out, norm_mix_pre, norm_mix_post, norm_ffn_pre,
    norm_ffn_post, ffn_w_gate, ffn_w_up, ffn_w_down, attn_norm_2, attn_w_in_2, dil_q_gain_2,
    dil_k_gain_2, diff_q_gain_2, diff_k_gain_2, diff_lambda_q1_2, diff_lambda_k1_2,
    diff_lambda_q2_2, diff_lambda_k2_2, diff_out_gain_2, attn_w_out_2, ffn_norm_2, ffn_w_gate_2,
    ffn_w_up_2, ffn_w_down_2, hgrn_norm_2, hgrn_w_in_2, hgrn_lb_logits_2, hgrn_out_gain_2,
    hgrn_w_out_2, moe_norm_2, moe_w_router_2, moe_w_gate_2, moe_w_up_2, moe_w_down_2,
):
    x = first_block(
        x, attn_w_in, attn_rel_bias, attn_w_out, rg_w_in, rg_conv_w, rg_conv_b, rg_w_a, rg_b_a,
        rg_w_i, rg_b_i, rg_lambda, rg_w_out, norm_mix_pre, norm_mix_post, norm_ffn_pre,
        norm_ffn_post, ffn_w_gate, ffn_w_up, ffn_w_down,
    )
    return second_block(
        x, attn_norm_2, attn_w_in_2, dil_q_gain_2, dil_k_gain_2, diff_q_gain_2, diff_k_gain_2,
        diff_lambda_q1_2, diff_lambda_k1_2, diff_lambda_q2_2, diff_lambda_k2_2, diff_out_gain_2,
        attn_w_out_2, ffn_norm_2, ffn_w_gate_2, ffn_w_up_2, ffn_w_down_2, hgrn_norm_2,
        hgrn_w_in_2, hgrn_lb_logits_2, hgrn_out_gain_2, hgrn_w_out_2, moe_norm_2,
        moe_w_router_2, moe_w_gate_2, moe_w_up_2, moe_w_down_2,
    )


_drawn_inputs = setup_inputs


def setup_inputs(seed=0):
    import zlib

    import numpy as np

    out = dict(_drawn_inputs(seed))
    spreads = {}
    factors = {'rg_b_a': 8.0,
     'rg_b_i': 8.0,
     'attn_norm_2': 7.052,
     'dil_q_gain_2': 8.0,
     'dil_k_gain_2': 8.0,
     'diff_q_gain_2': 4.808,
     'diff_k_gain_2': 5.316,
     'diff_lambda_q2_2': 5.207,
     'diff_lambda_k2_2': 3.546,
     'diff_out_gain_2': 5.576,
     'ffn_norm_2': 3.454,
     'hgrn_norm_2': 4.36,
     'hgrn_lb_logits_2': 3.228,
     'hgrn_out_gain_2': 3.561,
     'moe_norm_2': 3.072}
    for name, (base, spread) in spreads.items():
        noise = np.random.default_rng([zlib.crc32(name.encode()), seed]).standard_normal(out[name].shape)
        drawn = base * np.exp(spread * noise) if base else spread * noise
        out[name] = __import__('jax').numpy.asarray(drawn.astype(out[name].dtype))
    for name, factor in factors.items():
        out[name] = (out[name] * factor).astype(out[name].dtype)
    return out
```

```python
from contextlib import ExitStack

import concourse.bass as bass
from concourse import mybir

P = 128
D = 1024
SEQ = 256
KT = D // P
TT = SEQ // P
HD = 64
KEYS = P + SEQ
N_HEADS_A = 8
N_HEADS_B = 8
CHUNK = 64
REL_CLIP = 256
D_FF = 2816
FT_FF = D_FF // P
GROUPS_FF = FT_FF // 4
CONV_WIDTH = 4
LRU_BLOCKS = 4
LRU_C = 8.0
N_DIL = 12
N_DIFF = 4
DIL_WINDOW = (128, 512, 2048)
DIL_STEP = (1, 4, 16)
LAM_INIT = 0.8 - 0.6
HG = 8
NE = 8
FE = 3584
CE = FE // 512
NLOAD_E = 3 * CE
CAP = P
EPS = 1e-6
MASKED = 1e30

NS = 7
NS_EARLY = 5
SLOT = 4096

F32 = mybir.dt.float32
I32 = mybir.dt.int32
U32 = mybir.dt.uint32
ALU = mybir.AluOpType
ACT = mybir.ActivationFunctionType
AX = mybir.AxisListType


def build(nc, a, out):
    ctx = ExitStack()
    with ctx:
        def sb(name, shape, dt=F32):
            return ctx.enter_context(nc.sbuf_tensor(name, shape, dt))

        def sem(name):
            return ctx.enter_context(nc.semaphore(name))

        ring = sb("ring", [P, NS, SLOT])
        arena = sb("arena", [P, 8, 2048])
        ps = ctx.enter_context(nc.psum_tensor("ps", [P, 8, 512], F32))

        def page(i, n=1):
            if i >= 8:
                flat = ring[:, NS_EARLY:NS, :].rearrange("p s n -> p (s n)")
                return flat[:, (i - 8) * 2048:(i - 8 + n) * 2048]
            return arena[:, i:i + n, :].rearrange("p s n -> p (s n)")

        X = page(0).rearrange("p (t d) -> p t d", t=TT)
        HT = page(1).rearrange("p (k t) -> p k t", k=KT)
        XN = page(2).rearrange("p (t d) -> p t d", t=TT)
        junk = sb("junk", [P, D])
        gpost = sb("gpost", [P, D])
        rows = sb("rows", [P, 2, P])
        cols = sb("cols", [P, 160])
        ident = sb("ident", [P, P])
        ones128 = sb("ones128", [P, P])
        ones64 = sb("ones64", [P, P])
        ones32 = sb("ones32", [P, P])
        before = sb("before", [P, P])
        stickmask = sb("stickmask", [P, KEYS])
        disti = sb("disti", [P, KEYS], I32)
        distm = sb("distm", [P, KEYS], I32)
        dist = sb("dist", [P, 4, KEYS])
        causal = sb("causal", [P, 2, CHUNK])
        restart = sb("restart", [P, SEQ])
        scores_T = sb("scores_T", [P, 2, TT, P])
        halves = sb("halves", [P, 4])
        epscol = sb("epscol", [P, 2])
        sumsq = sb("sumsq", [P, 32])
        rstd = sb("rstd", [P, 32])
        neg_max = sb("neg_max", [P, 2, 16])
        sums = sb("sums", [P, 2, 16])
        small = sb("small", [P, 256])
        iota_j = sb("iota_j", [P, 3 * CAP])
        wrouter = sb("wrouter", [P, KT, NE])
        rt = sb("rt", [P, 16, 16])
        rti = sb("rti", [P, 2, 8], U32)
        nblk = sb("nblk", [1, 1], I32)
        lamv = sb("lamv", [P, 4, 32])

        col = {}
        row_loads = []
        at = [0, 0]

        def rows_of(name, tile, src):
            n = src.shape[0]
            row_loads.append((rows[at[tile]:at[tile] + n, tile, :], src))
            col[name] = at[tile] + P * tile
            at[tile] += n

        def row_repeated(name, src, width):
            for r in range(P // width):
                row_loads.append((rows[at[1]:at[1] + 1, 1, r * width:(r + 1) * width], src))
            col[name] = at[1] + P
            at[1] += 1

        split = lambda ap: ap.rearrange("l (k p) -> (l k) p", p=P)
        rows_of("norm_mix_pre", 0, split(a["norm_mix_pre"]))
        rows_of("norm_ffn_pre", 0, split(a["norm_ffn_pre"]))
        rows_of("attn_norm", 0, split(a["attn_norm_2"]))
        rows_of("ffn_norm", 0, split(a["ffn_norm_2"]))
        rows_of("hgrn_norm", 0, split(a["hgrn_norm_2"]))
        rows_of("moe_norm", 0, split(a["moe_norm_2"]))
        rows_of("conv_w", 0, a["rg_conv_w"].rearrange("a w b (f p) -> (a w b f) p", p=P))
        rows_of("conv_b", 0, split(a["rg_conv_b"]))
        rows_of("b_a", 0, a["rg_b_a"].rearrange("a n (j p) -> (a n j) p", p=P))
        rows_of("b_i", 0, a["rg_b_i"].rearrange("a n (j p) -> (a n j) p", p=P))
        rows_of("lambda", 0, split(a["rg_lambda"]))
        rows_of("lb", 1, split(a["hgrn_lb_logits_2"]))
        rows_of("hgrn_out_gain", 1, a["hgrn_out_gain_2"])
        row_repeated("dil_q_gain", a["dil_q_gain_2"], HD)
        row_repeated("dil_k_gain", a["dil_k_gain_2"], HD)
        row_repeated("diff_q_gain", a["diff_q_gain_2"], HD // 2)
        row_repeated("diff_k_gain", a["diff_k_gain_2"], HD // 2)
        row_repeated("diff_out_gain", a["diff_out_gain_2"], HD)
        NROW1 = at[1]
        lam_names = ("diff_lambda_q1_2", "diff_lambda_k1_2", "diff_lambda_q2_2", "diff_lambda_k2_2")

        def column(name, i=0, n=1):
            return cols[:, col[name] + i:col[name] + i + n]

        landed = [sem(f"landed{s}") for s in range(NS)]
        landed_half = sem("landed_half")
        x_in = sem("x_in")
        rows_in = sem("rows_in")
        side_in = sem("side_in")
        gpost_in = sem("gpost_in")
        const_ok = sem("const_ok")
        pool_step = sem("pool_step")
        dve_step = sem("dve_step")
        act_step = sem("act_step")
        rows_t = sem("rows_t")
        cols_ok = sem("cols_ok")
        params_ok = sem("params_ok")
        exp_par = sem("exp_par")
        s_ss = sem("s_ss")
        s_rstd = sem("s_rstd")
        s_xn = sem("s_xn")
        s_tr = sem("s_tr")
        s_ht = sem("s_ht")
        s_unit = sem("s_unit")
        s_evac = sem("s_evac")
        s_y = sem("s_y")
        s_yss = sem("s_yss")
        s_yrstd = sem("s_yrstd")
        s_x = sem("s_x")
        s_gu = sem("s_gu")
        s_sg = sem("s_sg")
        s_h = sem("s_h")
        s_dn = sem("s_dn")
        s_out = sem("s_out")

        stream = []
        count = [0] * NS
        freed = [None] * NS
        nxt = [0]

        def next_slot():
            s = nxt[0]
            nxt[0] = (s + 1) % NS_EARLY
            return s

        def load(pairs, used):
            s = next_slot()
            stream.append((s, pairs(s), freed[s]))
            count[s] += 16 * len(pairs(s))
            freed[s] = used
            return s, count[s]

        def slot_k(s):
            return ring[:, s, :].rearrange("p (k n) -> p k n", k=KT)

        def columns_of(w, c0, n=512):
            return lambda s: [(slot_k(s)[:, :, 0:n], w.rearrange("(k p) n -> p k n", p=P)[:, :, c0:c0 + n])]

        units = [0]

        def project(w, parts):
            plan = []
            for c0, kinds in parts:
                units_before = units[0]
                units[0] += len(kinds)
                s, n = load(columns_of(w, c0), (s_unit, units[0]))
                off = 0
                tt = 0
                for j, kind in enumerate(kinds):
                    plan.append((kind, s, n, off, tt, units_before + j))
                    if kind in "FH":
                        off += 256
                    else:
                        tt += 1
            return plan

        y_n = [0]

        def project_out(w):
            y_n[0] += 2
            return [load(columns_of(w, c * 512), (s_y, y_n[0])) for c in range(2)] + [y_n[0] - 2]

        ffn_tiles = [0]

        half_n = [0]

        def plan_ffn(wg, wu, wd):
            y_n[0] += 2
            base = ffn_tiles[0]
            ffn_tiles[0] += FT_FF
            g0, g1, dn, tg, td = (next_slot() for _ in range(5))
            gate, up = (w.rearrange("(k p) (f n) -> f p k n", p=P, n=256) for w in (wg, wu))
            down = wd.rearrange("(f r p) n -> f p r n", r=2, p=P)
            f = dict(base=base, y=y_n[0] - 2, g0=g0, g1=g1, dn=dn, tg=tg, td=td, gate=gate, up=up, down=down,
                     n={s: count[s] for s in (g0, g1, dn, tg, td)}, half=half_n[0],
                     freed={s: freed[s] for s in (g0, g1, dn, tg, td)})
            for s in (g0, g1):
                count[s] += 32 * GROUPS_FF
                freed[s] = (s_gu, base + 4 * GROUPS_FF)
            count[dn] += 16 * GROUPS_FF
            half_n[0] += 16 * GROUPS_FF
            freed[dn] = (s_dn, (FT_FF - 1) * (base // FT_FF) + 4 * GROUPS_FF)
            count[tg] += 32
            freed[tg] = (s_gu, base + FT_FF)
            count[td] += 16
            freed[td] = (s_y, y_n[0])
            stream.append(f)
            return f

        A_w_in = a["attn_w_in"][0]
        R_w_in = a["rg_w_in"][0]
        E_w_in = a["attn_w_in_2"][0]
        G_w_in = a["hgrn_w_in_2"][0]
        A_plan = project(A_w_in, [(0, "FF"), (512, "FF"), (1024, "TT"), (1536, "FF"), (2048, "FF"), (2560, "TT")])
        A_out = project_out(a["attn_w_out"][0])
        FFN = [plan_ffn(a["ffn_w_gate"][0], a["ffn_w_up"][0], a["ffn_w_down"][0])]
        R_plan = project(R_w_in, [(1024, "FF"), (1536, "FF")])
        gate_n = [0]
        r_gates = sem("r_gates")

        def gate_weights(s):
            v = ring[:, s, :].rearrange("p (w k n) -> p w k n", w=2, k=KT)
            return [(v[:, i], a[n][0].rearrange("n (k p) j -> p (n k) j", p=P)) for i, n in enumerate(("rg_w_a", "rg_w_i"))]

        R_gate_w = load(gate_weights, (r_gates, KT))
        R_plan += project(R_w_in, [(0, "FF"), (512, "FF")])
        R_out = project_out(a["rg_w_out"][0])
        FFN.append(plan_ffn(a["ffn_w_gate"][1], a["ffn_w_up"][1], a["ffn_w_down"][1]))
        E_plan = project(E_w_in, [(0, "FF"), (512, "FF"), (1024, "FF"), (1536, "TT"), (2048, "HF"), (2560, "FH")])
        E_out = project_out(a["attn_w_out_2"][0])
        FFN.append(plan_ffn(a["ffn_w_gate_2"][0], a["ffn_w_up_2"][0], a["ffn_w_down_2"][0]))
        G_plan = project(G_w_in, [(1024, "FF"), (1536, "FF"), (0, "FF"), (512, "FF"), (2048, "TT"), (2560, "TT"),
                                  (3072, "FF"), (3584, "FF")])
        G_out = project_out(a["hgrn_w_out_2"][0])

        block = ctx.enter_context(nc.Block())

        class Steps:

            def __init__(self, eng, s):
                self.eng, self.s, self.n = eng, s, 0

            def link(self, ins):
                self.n += 1
                ins.then_inc(self.s, 1)
                self.eng.wait_ge(self.s, self.n)

        gain_of = [("norm_mix_pre", 0), ("norm_ffn_pre", 0), ("norm_mix_pre", 8), ("norm_ffn_pre", 8),
                   ("attn_norm", 0), ("ffn_norm", 0), ("hgrn_norm", 0), ("moe_norm", 0)]

        def norm_scalar(act, k):
            for t in range(TT):
                if k == 0:
                    act.wait_ge(x_in, 16)
                else:
                    act.wait_ge(s_x, 2 * (k - 1) + t + 1)
                nc.scalar.activation(XN[:, t, :], X[:, t, :], ACT.Square,
                                     accum_out=sumsq[:, 2 * k + t:2 * k + t + 1]).then_inc(s_ss, 1)

        def norm_gpsimd(pool, step, k):
            for t in range(TT):
                c = slice(2 * k + t, 2 * k + t + 1)
                pool.wait_ge(s_ss, 2 * k + t + 1)
                step.link(nc.gpsimd.tensor_scalar(sumsq[:, c], sumsq[:, c], D * EPS, None, ALU.add))
                nc.gpsimd.tensor_tensor(rstd[:, c], sumsq[:, c], halves[:, 0:1], ALU.pow).then_inc(s_rstd, 1)

        def norm_vector(dve, k):
            for t in range(TT):
                dve.wait_ge(s_rstd, 2 * k + t + 1)
                nc.vector.tensor_scalar(XN[:, t, :], X[:, t, :], rstd[:, 2 * k + t:2 * k + t + 1], float(D) ** 0.5,
                                        ALU.mult, ALU.mult).then_inc(s_xn, 1)
            name, i = gain_of[k]
            for t in range(TT):
                for h in range(2):
                    dve.wait_ge(s_tr, 4 * k + 2 * t + h + 1)
                    g = column(name, i + 4 * h, 4).rearrange("p (k o) -> p k o", o=1).to_broadcast([P, 4, P])
                    nc.vector.tensor_tensor(HT[:, 4 * h:4 * h + 4, t * P:(t + 1) * P],
                                            ps[:, 2 * t + h, :].rearrange("p (k t) -> p k t", k=4), g,
                                            ALU.mult).then_inc(s_ht, 1)

        def norm_tensor(pe, k):
            for t in range(TT):
                pe.wait_ge(s_xn, 2 * k + t + 1)
                for h in range(2):
                    for kt in range(4 * h, 4 * h + 4):
                        mm = nc.tensor.transpose(ps[:, 2 * t + h, (kt % 4) * P:(kt % 4 + 1) * P],
                                                 XN[:, t, kt * P:(kt + 1) * P], ident[:, :])
                    mm.then_inc(s_tr, 1)
            pe.wait_ge(s_ht, 4 * k + 4)

        def unit_tensor(pe, plan, j, nbanks):
            kind, s, n, off, tt, u = plan[j]
            pe.wait_ge(landed[s], n)
            if j >= nbanks:
                pe.wait_ge(s_evac, u - nbanks + 1)
            bank = ps[:, j % nbanks, :]
            w = slot_k(s)
            if kind == "F":
                for f in range(2):
                    for kt in range(KT):
                        mm = nc.tensor.matmul(bank[:, f * SEQ:(f + 1) * SEQ], w[:, kt, off + f * P:off + (f + 1) * P],
                                              HT[:, kt, :], start=(kt == 0), stop=(kt == KT - 1))
            elif kind == "T":
                for kt in range(KT):
                    mm = nc.tensor.matmul(bank, HT[:, kt, tt * P:(tt + 1) * P], w[:, kt, :],
                                          start=(kt == 0), stop=(kt == KT - 1))
            else:
                for t in range(TT):
                    for kt in range(KT):
                        mm = nc.tensor.matmul(bank[:, t * 256:(t + 1) * 256], HT[:, kt, t * P:(t + 1) * P],
                                              w[:, kt, off:off + 256], start=(kt == 0), stop=(kt == KT - 1))
            mm.then_inc(s_unit, 1)

        def unit_scalar(act, plan, j, nbanks, dst, func=ACT.Copy, scale=1.0):
            u = plan[j][5]
            act.wait_ge(s_unit, u + 1)
            nc.scalar.activation(dst, ps[:, j % nbanks, :], func, scale=scale).then_inc(s_evac, 1)

        Y = ps[:, 4:8, :].rearrange("p (t h) n -> p t (h n)", t=TT)

        def out_tensor(pe, plan, actT):
            for c in range(2):
                pe.wait_ge(landed[plan[c][0]], plan[c][1])
            for t in range(TT):
                for c in range(2):
                    for kt in range(KT):
                        mm = nc.tensor.matmul(Y[:, t, c * 512:(c + 1) * 512], actT[:, kt, t * P:(t + 1) * P],
                                              slot_k(plan[c][0])[:, kt, :], start=(kt == 0), stop=(kt == KT - 1))
                mm.then_inc(s_y, 1)

        def postnorm_scalar(act, m):
            for t in range(TT):
                act.wait_ge(s_y, 2 * m + t + 1)
                nc.scalar.activation(XN[:, 1, :] if t else junk[:, :], Y[:, t, :], ACT.Square,
                                     accum_out=sumsq[:, 16 + 2 * m + t:17 + 2 * m + t]).then_inc(s_yss, 1)

        def postnorm_gpsimd(pool, step, m):
            for t in range(TT):
                c = slice(16 + 2 * m + t, 17 + 2 * m + t)
                pool.wait_ge(s_yss, 2 * m + t + 1)
                step.link(nc.gpsimd.tensor_scalar(sumsq[:, c], sumsq[:, c], D * EPS, None, ALU.add))
                nc.gpsimd.tensor_tensor(rstd[:, c], sumsq[:, c], halves[:, 0:1], ALU.pow).then_inc(s_yrstd, 1)

        def postnorm_vector(dve, step, m):
            dve.wait_ge(gpost_in, 16 * (m + 1))
            for t in range(TT):
                dve.wait_ge(s_yrstd, 2 * m + t + 1)
                step.link(nc.vector.scalar_tensor_tensor(XN[:, t, :], Y[:, t, :],
                                                         rstd[:, 16 + 2 * m + t:17 + 2 * m + t], gpost[:, :],
                                                         ALU.mult, ALU.mult))
                nc.vector.scalar_tensor_tensor(X[:, t, :], XN[:, t, :], float(D) ** 0.5, X[:, t, :],
                                               ALU.mult, ALU.add).then_inc(s_x, 1)

        def residual_vector(dve, m):
            for t in range(TT):
                dve.wait_ge(s_y, 2 * m + t + 1)
                nc.vector.tensor_tensor(X[:, t, :], X[:, t, :], Y[:, t, :], ALU.add).then_inc(s_x, 1)

        hidden = page(3).rearrange("p (f t) -> p f t", f=8)
        silu = page(4).rearrange("p (f t) -> p f t", f=8)

        def gate_up(pe, f4, w, off, freed_h, u):
            if freed_h is not None:
                pe.wait_ge(s_h, freed_h)
            for i in range(2):
                for kt in range(KT):
                    mm = nc.tensor.matmul(ps[:, f4, i * SEQ:(i + 1) * SEQ], w[:, i, kt, off:off + P], HT[:, kt, :],
                                          start=(kt == 0), stop=(kt == KT - 1))
            mm.then_inc(s_gu, 1)

        def down(pe, f4, w, ready_h, first=False, last=False):
            pe.wait_ge(s_h, ready_h)
            for t in range(TT):
                for c in range(2):
                    mm = nc.tensor.matmul(Y[:, t, c * 512:(c + 1) * 512], hidden[:, f4, t * P:(t + 1) * P],
                                          w[:, c * 512:(c + 1) * 512], start=first, stop=last)
                if last:
                    mm.then_inc(s_y, 1)
            if not last:
                mm.then_inc(s_dn, 1)

        def ffn_views(f):
            v = lambda s: ring[:, s, :].rearrange("p (w k n) -> p w k n", w=2, k=KT)
            d = lambda s: ring[:, s, :].rearrange("p (r n) -> p r n", n=D)
            return v(f["g0"]), v(f["g1"]), d(f["dn"]), v(f["tg"]), d(f["td"])

        def ffn_tensor(pe, f):
            g0, g1, dn, tg, td = ffn_views(f)
            b, n = f["base"], f["n"]
            pe.wait_ge(landed[f["g0"]], n[f["g0"]] + 32)
            gate_up(pe, 0, g0, 0, None, b)
            gate_up(pe, 1, g0, P, None, b)
            pe.wait_ge(landed[f["g1"]], n[f["g1"]] + 32)
            gate_up(pe, 2, g1, 0, None, b)
            pe.wait_ge(landed[f["dn"]], n[f["dn"]] + 16)
            down(pe, 0, dn[:, 0, :], b + 1, first=True)
            gate_up(pe, 3, g1, P, None, b)
            down(pe, 1, dn[:, 1, :], b + 2)
            with pe.Fori(1, GROUPS_FF) as i:
                pe.wait_ge(landed[f["g0"]], 32 * i + (n[f["g0"]] + 32))
                gate_up(pe, 0, g0, 0, 4 * i + (b - 3), b)
                pe.wait_ge(landed_half, 16 * i + f["half"])
                down(pe, 2, dn[:, 2, :], 4 * i + (b - 1))
                gate_up(pe, 1, g0, P, 4 * i + (b - 2), b)
                down(pe, 3, dn[:, 3, :], 4 * i + b)
                pe.wait_ge(landed[f["g1"]], 32 * i + (n[f["g1"]] + 32))
                gate_up(pe, 2, g1, 0, 4 * i + (b - 1), b)
                pe.wait_ge(landed[f["dn"]], 16 * i + (n[f["dn"]] + 16))
                down(pe, 0, dn[:, 0, :], 4 * i + (b + 1))
                gate_up(pe, 3, g1, P, 4 * i + b, b)
                down(pe, 1, dn[:, 1, :], 4 * i + (b + 2))
            t0 = 4 * GROUPS_FF
            pe.wait_ge(landed[f["tg"]], n[f["tg"]] + 32)
            gate_up(pe, 0, tg, 0, b + t0 - 3, b)
            pe.wait_ge(landed_half, f["half"] + 16 * GROUPS_FF)
            down(pe, 2, dn[:, 2, :], b + t0 - 1)
            gate_up(pe, 1, tg, P, b + t0 - 2, b)
            down(pe, 3, dn[:, 3, :], b + t0)
            pe.wait_ge(landed[f["td"]], n[f["td"]] + 16)
            down(pe, 0, td[:, 0, :], b + t0 + 1)
            down(pe, 1, td[:, 1, :], b + t0 + 2, last=True)

        def ffn_scalar(act, f):
            b = f["base"]

            def tile(f4, gu, used):
                act.wait_ge(s_gu, gu)
                if used is not None:
                    act.wait_ge(s_h, used)
                nc.scalar.activation(silu[:, f4, :], ps[:, f4, 0:SEQ], ACT.Silu).then_inc(s_sg, 1)

            for f4 in range(4):
                tile(f4, b + f4 + 1, None)
            with act.Fori(1, GROUPS_FF) as i:
                for f4 in range(4):
                    tile(f4, 4 * i + (b + f4 + 1), 4 * i + (b + f4 - 3))
            for f4 in range(2):
                tile(f4, b + 4 * GROUPS_FF + f4 + 1, b + 4 * GROUPS_FF + f4 - 3)

        def ffn_vector(dve, f):
            b = f["base"]
            k = (FT_FF - 1) * (b // FT_FF)

            def tile(f4, sg, dn_used):
                dve.wait_ge(s_sg, sg)
                if dn_used is not None:
                    dve.wait_ge(s_dn, dn_used)
                nc.vector.tensor_tensor(hidden[:, f4, :], silu[:, f4, :], ps[:, f4, SEQ:2 * SEQ],
                                        ALU.mult).then_inc(s_h, 1)

            for f4 in range(4):
                tile(f4, b + f4 + 1, None)
            with dve.Fori(1, GROUPS_FF) as i:
                for f4 in range(4):
                    tile(f4, 4 * i + (b + f4 + 1), 4 * i + (k + f4 - 3))
            for f4 in range(2):
                tile(f4, b + 4 * GROUPS_FF + f4 + 1, k + 4 * GROUPS_FF + f4 - 3)

        def ffn_sync(sp, f):
            g0, g1, dn, tg, td = ffn_views(f)
            b, fr = f["base"], f["freed"]
            k = (FT_FF - 1) * (b // FT_FF)

            def pair(s, v, j):
                sp.dma_start(v[:, 0], f["gate"][j]).then_inc(landed[s], 16)
                sp.dma_start(v[:, 1], f["up"][j]).then_inc(landed[s], 16)

            def halves_of(s, v, j, r):
                sp.dma_start(v[:, 2 * r:2 * r + 2, :], f["down"][j]).then_inc(landed_half if r else landed[s], 16)

            for s in (f["g0"], f["g1"], f["dn"]):
                if fr[s]:
                    sp.wait_ge(*fr[s])
            pair(f["g0"], g0, 0)
            pair(f["g1"], g1, 1)
            halves_of(f["dn"], dn, 0, 0)
            halves_of(f["dn"], dn, 1, 1)
            with sp.Fori(1, GROUPS_FF) as i:
                at_i = lambda v, j: v[bass.ds(2 * i + j, 1)].rearrange("o p k n -> p (o k) n")
                sp.wait_ge(s_gu, 4 * i + (b - 2))
                for v, w in ((g0[:, 0], f["gate"]), (g0[:, 1], f["up"])):
                    sp.dma_start(v, at_i(w, 0)).then_inc(landed[f["g0"]], 16)
                sp.wait_ge(s_gu, 4 * i + b)
                for v, w in ((g1[:, 0], f["gate"]), (g1[:, 1], f["up"])):
                    sp.dma_start(v, at_i(w, 1)).then_inc(landed[f["g1"]], 16)
                sp.wait_ge(s_dn, 4 * i + (k - 2))
                sp.dma_start(dn[:, 0:2, :], at_i(f["down"], 0)).then_inc(landed[f["dn"]], 16)
                sp.wait_ge(s_dn, 4 * i + k)
                sp.dma_start(dn[:, 2:4, :], at_i(f["down"], 1)).then_inc(landed_half, 16)
            for s in (f["tg"], f["td"]):
                if fr[s]:
                    sp.wait_ge(*fr[s])
            pair(f["tg"], tg, 2 * GROUPS_FF)
            halves_of(f["td"], td, 2 * GROUPS_FF, 0)

        def setup_gpsimd(pool, step):
            step.link(nc.gpsimd.memset(halves[:, :], -0.5))
            nc.gpsimd.memset(epscol[:, :], EPS)
            step.link(nc.gpsimd.memset(ident[:, :], 0.0))
            step.link(nc.gpsimd.affine_select(out=ident[:, :], in_=ident[:, :], compare_op=ALU.not_equal, fill=1.0,
                                              base=0, pattern=[[-1, P]], channel_multiplier=1))
            nc.gpsimd.iota(disti[:, 0:P], [[-1, P]], base=0, channel_multiplier=1)
            nc.gpsimd.iota(disti[:, P:], [[-1, SEQ]], base=P, channel_multiplier=1)
            nc.gpsimd.iota(distm[:, :], [[1, 3 * CAP]], base=0, channel_multiplier=0)
            nc.gpsimd.memset(ones128[:, :], 1.0)
            nc.gpsimd.memset(stickmask[:, :], 0.0)
            nc.gpsimd.memset(causal[:, :, :], 1.0)
            nc.gpsimd.memset(restart[:, :], 1.0)
            step.link(nc.gpsimd.memset(scores_T[:, :, :, :], 0.0))
            nc.gpsimd.tensor_copy(iota_j[:, :], distm[:, :]).then_inc(const_ok, 1)
            pool.wait_ge(const_ok, 1)
            for q in range(2):
                step.link(nc.gpsimd.affine_select(out=causal[64 * q:64 * q + 64], in_=causal[64 * q:64 * q + 64],
                                                  compare_op=ALU.is_ge, fill=0.0, base=0, pattern=[[0, 2], [1, CHUNK]],
                                                  channel_multiplier=-1))
            nc.gpsimd.memset(restart[:, :].rearrange("p (c t) -> p c t", t=CHUNK)[:, :, 0:1], 0.0)
            nc.gpsimd.affine_select(out=before[:, :], in_=ones128[:, :], compare_op=ALU.is_gt, fill=0.0, base=0,
                                    pattern=[[1, P]], channel_multiplier=-1)
            step.link(keys_select(stickmask, ALU.is_gt, 0, 1, -MASKED))
            pool.wait_ge(dve_step, 5)
            for g in range(4):
                step.link(keys_select(dist[:, g, :], ALU.is_ge, 0, 1, MASKED))
            keys_select(dist[:, 0, :], ALU.is_ge, DIL_WINDOW[0], -1, MASKED).then_inc(const_ok, 1)

        def keys_select(m, op, base, sign, fill):
            nc.gpsimd.affine_select(out=m[:, 0:P], in_=m[:, 0:P], compare_op=op, fill=fill, base=base,
                                    pattern=[[-sign, P]], channel_multiplier=sign)
            return nc.gpsimd.affine_select(out=m[:, P:KEYS], in_=m[:, P:KEYS], compare_op=op, fill=fill,
                                           base=base + sign * P, pattern=[[-sign, SEQ]], channel_multiplier=sign)

        def setup_loads(act):
            for dst, src in row_loads:
                act.dma_start(dst, src).then_inc(rows_in, 16)

        z24, e24, sp24 = small[:, 0:24], small[:, 24:48], small[:, 48:72]
        decay_scale, decay_neg = small[:, 72:80], small[:, 80:88]
        ln_lb, ln_1lb, ln_dif = small[:, 88:96], small[:, 96:104], small[:, 104:112]
        gains = small[:, 112:116]
        lam2, elam, neg_lam = small[:, 116:118], small[:, 118:120], small[:, 120:121]
        lam_prod = small[:, 128:192].rearrange("p (a d) -> p a d", a=2)

        def setup_tensor(pe):
            pe.wait_ge(const_ok, 1)
            pe.wait_ge(rows_in, 16 * len(row_loads))
            nc.tensor.transpose(ps[:, 7, 0:P], rows[:, 0, :], ident[:, :])
            nc.tensor.transpose(ps[:, 7, P:P + NROW1], rows[0:NROW1, 1, :], ident[0:NROW1, 0:NROW1]).then_inc(rows_t, 1)

        def setup_vector(dve, step):
            nc.vector.memset(ones64[:, :], 0.0)
            step.link(nc.vector.memset(ones32[:, :], 0.0))
            for q in range(4):
                nc.vector.memset(ones32[32 * q:32 * q + 32, 32 * q:32 * q + 32], 1.0)
            for q in range(2):
                nc.vector.memset(ones64[64 * q:64 * q + 64, 64 * q:64 * q + 64], 1.0)
            dve.wait_ge(const_ok, 1)
            nc.vector.tensor_copy(dist[:, 0, :], disti[:, :])
            nc.vector.tensor_copy(dist[:, 3, :], disti[:, :])
            step.link(nc.vector.tensor_scalar(distm[:, :], disti[:, :], DIL_STEP[1] - 1, None, ALU.bitwise_and))
            step.link(nc.vector.scalar_tensor_tensor(dist[:, 1, :], distm[:, :], MASKED, disti[:, :], ALU.mult, ALU.add))
            step.link(nc.vector.tensor_scalar(distm[:, :], disti[:, :], DIL_STEP[2] - 1, None, ALU.bitwise_and))
            step.link(nc.vector.scalar_tensor_tensor(dist[:, 2, :], distm[:, :], MASKED, disti[:, :], ALU.mult, ALU.add))
            dve.wait_ge(rows_t, 1)
            step.link(nc.vector.tensor_copy(cols[:, 0:P + NROW1], ps[:, 7, 0:P + NROW1]))

        def params_vector(dve, step):
            nc.vector.tensor_scalar(z24[:, 0:8], column("lambda", 0, 8), -1.0, None, ALU.mult)
            nc.vector.tensor_tensor(z24[:, 8:16], column("lb", 0, 8), column("lb", 8, 8), ALU.subtract)
            nc.vector.tensor_tensor(z24[:, 16:24], column("lb", 8, 8), column("lb", 0, 8), ALU.subtract)
            nc.vector.tensor_scalar(gains[:, 0:1], column("dil_q_gain"), HD ** -0.5, None, ALU.mult)
            nc.vector.tensor_scalar(gains[:, 1:2], column("diff_q_gain"), (HD // 2) ** -0.5, None, ALU.mult)
            nc.vector.tensor_scalar(gains[:, 2:3], column("diff_out_gain"), 1.0 - LAM_INIT, None, ALU.mult)
            dve.wait_ge(side_in, 16 * 6)
            nc.vector.tensor_tensor(lam_prod[:, 0], lamv[:, 0], lamv[:, 1], ALU.mult)
            step.link(nc.vector.tensor_tensor(lam_prod[:, 1], lamv[:, 2], lamv[:, 3], ALU.mult))
            nc.vector.tensor_reduce(lam2, lam_prod, AX.X, ALU.add)
            nc.vector.scalar_tensor_tensor(e24, z24, -1.0, z24, ALU.mult, ALU.min).then_inc(params_ok, 1)
            dve.wait_ge(exp_par, 3)
            step.link(nc.vector.scalar_tensor_tensor(sp24, z24, 0.0, e24, ALU.max, ALU.add))
            nc.vector.tensor_scalar(decay_scale, sp24[:, 0:8], -LRU_C, None, ALU.mult)
            nc.vector.tensor_scalar(decay_neg, sp24[:, 0:8], LRU_C, None, ALU.mult)
            nc.vector.tensor_scalar(ln_lb, sp24[:, 8:16], -1.0, None, ALU.mult)
            nc.vector.tensor_scalar(ln_1lb, sp24[:, 16:24], -1.0, None, ALU.mult)
            nc.vector.tensor_tensor(ln_dif, sp24[:, 8:16], sp24[:, 16:24], ALU.subtract)
            step.link(nc.vector.tensor_tensor(neg_lam, elam[:, 1:2], elam[:, 0:1], ALU.subtract))
            nc.vector.tensor_scalar(neg_lam, neg_lam, -LAM_INIT, None, ALU.add).then_inc(params_ok, 1)

        def setup_scalar(act):
            act.wait_ge(params_ok, 1)
            nc.scalar.activation(e24, e24, ACT.Exp).then_inc(exp_par, 1)
            nc.scalar.activation(elam, lam2, ACT.Exp).then_inc(exp_par, 1)
            act.wait_ge(exp_par, 2)
            nc.scalar.activation(e24, e24, ACT.Ln, bias=1.0).then_inc(exp_par, 1)

        QK = page(3, 2).rearrange("p (f t) -> p f t", t=SEQ)
        V = page(5).rearrange("p (t d) -> p t d", t=TT)
        OT = page(6).rearrange("p (f t) -> p f t", t=SEQ)
        four = lambda pg: pg[:, 0:4 * KEYS].rearrange("p (h k) -> p h k", h=4)
        A_sc = [four(page(2)), four(page(7))]
        A_w = [four(page(10)), four(page(11))]
        A_na = four(page(1))
        A_bias = page(8, 2)[:, 0:8 * KEYS].rearrange("p (h k) -> p h k", h=8)
        A_pt = page(8, 2)[:, 8 * KEYS:10 * KEYS].rearrange("p (h k) -> p h k", h=2)
        a_s, a_sc, a_mx, a_e, a_pn = (sem("a_" + n) for n in ("s", "sc", "mx", "e", "pn"))
        a_na, a_ln, a_d, a_w = (sem("a_" + n) for n in ("na", "ln", "d", "w"))
        a_t, a_pt, a_pv, a_ot = (sem("a_" + n) for n in ("t", "pt", "pv", "ot"))

        def A_tensor(pe):
            norm_tensor(pe, 0)

            def gemm(*js):
                for j in js:
                    unit_tensor(pe, A_plan, j, 2)

            def scores(b):
                pe.wait_ge(s_evac, 4 if b < 2 else 10)
                for g in range(4 * b, 4 * b + 4):
                    if g >= 2:
                        pe.wait_ge(a_sc, g - 1)
                    fq = g // 2 if g < 8 else 8 + (g - 8) // 2
                    r = slice(HD * (g % 2), HD * (g % 2) + HD)
                    nc.tensor.matmul(ps[:, 4 + g % 2, 0:P], QK[r, fq, 0:P], QK[r, fq + 4, 0:P], start=True, stop=True)
                    nc.tensor.matmul(ps[:, 4 + g % 2, P:KEYS], QK[r, fq, P:SEQ], QK[r, fq + 4, :], start=True,
                                     stop=True).then_inc(a_s, 1)

            def turn(g):
                if g >= 2:
                    pe.wait_ge(a_pt, g - 1)
                for c in range(3):
                    mm = nc.tensor.transpose(ps[:, 6 + g % 2, c * P:(c + 1) * P],
                                             A_w[g // 4 % 2][:, g % 4, c * P:(c + 1) * P], ident[:, :])
                mm.then_inc(a_t, 1)

            def values(g):
                pe.wait_ge(a_pt, g + 1)
                if g >= 4 and g % 2 == 0:
                    pe.wait_ge(a_ot, g // 2 - 1)
                o = ps[HD * (g % 2):HD * (g % 2) + HD, 2 + g // 2 % 2, :]
                nc.tensor.matmul(o[:, 0:SEQ], V[:, 0, g * HD:(g + 1) * HD], A_pt[:, g % 2, 0:SEQ], start=True, stop=False)
                nc.tensor.matmul(o[:, P:SEQ], V[:, 1, g * HD:(g + 1) * HD], A_pt[:, g % 2, SEQ:KEYS], start=False,
                                 stop=True).then_inc(a_pv, 1)

            def attend(b):
                if b < 2:
                    pe.wait_ge(a_pn, b + 1)
                else:
                    pe.wait_ge(a_w, b - 1)
                turn(4 * b)
                for g in range(4 * b, 4 * b + 4):
                    if g % 4 < 3:
                        turn(g + 1)
                    values(g)

            gemm(0, 1, 2, 3, 4, 5)
            scores(0)
            gemm(6, 7)
            scores(1)
            gemm(8, 9)
            attend(0)
            gemm(10, 11)
            attend(1)
            scores(2)
            scores(3)
            attend(2)
            attend(3)
            pe.wait_ge(a_ot, 8)
            out_tensor(pe, A_out, OT)

        def A_scalar(act, step):
            norm_scalar(act, 0)
            setup_scalar(act)

            def evac(j):
                c = A_plan[j]
                if c[0] == "T":
                    unit_scalar(act, A_plan, j, 2, V[:, c[4], (0 if j < 6 else 512):(512 if j < 6 else D)])
                else:
                    f = 2 * (j if j < 4 else j - 2)
                    unit_scalar(act, A_plan, j, 2, QK[:, f:f + 2, :], scale=HD ** -0.5 if f // 4 in (0, 2) else 1.0)

            def exps(b):
                act.wait_ge(a_mx, b + 1)
                for i in range(4):
                    for t, c in enumerate((slice(0, P), slice(P, KEYS))):
                        ins = nc.scalar.activation(A_w[b % 2][:, i, c], A_sc[b % 2][:, i, c], ACT.Exp,
                                                   bias=neg_max[:, t, 4 * b + i:4 * b + i + 1],
                                                   accum_out=sums[:, t, 4 * b + i:4 * b + i + 1])
                ins.then_inc(a_e, 1)

            def softplus(b):
                act.wait_ge(a_na, b - 1)
                step.link(nc.scalar.activation(A_na, A_na, ACT.Exp))
                nc.scalar.activation(A_na, A_na, ACT.Ln, bias=1.0).then_inc(a_ln, 1)

            def weights(b):
                act.wait_ge(a_d, b - 1)
                nc.scalar.activation(A_w[b % 2], A_sc[b % 2], ACT.Exp).then_inc(a_w, 1)

            def copies(b):
                for g in range(4 * b, 4 * b + 5):
                    if g < 4 * b + 4:
                        act.wait_ge(a_t, g + 1)
                        if g >= 2:
                            act.wait_ge(a_pv, g - 1)
                        nc.scalar.activation(A_pt[:, g % 2, :], ps[:, 6 + g % 2, 0:KEYS], ACT.Copy).then_inc(a_pt, 1)
                    if g % 2 == 0 and g > 4 * b:
                        act.wait_ge(a_pv, g)
                        nc.scalar.activation(OT[:, g // 2 - 1, :], ps[:, 2 + (g // 2 - 1) % 2, 0:SEQ],
                                             ACT.Copy).then_inc(a_ot, 1)

            for j in range(6):
                evac(j)
            exps(0)
            evac(6), evac(7)
            exps(1)
            evac(8), evac(9)
            copies(0)
            evac(10), evac(11)
            copies(1)
            softplus(2)
            weights(2)
            softplus(3)
            copies(2)
            weights(3)
            copies(3)
            postnorm_scalar(act, 0)

        def A_vector(dve, step):
            norm_vector(dve, 0)
            params_vector(dve, step)
            step.link(nc.vector.memset(A_bias[0:CHUNK, :, P:P + CHUNK], -MASKED))

            def biased(b):
                sc = A_sc[b]
                for i in range(4):
                    g = 4 * b + i
                    dve.wait_ge(a_s, g + 1)
                    nc.vector.tensor_tensor(sc[:, i, 0:P], ps[:, 4 + g % 2, 0:P], A_bias[:, g, P:SEQ][:, ::-1], ALU.add)
                    nc.vector.tensor_tensor(sc[:, i, P:KEYS], ps[:, 4 + g % 2, P:KEYS], A_bias[:, g, P:KEYS][:, ::-1],
                                            ALU.add).then_inc(a_sc, 1)
                dve.wait_ge(a_sc, 4 * b + 4)
                nc.vector.tensor_reduce(neg_max[:, 0, 4 * b:4 * b + 4], sc[:, :, 0:P], AX.X, ALU.max, negate=True)
                nc.vector.tensor_reduce(neg_max[:, 1, 4 * b:4 * b + 4], sc[:, :, P:KEYS], AX.X, ALU.max,
                                        negate=True).then_inc(a_mx, 1)

            def normalised(b):
                dve.wait_ge(a_e, b + 1)
                r = sums[:, :, 4 * b:4 * b + 4]
                step.link(nc.vector.reciprocal(r, r))
                for i in range(4):
                    for t, c in enumerate((slice(0, P), slice(P, KEYS))):
                        w = A_w[b][:, i, c]
                        ins = nc.vector.tensor_scalar(w, w, sums[:, t, 4 * b + i:4 * b + i + 1], None, ALU.mult)
                ins.then_inc(a_pn, 1)

            def stick_scores(b):
                sc = A_sc[b % 2]
                for i in range(4):
                    g = 4 * b + i
                    dve.wait_ge(a_s, g + 1)
                    nc.vector.tensor_tensor(sc[:, i, :], ps[:, 4 + g % 2, 0:KEYS], stickmask[:, :],
                                            ALU.add).then_inc(a_sc, 1)
                dve.wait_ge(a_sc, 4 * b + 4)
                nc.vector.scalar_tensor_tensor(A_na, sc, -1.0, sc, ALU.mult, ALU.min).then_inc(a_na, 1)

            def stick_sums(b):
                sc, w = A_sc[b % 2], A_w[b % 2]
                dve.wait_ge(a_ln, b - 1)
                dve.wait_ge(a_t, 4 * (b - 1))
                step.link(nc.vector.scalar_tensor_tensor(w, sc, 0.0, A_na, ALU.max, ALU.add))
                for i in range(4):
                    for c in (slice(0, P), slice(P, KEYS)):
                        v = w[:, i, c][:, ::-1]
                        ins = nc.vector.tensor_tensor_scan(A_na[:, i, c][:, ::-1], v, v, 0.0, ALU.add, ALU.bypass)
                step.link(ins)
                nc.vector.tensor_tensor(sc, sc, A_na, ALU.subtract).then_inc(a_d, 1)

            biased(0)
            normalised(0)
            biased(1)
            normalised(1)
            stick_scores(2)
            stick_sums(2)
            stick_scores(3)
            stick_sums(3)
            postnorm_vector(dve, step, 0)

        norm_at_ffn = (1, 3, 5)

        def F_tensor(pe, i):
            norm_tensor(pe, norm_at_ffn[i])
            ffn_tensor(pe, FFN[i])

        def F_scalar(act, i):
            norm_scalar(act, norm_at_ffn[i])
            ffn_scalar(act, FFN[i])
            if i < 2:
                postnorm_scalar(act, 2 * i + 1)

        def F_vector(dve, step, i):
            norm_vector(dve, norm_at_ffn[i])
            ffn_vector(dve, FFN[i])
            if i < 2:
                postnorm_vector(dve, step, 2 * i + 1)
            else:
                residual_vector(dve, 5)

        TAPS = CONV_WIDTH - 1
        R_x = page(3, 2)[:, 0:KT * (TAPS + SEQ)].rearrange("p (f t) -> p f t", f=KT)
        tiles = lambda i: page(i).rearrange("p (f t) -> p f t", f=KT)
        R_xc, R_r, R_i, R_gate, R_tau, R_a, R_u, R_y = (tiles(i) for i in (5, 6, 7, 8, 9, 10, 11, 9))
        R_h = page(3).rearrange("p (f t) -> p f t", f=KT)
        r_pad, r_xc, r_sig, r_tau, r_exp, r_v, r_mult, r_out = (
            sem("r_" + n) for n in ("pad", "xc", "sig", "tau", "exp", "v", "mult", "out"))

        def R_tensor(pe):
            norm_tensor(pe, 2)
            for j in range(5):
                unit_tensor(pe, R_plan, j, 2)
            s, n = R_gate_w
            pe.wait_ge(landed[s], n)
            w = ring[:, s, :].rearrange("p (w k n) -> p w k n", w=2, k=KT)
            for j in range(KT):
                pe.wait_ge(r_xc, j // 2 + 1)
                if j >= 2:
                    pe.wait_ge(r_sig, j - 1)
                for i in range(2):
                    for kt in range(2):
                        f = j // 2 * 2 + kt
                        mm = nc.tensor.matmul(ps[:, 2 + j % 2, i * SEQ:(i + 1) * SEQ],
                                              w[:, i, f, j % 2 * P:(j % 2 + 1) * P], R_xc[:, f, :],
                                              start=(kt == 0), stop=(kt == 1))
                mm.then_inc(r_gates, 1)
            for j in range(5, 8):
                unit_tensor(pe, R_plan, j, 2)
            pe.wait_ge(r_out, 4)
            out_tensor(pe, R_out, R_y)

        def R_scalar(act, step):
            norm_scalar(act, 2)
            act.wait_ge(r_pad, 1)
            for j in range(4):
                unit_scalar(act, R_plan, j, 2, R_x[:, 2 * j:2 * j + 2, TAPS:])
            gate = lambda j: unit_scalar(act, R_plan, j, 2, R_gate[:, 2 * (j - 4):2 * (j - 4) + 2, :], ACT.Gelu_apprx_tanh)
            gate(4)
            for j in range(KT):
                act.wait_ge(r_gates, j + 1)
                bank = ps[:, 2 + j % 2, :]
                nc.scalar.activation(R_r[:, j, :], bank[:, 0:SEQ], ACT.Sigmoid, bias=column("b_a", j))
                nc.scalar.activation(R_i[:, j, :], bank[:, SEQ:], ACT.Sigmoid, bias=column("b_i", j)).then_inc(r_sig, 1)
            act.wait_ge(r_sig, KT)
            for j in range(KT):
                ins = nc.scalar.activation(R_tau[:, j, :], R_r[:, j, :], ACT.Tanh, scale=decay_neg[:, j:j + 1])
            ins.then_inc(r_tau, 1)
            for j in range(KT):
                ins = nc.scalar.activation(R_a[:, j, :], R_r[:, j, :], ACT.Exp, scale=decay_scale[:, j:j + 1])
            ins.then_inc(r_exp, 1)
            gate(5)
            act.wait_ge(r_v, 1)
            nc.scalar.activation(R_u, R_u, ACT.Sqrt, scale=2.0).then_inc(r_mult, 1)
            gate(6)
            gate(7)
            postnorm_scalar(act, 2)

        def R_vector(dve, step):
            nc.vector.memset(R_x[:, :, 0:TAPS], 0.0).then_inc(r_pad, 1)
            norm_vector(dve, 2)
            for u in range(4):
                dve.wait_ge(s_evac, R_plan[u][5] + 1)
                for k in range(CONV_WIDTH):
                    for f in (2 * u, 2 * u + 1):
                        w = column("conv_w", k * KT + f)
                        v = R_x[:, f, k:k + SEQ]
                        if k == 0:
                            ins = nc.vector.tensor_scalar(R_xc[:, f, :], v, w, column("conv_b", f), ALU.mult, ALU.add)
                        else:
                            ins = nc.vector.scalar_tensor_tensor(R_xc[:, f, :], v, w, R_xc[:, f, :], ALU.mult, ALU.add)
                    if k < CONV_WIDTH - 1:
                        step.link(ins)
                ins.then_inc(r_xc, 1)
            dve.wait_ge(r_xc, 4)
            dve.wait_ge(r_sig, KT)
            step.link(nc.vector.tensor_tensor(R_i, R_i, R_xc, ALU.mult))
            dve.wait_ge(r_tau, 1)
            step.link(nc.vector.tensor_scalar(R_u, R_tau, 1.0, None, ALU.add))
            step.link(nc.vector.reciprocal(R_u, R_u))
            nc.vector.tensor_tensor(R_u, R_u, R_tau, ALU.mult).then_inc(r_v, 1)
            dve.wait_ge(r_mult, 1)
            step.link(nc.vector.tensor_tensor(R_u, R_u, R_i, ALU.mult))
            dve.wait_ge(r_exp, 1)
            for f in range(KT):
                ins = nc.vector.tensor_tensor_scan(R_h[:, f, :], R_a[:, f, :], R_u[:, f, :], 0.0, ALU.mult, ALU.add)
            step.link(ins)
            for u in range(4):
                dve.wait_ge(s_evac, R_plan[4 + u][5] + 1)
                nc.vector.tensor_tensor(R_y[:, 2 * u:2 * u + 2, :], R_h[:, 2 * u:2 * u + 2, :],
                                        R_gate[:, 2 * u:2 * u + 2, :], ALU.mult).then_inc(r_out, 1)
            postnorm_vector(dve, step, 2)
        E_sc = [page(i)[:, 0:3 * KEYS].rearrange("p (n k) -> p n k", n=3) for i in (7, 8)]
        E_pt = page(9)[:, 0:2 * KEYS].rearrange("p (n k) -> p n k", n=2)
        E_sq = page(10).rearrange("p (n k) -> p n k", k=512)
        E_rs = page(11).rearrange("p (n k) -> p n k", k=512)
        e_sq, e_nn, e_rt, e_qn, e_s, e_sc, e_mx, e_e, e_pn, e_t, e_pt, e_pv, e_ot = (
            sem("e_" + n) for n in ("sq", "nn", "rt", "qn", "s", "sc", "mx", "e", "pn", "t", "pt", "pv", "ot"))
        E_F = [j for j, u in enumerate(E_plan) if u[0] == "F"]
        NG = 8
        maps_of = lambda g: 3 if g < 4 else 2
        heads_of = lambda g: [g, 4 + g, 8 + g] if g < 4 else [8 + g]
        maps_before = lambda g: sum(maps_of(x) for x in range(g))
        heads_before = lambda g: sum(len(heads_of(x)) for x in range(g))
        E_gain = [gains[:, 0:1]] * 3 + [column("dil_k_gain")] * 3 + [gains[:, 1:2], column("diff_k_gain"), gains[:, 2:3]]
        slope_of = lambda head: 2.0 ** (-8.0 * (head + 1) / (N_DIL + N_DIFF))
        tile_cols = (slice(0, P), slice(P, KEYS))

        def E_rows(i):
            return QK[:, 2 * i:2 * i + 2, :] if i < 8 else OT[:, 6:8, :]

        def E_tensor(pe):
            norm_tensor(pe, 4)

            def sum_squares(i):
                pe.wait_ge(e_sq, i + 1)
                if i >= 2:
                    pe.wait_ge(e_rt, i - 1)
                nc.tensor.matmul(ps[:, 2 + i % 2, :], (ones32 if i in (6, 7) else ones64)[:, :], E_sq[:, i % 2, :],
                                 start=True, stop=True).then_inc(e_nn, 1)

            pe.wait_ge(const_ok, 2)
            for j in range(12):
                unit_tensor(pe, E_plan, j, 2)
                if j - 1 in E_F:
                    sum_squares(E_F.index(j - 1))

            def scores(g):
                for n in range(maps_of(g)):
                    c = maps_before(g) + n
                    if g < 4:
                        head = g + 4 * n
                        fq, fk, r0, width = head // 2, 6 + head // 2, head % 2 * HD, HD
                    else:
                        i = g - 4
                        fq, fk, r0, width = 12 + i // 2, 14 + i // 2, i % 2 * HD + n * HD // 2, HD // 2
                    if c >= 2:
                        pe.wait_ge(e_sc, c - 1)
                    r = slice(r0, r0 + width)
                    nc.tensor.matmul(ps[:, 4 + c % 2, 0:P], QK[r, fq, 0:P], QK[r, fk, 0:P], start=True, stop=True,
                                     tile_position=(r0, 0))
                    nc.tensor.matmul(ps[:, 4 + c % 2, P:KEYS], QK[r, fq, P:SEQ], QK[r, fk, :], start=True, stop=True,
                                     tile_position=(r0, 0)).then_inc(e_s, 1)

            def turn(g, n, c):
                if c >= 2:
                    pe.wait_ge(e_pt, c - 1)
                for b in range(3):
                    mm = nc.tensor.transpose(ps[:, 6 + c % 2, b * P:(b + 1) * P], E_sc[g % 2][:, n, b * P:(b + 1) * P],
                                             ident[:, :])
                mm.then_inc(e_t, 1)

            def values(head, c):
                pe.wait_ge(e_pt, c + 1)
                if c >= 2:
                    pe.wait_ge(e_ot, c - 1)
                o = ps[HD * (head % 2):HD * (head % 2) + HD, 2 + c % 2, :]
                nc.tensor.matmul(o[:, 0:SEQ], V[:, 0, head * HD:(head + 1) * HD], E_pt[:, c % 2, 0:SEQ],
                                 start=True, stop=False)
                nc.tensor.matmul(o[:, P:SEQ], V[:, 1, head * HD:(head + 1) * HD], E_pt[:, c % 2, SEQ:KEYS],
                                 start=False, stop=True).then_inc(e_pv, 1)

            def attend(g):
                pe.wait_ge(e_pn, g + 1)
                hs, c0 = heads_of(g), heads_before(g)
                turn(g, 0, c0)
                for n, head in enumerate(hs):
                    if n + 1 < len(hs):
                        turn(g, n + 1, c0 + n + 1)
                    values(head, c0 + n)

            pe.wait_ge(e_qn, 8)
            scores(0)
            for g in range(NG):
                if g + 1 < NG:
                    scores(g + 1)
                attend(g)
            sum_squares(8)
            pe.wait_ge(e_qn, 9)
            out_tensor(pe, E_out, OT)

        def E_scalar(act, step):
            norm_scalar(act, 4)

            def squares(i):
                if i >= 2:
                    act.wait_ge(e_nn, i - 1)
                nc.scalar.activation(E_sq[:, i % 2, :], E_rows(i).rearrange("p f t -> p (f t)"), ACT.Square).then_inc(e_sq, 1)

            def root(i):
                act.wait_ge(e_nn, i + 1)
                if i >= 2:
                    act.wait_ge(e_qn, i - 1)
                nc.scalar.activation(E_rs[:, i % 2, :], ps[:, 2 + i % 2, :], ACT.Sqrt, bias=epscol[:, 0:1],
                                     scale=1.0 / (HD // 2 if i in (6, 7) else HD)).then_inc(e_rt, 1)

            for j in range(12):
                kind, tt = E_plan[j][0], E_plan[j][4]
                if kind == "F":
                    i = E_F.index(j)
                    unit_scalar(act, E_plan, j, 2, QK[:, 2 * i:2 * i + 2, :])
                    act.wait_ge(s_evac, E_plan[j][5] + 1)
                    squares(i)
                elif kind == "T":
                    unit_scalar(act, E_plan, j, 2, V[:, tt, 0:512])
                else:
                    c0 = 512 if j == 8 else 768
                    unit_scalar(act, E_plan, j, 2, V[:, :, c0:c0 + 256])
                if j - 1 in E_F:
                    root(E_F.index(j - 1))

            def exps(g):
                act.wait_ge(e_mx, g + 1)
                sc = E_sc[g % 2]
                for t, c in enumerate(tile_cols):
                    for m in range(1 if g < 4 else 2):
                        v = sc[:, 0:3, c] if g < 4 else sc[:, m, c]
                        k = 2 * g + m
                        ins = nc.scalar.activation(v, v, ACT.Exp, bias=neg_max[:, t, k:k + 1], accum_out=sums[:, t, k:k + 1])
                ins.then_inc(e_e, 1)

            def copies(g):
                c0, hs = heads_before(g), heads_of(g)
                for c in range(c0, c0 + len(hs) + 1):
                    if c < c0 + len(hs):
                        act.wait_ge(e_t, c + 1)
                        if c >= 2:
                            act.wait_ge(e_pv, c - 1)
                        nc.scalar.activation(E_pt[:, c % 2, :], ps[:, 6 + c % 2, 0:KEYS], ACT.Copy).then_inc(e_pt, 1)
                    if c > c0:
                        head = hs[c - 1 - c0]
                        r = slice(HD * (head % 2), HD * (head % 2) + HD)
                        act.wait_ge(e_pv, c)
                        nc.scalar.activation(OT[r, head // 2, :], ps[r, 2 + (c - 1) % 2, 0:SEQ], ACT.Copy).then_inc(e_ot, 1)

            exps(0)
            for g in range(NG):
                if g + 1 < NG:
                    exps(g + 1)
                copies(g)
            act.wait_ge(e_ot, 16)
            squares(8)
            root(8)

        def E_vector(dve, step):
            norm_vector(dve, 4)

            def normalise(i):
                dve.wait_ge(e_rt, i + 1)
                step.link(nc.vector.reciprocal(E_rs[:, i % 2, :], E_rs[:, i % 2, :]))
                v = E_rows(i).rearrange("p f t -> p (f t)")
                nc.vector.scalar_tensor_tensor(v, v, E_gain[i], E_rs[:, i % 2, :], ALU.mult, ALU.mult).then_inc(e_qn, 1)

            for i in range(8):
                normalise(i)
            dve.wait_ge(const_ok, 2)

            def biased(g):
                sc = E_sc[g % 2]
                if g >= 2:
                    dve.wait_ge(e_t, heads_before(g - 1))
                for n in range(maps_of(g)):
                    c = maps_before(g) + n
                    head, d = (g + 4 * n, n) if g < 4 else (8 + g, 3)
                    dve.wait_ge(e_s, c + 1)
                    nc.vector.scalar_tensor_tensor(sc[:, n, :], dist[:, d, :], -slope_of(head), ps[:, 4 + c % 2, 0:KEYS],
                                                   ALU.mult, ALU.add).then_inc(e_sc, 1)
                dve.wait_ge(e_sc, maps_before(g + 1))
                for t, c in enumerate(tile_cols):
                    if g < 4:
                        ins = nc.vector.tensor_reduce(neg_max[:, t, 2 * g:2 * g + 1], sc[:, :, c], AX.XY, ALU.max, negate=True)
                    else:
                        ins = nc.vector.tensor_reduce(neg_max[:, t, 2 * g:2 * g + 2], sc[:, 0:2, c], AX.X, ALU.max, negate=True)
                ins.then_inc(e_mx, 1)

            def normalised(g):
                sc = E_sc[g % 2]
                dve.wait_ge(e_e, g + 1)
                k = 2 * g
                if g < 4:
                    step.link(nc.vector.reciprocal(sums[:, :, k:k + 1], sums[:, :, k:k + 1]))
                    for t, c in enumerate(tile_cols):
                        ins = nc.vector.tensor_scalar(sc[:, :, c], sc[:, :, c], sums[:, t, k:k + 1], None, ALU.mult)
                else:
                    step.link(nc.vector.reciprocal(sums[:, :, k:k + 2], sums[:, :, k:k + 2]))
                    step.link(nc.vector.tensor_scalar(sums[:, :, k + 1:k + 2], sums[:, :, k + 1:k + 2], neg_lam, None, ALU.mult))
                    for t, c in enumerate(tile_cols):
                        ins = nc.vector.tensor_scalar(sc[:, 0, c], sc[:, 0, c], sums[:, t, k:k + 1], None, ALU.mult)
                    step.link(ins)
                    for t, c in enumerate(tile_cols):
                        ins = nc.vector.scalar_tensor_tensor(sc[:, 0, c], sc[:, 1, c], sums[:, t, k + 1:k + 2], sc[:, 0, c],
                                                             ALU.mult, ALU.add)
                ins.then_inc(e_pn, 1)

            biased(0)
            for g in range(NG):
                if g + 1 < NG:
                    biased(g + 1)
                normalised(g)
            normalise(8)
            residual_vector(dve, 4)

        G_q, G_k, G_b, G_g, G_o = (tiles(i) for i in (3, 4, 5, 7, 8))
        G_v = page(6).rearrange("p (t d) -> p t d", t=TT)
        G_ls, G_mx, G_ad = (page(i).rearrange("p (u n) -> p u n", u=4) for i in (9, 10, 11))
        G_pr = page(9, 2).rearrange("p (r n t) -> p r n t", r=4, n=4)
        G_e = page(11).rearrange("p (r n t) -> p r n t", r=2, n=4)
        G_tmp = page(2)
        G_st = G_tmp[:, 0:2 * 3 * P].rearrange("p (r c v) -> p r c v", r=2, c=3)
        G_ks = G_tmp[:, 768:768 + 2 * SEQ].rearrange("p (r t k) -> p r t k", r=2, t=TT)
        G_dec = G_tmp[:, 1280:1280 + HG * 4].rearrange("p (h c) -> p h c", h=HG)
        g_na, g_ln, g_kk, g_k, g_b, g_d, g_ex, g_pr, g_t, g_ks, g_s, g_at, g_kv, g_st, g_o, g_oc, g_sq, g_nn, g_rt, g_y = (
            sem("g_" + n) for n in ("na", "ln", "kk", "k", "b", "d", "ex", "pr", "t", "ks", "s", "at", "kv", "st", "o",
                                    "oc", "sq", "nn", "rt", "y"))
        G_evac = lambda j: G_plan[j][5] + 1

        def G_tensor(pe):
            norm_tensor(pe, 6)
            for j in range(16):
                unit_tensor(pe, G_plan, j, 4)

            def scores(h):
                pe.wait_ge(g_pr, h + 1)
                if h >= 1:
                    pe.wait_ge(g_ks, h)
                for t in range(TT):
                    mm = nc.tensor.transpose(ps[:, 5, t * P:(t + 1) * P], G_pr[:, h % 4, 3, t * P:(t + 1) * P], ident[:, :])
                mm.then_inc(g_t, 1)
                if h >= 1:
                    pe.wait_ge(g_at, h)
                for t in range(TT):
                    for q in range(4):
                        c0 = t * P + q // 2 * CHUNK
                        first = q % 2 * 32
                        mm = nc.tensor.matmul(ps[32 * q:32 * q + 32, 4, t * CHUNK + first:(t + 1) * CHUNK],
                                              G_pr[:, h % 4, 1, c0 + first:c0 + first + 32],
                                              G_pr[:, h % 4, 0, c0 + first:c0 + CHUNK], start=True, stop=True)
                mm.then_inc(g_s, 1)

            def states(h):
                pe.wait_ge(g_ks, h + 1)
                if h >= 1:
                    pe.wait_ge(g_st, h)
                else:
                    pe.wait_ge(s_evac, G_evac(12))
                for c in range(3):
                    r = slice(c % 2 * CHUNK, c % 2 * CHUNK + CHUNK)
                    mm = nc.tensor.matmul(ps[:, c % 2 * -6 + 6, c * P:(c + 1) * P], G_ks[r, h % 2, c // 2, :],
                                          G_v[r, c // 2, h * P:(h + 1) * P], start=True, stop=True)
                mm.then_inc(g_kv, 1)

            def outputs(h):
                pe.wait_ge(g_at, h + 1)
                if h >= 1:
                    pe.wait_ge(g_oc, h)
                for t in range(TT):
                    nc.tensor.matmul(ps[:, 7, t * P:(t + 1) * P], G_v[:, t, h * P:(h + 1) * P], scores_T[:, h % 2, t, :],
                                     start=(t == 0), stop=False, skip_group_check=True)
                pe.wait_ge(g_st, h + 1)
                for c in range(1, 4):
                    mm = nc.tensor.matmul(ps[:, 7, c * CHUNK:(c + 1) * CHUNK], G_st[:, h % 2, c - 1, :],
                                          G_pr[:, h % 4, 2, c * CHUNK:(c + 1) * CHUNK], start=False, stop=(c == 3),
                                          skip_group_check=True)
                mm.then_inc(g_o, 1)

            pe.wait_ge(s_evac, G_evac(11))
            scores(0)
            for h in range(HG):
                states(h)
                if h + 1 < HG:
                    scores(h + 1)
                outputs(h)
            for u in range(4):
                pe.wait_ge(g_sq, u + 1)
                nc.tensor.matmul(ps[:, u, :], ones128[:, :], G_ls[:, u, :], start=True, stop=True).then_inc(g_nn, 1)
            pe.wait_ge(g_y, 4)
            out_tensor(pe, G_out, G_o)

        def G_scalar(act, step):
            norm_scalar(act, 6)
            for u in range(4):
                unit_scalar(act, G_plan, u, 4, G_b[:, 2 * u:2 * u + 2, :])
                act.wait_ge(g_na, u + 1)
                step.link(nc.scalar.activation(G_ls[:, u, :], G_ls[:, u, :], ACT.Exp))
                nc.scalar.activation(G_ls[:, u, :], G_ls[:, u, :], ACT.Ln, bias=1.0).then_inc(g_ln, 1)
                act.wait_ge(g_kk, u + 1)
                step.link(nc.scalar.activation(G_ad[:, u, :], G_ad[:, u, :], ACT.Exp))
                nc.scalar.activation(G_ad[:, u, :], G_ad[:, u, :], ACT.Ln, bias=1.0)
                for f in (2 * u, 2 * u + 1):
                    ins = nc.scalar.activation(G_k[:, f, :], G_ls[:, u, (f % 2) * SEQ:(f % 2 + 1) * SEQ], ACT.Exp,
                                               bias=ln_1lb[:, f:f + 1])
                ins.then_inc(g_k, 1)
            for u in range(4):
                unit_scalar(act, G_plan, 4 + u, 4, G_q[:, 2 * u:2 * u + 2, :], ACT.Silu)

            def exps(h):
                act.wait_ge(g_d, h + 1)
                if h >= 2:
                    act.wait_ge(g_pr, h - 1)
                e = G_e[:, h % 2]
                nc.scalar.activation(e[:, 1], e[:, 0], ACT.Exp, scale=-1.0)
                nc.scalar.activation(e[:, 3], G_b[:, h, :], ACT.Exp)
                step.link(nc.scalar.activation(e[:, 2], e[:, 2], ACT.Exp))
                nc.scalar.activation(e[:, 0], e[:, 0], ACT.Exp).then_inc(g_ex, 1)

            def keys(h):
                act.wait_ge(g_t, h + 1)
                if h >= 2:
                    act.wait_ge(g_kv, h - 1)
                nc.scalar.activation(G_ks[:, h % 2], ps[:, 5, 0:SEQ].rearrange("p (t k) -> p t k", t=TT), ACT.Copy)\
                    .then_inc(g_ks, 1)

            def output(h):
                act.wait_ge(g_o, h + 1)
                nc.scalar.activation(G_o[:, h, :], ps[:, 7, 0:SEQ], ACT.Copy).then_inc(g_oc, 1)

            for i in range(4):
                unit_scalar(act, G_plan, 8 + i, 4, G_v[:, i % 2, i // 2 * 512:(i // 2 + 1) * 512])
                exps(i)
            for u in range(4):
                unit_scalar(act, G_plan, 12 + u, 4, G_g[:, 2 * u:2 * u + 2, :], ACT.Sigmoid)
            keys(0)
            for h in range(HG):
                if h + 4 < HG:
                    exps(h + 4)
                if h + 1 < HG:
                    keys(h + 1)
                output(h)
            for u in range(4):
                act.wait_ge(g_oc, 2 * u + 2)
                nc.scalar.activation(G_ls[:, u, :], G_o[:, 2 * u:2 * u + 2, :].rearrange("p f t -> p (f t)"), ACT.Square)\
                    .then_inc(g_sq, 1)
            for u in range(4):
                act.wait_ge(g_nn, u + 1)
                nc.scalar.activation(G_ad[:, u, :], ps[:, u, :], ACT.Sqrt, bias=epscol[:, 0:1], scale=1.0 / P).then_inc(g_rt, 1)

        def G_vector(dve, step):
            norm_vector(dve, 6)
            for u in range(4):
                f2 = G_b[:, 2 * u:2 * u + 2, :].rearrange("p f t -> p (f t)")
                ls, mx, ad = G_ls[:, u, :], G_mx[:, u, :], G_ad[:, u, :]
                dve.wait_ge(s_evac, G_evac(u))
                nc.vector.scalar_tensor_tensor(ls, f2, -1.0, f2, ALU.mult, ALU.min).then_inc(g_na, 1)
                dve.wait_ge(g_ln, u + 1)
                step.link(nc.vector.scalar_tensor_tensor(ls, f2, 0.0, ls, ALU.min, ALU.subtract))
                for f in (2 * u, 2 * u + 1):
                    c = slice(f % 2 * SEQ, (f % 2 + 1) * SEQ)
                    nc.vector.tensor_scalar(mx[:, c], ls[:, c], ln_1lb[:, f:f + 1], ln_lb[:, f:f + 1], ALU.add, ALU.max)
                    ins = nc.vector.tensor_scalar(ad[:, c], ls[:, c], ln_dif[:, f:f + 1], None, ALU.add)
                step.link(ins)
                step.link(nc.vector.scalar_tensor_tensor(ad, ad, -1.0, ad, ALU.mult, ALU.min))
                nc.vector.tensor_tensor(ls, ls, f2, ALU.subtract).then_inc(g_kk, 1)
                dve.wait_ge(g_k, u + 1)
                step.link(nc.vector.tensor_tensor(mx, mx, ad, ALU.add))
                for f in (2 * u, 2 * u + 1):
                    ins = nc.vector.tensor_tensor_scan(G_b[:, f, :], restart[:, :], mx[:, f % 2 * SEQ:(f % 2 + 1) * SEQ], 0.0,
                                                       ALU.mult, ALU.add)
                ins.then_inc(g_b, 1)

            chunks = lambda v: v.rearrange("p (c t) -> p c t", t=CHUNK)

            def exponents(h):
                dve.wait_ge(g_b, h // 2 + 1)
                if h >= 2:
                    dve.wait_ge(g_pr, h - 1)
                b, e = chunks(G_b[:, h, :]), G_e[:, h % 2]
                if h < 2:
                    dve.wait_ge(g_b, 4)
                nc.vector.tensor_tensor(chunks(e[:, 0]), b, b[:, :, CHUNK // 2:CHUNK // 2 + 1].to_broadcast([P, 4, CHUNK]),
                                        ALU.subtract)
                nc.vector.tensor_tensor(chunks(e[:, 2]), b[:, :, CHUNK - 1:CHUNK].to_broadcast([P, 4, CHUNK]), b,
                                        ALU.subtract).then_inc(g_d, 1)

            def products(h):
                dve.wait_ge(g_ex, h + 1)
                dve.wait_ge(s_evac, G_evac(4 + h // 2))
                if h >= 4:
                    dve.wait_ge(g_o, h - 3)
                e, pr = G_e[:, h % 2], G_pr[:, h % 4]
                nc.vector.tensor_copy(G_dec[:, h, :], chunks(e[:, 3])[:, :, CHUNK - 1])
                for n, (x, y) in enumerate(((G_q, 0), (G_k, 1), (G_q, 3), (G_k, 2))):
                    ins = nc.vector.tensor_tensor(pr[:, n], x[:, h, :], e[:, y], ALU.mult)
                ins.then_inc(g_pr, 1)

            def seen(h):
                dve.wait_ge(g_s, h + 1)
                if h >= 2:
                    dve.wait_ge(g_o, h - 1)
                for q in range(4):
                    r, first = slice(32 * q, 32 * q + 32), q % 2 * 32
                    c0 = q // 2 * CHUNK
                    ins = nc.vector.copy_predicated(scores_T[r, h % 2, :, c0 + first:c0 + CHUNK],
                                                    causal[r, :, first:CHUNK].bitcast(I32),
                                                    ps[r, 4, 0:P].rearrange("p (t c) -> p t c", t=TT)[:, :, first:CHUNK])
                ins.then_inc(g_at, 1)

            def states(h):
                dve.wait_ge(g_kv, h + 1)
                st = G_st[:, h % 2]
                step.link(nc.vector.tensor_copy(st[:, 0], ps[:, 6, 0:P]))
                step.link(nc.vector.scalar_tensor_tensor(st[:, 1], st[:, 0], G_dec[:, h, 1:2], ps[:, 0, P:2 * P],
                                                         ALU.mult, ALU.add))
                nc.vector.scalar_tensor_tensor(st[:, 2], st[:, 1], G_dec[:, h, 2:3], ps[:, 6, 2 * P:3 * P],
                                               ALU.mult, ALU.add).then_inc(g_st, 1)

            exponents(0)
            for h in range(4):
                if h < 3:
                    exponents(h + 1)
                products(h)
            for h in range(HG):
                if h + 4 < HG:
                    exponents(h + 4)
                seen(h)
                states(h)
                if h + 4 < HG:
                    products(h + 4)
            for u in range(4):
                o = G_o[:, 2 * u:2 * u + 2, :].rearrange("p f t -> p (f t)")
                dve.wait_ge(g_rt, u + 1)
                step.link(nc.vector.reciprocal(G_ad[:, u, :], G_ad[:, u, :]))
                step.link(nc.vector.scalar_tensor_tensor(o, o, column("hgrn_out_gain"), G_ad[:, u, :], ALU.mult, ALU.mult))
                dve.wait_ge(s_evac, G_evac(12 + u))
                nc.vector.tensor_tensor(o, o, G_g[:, 2 * u:2 * u + 2, :].rearrange("p f t -> p (f t)"), ALU.mult)\
                    .then_inc(g_y, 1)
            residual_vector(dve, 6)

        LOGIT, OH0, OH1, MASK, GATE, POS, TMP, CUM = (rt[:, n, :].rearrange("p (t e) -> p t e", t=TT) for n in range(8))
        M_top = rt[:, 8, 0:4].rearrange("p (n t o) -> p n t o", n=2, t=TT)
        M_w = rt[:, 9, 0:4].rearrange("p (n t o) -> p n t o", n=2, t=TT)
        M_cnt = rt[:, 10, :]
        XTE = page(1)[:, 0:KT * CAP].rearrange("p (k j) -> p k j", k=KT)
        M_sg = page(3)[:, 0:1024].rearrange("p (r n) -> p r n", r=2)
        M_h = page(3)[:, 1024:2048].rearrange("p (r n) -> p r n", r=2)
        M_hT = page(4)[:, 0:1024].rearrange("p (r f j) -> p r f j", r=2, f=4)
        M_y = page(5)[:, 0:D]
        M_sel = page(6)[:, 0:TT * CAP].rearrange("p (t j) -> p t j", t=TT)
        M_selg = page(6)[:, 256:256 + TT * CAP].rearrange("p (t j) -> p t j", t=TT)
        M_selT = page(6)[:, 512:512 + SEQ]
        m_lg, m_top, m_ex, m_mask, m_pos, m_route = (sem("m_" + n) for n in ("lg", "top", "ex", "mask", "pos", "route"))
        m_g, m_tt, m_ht, m_dn, m_sel, m_ga, m_xt, m_tr, m_st, m_sct, m_sc, m_yc = (
            sem("m_" + n) for n in ("g", "tt", "ht", "dn", "sel", "ga", "xt", "tr", "st", "sct", "sc", "yc"))
        B_M = 3 * FT_FF
        M_n0 = list(count)
        E_load = lambda k: (k % NS, k // NS)

        def before_use(c):
            return c - 1 if c != 0 else 0

        def gather(pe, half):
            for kt in range(4):
                for t in range(TT):
                    f = (4 * half + kt) * P
                    mm = nc.tensor.matmul(ps[:, 7, kt * CAP:(kt + 1) * CAP], XN[:, t, f:f + P], M_sel[:, t, :],
                                          start=(t == 0), stop=(t == TT - 1))
            mm.then_inc(m_ga, 1)

        def scatter(r, bank):
            return nc.tensor.matmul(ps[:, bank, :], M_selT[:, r // 2 * P:(r // 2 + 1) * P],
                                    M_y[:, r % 2 * 512:(r % 2 + 1) * 512], start=True, stop=True)

        def M_tensor(pe):
            norm_tensor(pe, 7)
            pe.wait_ge(side_in, 16 * 6)
            for t in range(TT):
                for kt in range(KT):
                    mm = nc.tensor.matmul(ps[:, 4, t * NE:(t + 1) * NE], HT[:, kt, t * P:(t + 1) * P], wrouter[:, kt, :],
                                          start=(kt == 0), stop=(kt == KT - 1))
            mm.then_inc(m_lg, 1)
            pe.wait_ge(m_mask, 1)
            nc.tensor.matmul(ps[:, 5, 0:NE], before[:, :], MASK[:, 0, :], start=True, stop=True)
            nc.tensor.matmul(ps[:, 5, NE:2 * NE], ones128[:, :], MASK[:, 0, :], start=True, stop=False)
            nc.tensor.matmul(ps[:, 5, NE:2 * NE], before[:, :], MASK[:, 1, :], start=False, stop=True)
            for t in range(TT):
                mm = nc.tensor.matmul(ps[:, 5, 2 * NE:3 * NE], ones128[:, :], MASK[:, t, :], start=(t == 0), stop=(t == TT - 1))
            mm.then_inc(m_pos, 1)
            pe.wait_ge(m_route, 1)
            n = pe.value_load(nblk[0:1, 0:1], min_val=1, max_val=2)
            pe.wait_ge(m_sel, 1)
            gather(pe, 0)
            pe.wait_ge(m_xt, 1)
            gather(pe, 1)

            def turn(i, c):
                pe.wait_ge(s_h, 7 * i + (B_M + c + 1))
                pe.wait_ge(m_ht, 7 * i + (c + 1))
                for f in range(4):
                    mm = nc.tensor.transpose(ps[:, 4, f * CAP:(f + 1) * CAP], M_h[:, c % 2, f * P:(f + 1) * P], ident[:, :])
                mm.then_inc(m_tt, 1)

            def down_chunk(i, c):
                s, r = E_load(3 * c + 2)
                pe.wait_ge(landed[s], 48 * i + (M_n0[s] + 16 * (r + 1)))
                pe.wait_ge(m_ht, 7 * i + (c + 2))
                if c == 0:
                    pe.wait_ge(m_yc, i + 1)
                w = ring[:, s, :].rearrange("p (r n) -> p r n", n=D)
                for r in range(4):
                    for h in range(2):
                        mm = nc.tensor.matmul(ps[:, 5 + h, :], M_hT[:, c % 2, r, :], w[:, r, h * 512:(h + 1) * 512],
                                              start=(c == 0 and r == 0), stop=(c == CE - 1 and r == 3))
                mm.then_inc(m_dn, 1)

            with pe.Fori(0, n * NE) as i:
                pe.wait_ge(m_xt, 2 * i + 2)
                for c in range(CE):
                    for u, (bank, read, done) in enumerate(((c % 2, s_sg, m_g), (2 + c % 2, s_h, s_gu))):
                        s, r = E_load(3 * c + u)
                        pe.wait_ge(landed[s], 48 * i + (M_n0[s] + 16 * (r + 1)))
                        pe.wait_ge(read, 7 * i + (B_M + c - (c > 0)) if c != 1 else 7 * i + (B_M - 1))
                        for kt in range(KT):
                            mm = nc.tensor.matmul(ps[:, bank, :], XTE[:, kt, :], slot_k(s)[:, kt, :],
                                                  start=(kt == 0), stop=(kt == KT - 1))
                        mm.then_inc(done, 1)
                        if u == 0 and c >= 1:
                            turn(i, c - 1)
                    if c >= 1:
                        down_chunk(i, c - 1)
                    if c == 0:
                        pe.wait_ge(m_yc, i + 1)
                        scatter(0, 7).then_inc(m_sct, 1)
                    elif c < 4:
                        pe.wait_ge(m_sc, 4 * i + c)
                        scatter(c, 7).then_inc(m_sct, 1)
                    elif c == 4:
                        pe.wait_ge(m_sc, 4 * i + 4)
                        pe.wait_ge(m_sel, i + 1)
                        for t in range(TT):
                            mm = nc.tensor.transpose(ps[:, 7, t * P:(t + 1) * P], M_selg[:, t, :], ident[:, :])
                        mm.then_inc(m_tr, 1)
                    elif c == 5:
                        pe.wait_ge(m_st, i + 1)
                        pe.wait_ge(m_sel, i + 2)
                        gather(pe, 0)
                turn(i, CE - 1)
                pe.wait_ge(m_xt, 2 * i + 3)
                gather(pe, 1)
                down_chunk(i, CE - 1)
            pe.wait_ge(m_xt, n * (2 * NE) + 2)
            pe.wait_ge(m_yc, n * NE + 1)
            for r, bank in enumerate((7, 0, 1, 2)):
                scatter(r, bank).then_inc(m_sct, 1)

        def M_scalar(act, step):
            norm_scalar(act, 7)
            act.wait_ge(m_top, 1)
            nc.scalar.activation(M_w[:, 1], M_w[:, 1], ACT.Exp).then_inc(m_ex, 1)
            act.wait_ge(m_route, 1)
            n = act.value_load(nblk[0:1, 0:1], min_val=1, max_val=2)

            def evac_turned(i, c):
                act.wait_ge(m_tt, 7 * i + (c + 1))
                nc.scalar.activation(M_hT[:, c % 2].rearrange("p f j -> p (f j)"), ps[:, 4, :], ACT.Copy).then_inc(m_ht, 1)

            with act.Fori(0, n * NE) as i:
                for c in range(CE):
                    act.wait_ge(m_g, 7 * i + (c + 1))
                    act.wait_ge(s_h, 7 * i + (B_M + c - (c > 0)) if c != 1 else 7 * i + (B_M - 1))
                    nc.scalar.activation(M_sg[:, c % 2, :], ps[:, c % 2, :], ACT.Silu).then_inc(s_sg, 1)
                    if c >= 1:
                        evac_turned(i, c - 1)
                    if c == 4:
                        act.wait_ge(m_tr, i + 1)
                        nc.scalar.activation(M_selT, ps[:, 7, 0:SEQ], ACT.Copy).then_inc(m_st, 1)
                evac_turned(i, CE - 1)
                act.wait_ge(m_dn, 7 * i + 7)
                nc.scalar.activation(M_y.rearrange("p (h n) -> p h n", h=2), ps[:, 5:7, :], ACT.Copy).then_inc(m_yc, 1)

        def M_vector(dve, step):
            nc.vector.memset(M_selT, 0.0).then_inc(m_ht, 1)
            nc.vector.memset(M_y, 0.0).then_inc(m_yc, 1)
            norm_vector(dve, 7)
            dve.wait_ge(m_lg, 1)
            step.link(nc.vector.tensor_copy(LOGIT, ps[:, 4, 0:TT * NE].rearrange("p (t e) -> p t e", t=TT)))
            src = LOGIT
            for k, onehot in enumerate((OH0, OH1)):
                step.link(nc.vector.tensor_reduce(M_top[:, k], src, AX.X, ALU.max))
                if k == 1:
                    nc.vector.tensor_tensor(M_w[:, 1], M_top[:, 1], M_top[:, 0], ALU.subtract).then_inc(m_top, 1)
                step.link(nc.vector.tensor_tensor(onehot, src, M_top[:, k].to_broadcast([P, TT, NE]), ALU.is_equal))
                for t in range(TT):
                    ins = nc.vector.tensor_tensor_scan(CUM[:, t, :], onehot[:, t, :], onehot[:, t, :], 0.0, ALU.add, ALU.bypass)
                step.link(ins)
                step.link(nc.vector.scalar_tensor_tensor(onehot, CUM, 1.0, onehot, ALU.is_equal, ALU.mult))
                if k == 0:
                    step.link(nc.vector.scalar_tensor_tensor(TMP, OH0, -MASKED, LOGIT, ALU.mult, ALU.add))
                    src = TMP
            nc.vector.tensor_tensor(MASK, OH0, OH1, ALU.add).then_inc(m_mask, 1)
            dve.wait_ge(m_ex, 1)
            step.link(nc.vector.tensor_scalar(M_w[:, 0], M_w[:, 1], 1.0, None, ALU.add))
            step.link(nc.vector.reciprocal(M_w[:, 0], M_w[:, 0]))
            step.link(nc.vector.tensor_tensor(M_w[:, 1], M_w[:, 1], M_w[:, 0], ALU.mult))
            for k, onehot in enumerate((OH0, OH1)):
                ins = nc.vector.tensor_tensor(onehot, onehot, M_w[:, k].to_broadcast([P, TT, NE]), ALU.mult)
            step.link(ins)
            step.link(nc.vector.tensor_tensor(GATE, OH0, OH1, ALU.add))
            dve.wait_ge(m_pos, 1)
            step.link(nc.vector.tensor_reduce(M_cnt[0:1, 0:1], ps[0:1, 5, 2 * NE:3 * NE], AX.X, ALU.max))
            step.link(nc.vector.tensor_scalar(nblk[0:1, 0:1], M_cnt[0:1, 0:1], float(CAP), 1.0, ALU.is_gt, ALU.add))
            nc.vector.scalar_tensor_tensor(POS, ps[:, 5, 0:2 * NE].rearrange("p (t e) -> p t e", t=TT), 1.0, MASK,
                                           ALU.add, ALU.mult).then_inc(m_route, 1)
            dve.wait_ge(m_route, 1)
            step.link(nc.vector.tensor_scalar(POS, POS, -1.0, None, ALU.add))
            n = dve.value_load(nblk[0:1, 0:1], min_val=1, max_val=2)

            def select(e, b):
                for v, scale in ((M_selg, True), (M_sel, False)):
                    for t in range(TT):
                        ins = nc.vector.tensor_scalar(v[:, t, :], iota_j[:, bass.ds(b * CAP, CAP)] if not isinstance(b, int) else
                                                      iota_j[:, b * CAP:(b + 1) * CAP],
                                                      POS[:, t, bass.ds(e, 1)], GATE[:, t, bass.ds(e, 1)] if scale else None,
                                                      ALU.is_equal, *((ALU.mult,) if scale else ()))
                ins.then_inc(m_sel, 1)

            def gathered(half):
                g = column("moe_norm", 4 * half, 4).rearrange("p (k o) -> p k o", o=1).to_broadcast([P, 4, CAP])
                nc.vector.tensor_tensor(XTE[:, 4 * half:4 * half + 4, :], ps[:, 7, :].rearrange("p (k j) -> p k j", k=4), g,
                                        ALU.mult).then_inc(m_xt, 1)

            def scattered(r, bank, done):
                x = X[:, r // 2, r % 2 * 512:(r % 2 + 1) * 512]
                nc.vector.tensor_tensor(x, x, ps[:, bank, :], ALU.add).then_inc(done, 1)

            select(0, 0)
            for half in range(2):
                dve.wait_ge(m_ga, half + 1)
                gathered(half)
            with dve.Fori(0, n * NE) as i:
                for c in range(CE):
                    dve.wait_ge(s_gu, 7 * i + (B_M + c + 1))
                    dve.wait_ge(s_sg, 7 * i + (B_M + c + 1))
                    nc.vector.tensor_tensor(M_h[:, c % 2, :], M_sg[:, c % 2, :], ps[:, 2 + c % 2, :], ALU.mult).then_inc(s_h, 1)
                    if c < 4:
                        dve.wait_ge(m_sct, 4 * i + (c + 1))
                        scattered(c, 7, m_sc)
                    elif c == 4:
                        dve.wait_ge(m_tr, i + 1)
                        select((i + 1) & (NE - 1), (i + 1) >> 3)
                for half in range(2):
                    dve.wait_ge(m_ga, 2 * i + (3 + half))
                    gathered(half)
            for r, bank in enumerate((7, 0, 1, 2)):
                dve.wait_ge(m_sct, n * (4 * NE) + (r + 1))
                scattered(r, bank, s_x if r % 2 else m_sc)


        @block.sync
        def _(sp):
            sp.dma_start(X, a["x"][0].rearrange("(t p) d -> p t d", p=P)).then_inc(x_in, 16)
            for item in stream:
                if isinstance(item, dict):
                    ffn_sync(sp, item)
                    continue
                s, pairs, used = item
                if used:
                    sp.wait_ge(*used)
                for dst, src in pairs:
                    sp.dma_start(dst, src).then_inc(landed[s], 16)
            def expert_load(e, k):
                s, _ = E_load(k)
                c, kind = k // 3, k % 3
                one = lambda w: w[0][bass.ds(e, 1)] if not isinstance(e, int) else w[0][e:e + 1]
                if kind < 2:
                    w = one(a[("moe_w_gate_2", "moe_w_up_2")[kind]])
                    src = w.rearrange("o (k p) n -> p (o k) n", p=P)[:, :, c * 512:(c + 1) * 512]
                    dst = slot_k(s)
                else:
                    w = one(a["moe_w_down_2"])
                    src = w.rearrange("o (r p) n -> p (o r) n", p=P)[:, 4 * c:4 * c + 4, :]
                    dst = ring[:, s, :].rearrange("p (r n) -> p r n", n=D)
                sp.dma_start(dst, src).then_inc(landed[s], 16)

            def used(k, i):
                c, kind = k // 3, k % 3
                done, base = ((m_g, 0), (s_gu, B_M), (m_dn, 0))[kind]
                sp.wait_ge(done, 7 * i + (base + c + 1))

            for k in range(NLOAD_E):
                if k < NS_EARLY:
                    sp.wait_ge(*freed[k])
                elif k < NS:
                    sp.wait_ge(s_y, 14)
                else:
                    used(k - NS, 0)
                expert_load(0, k)
            sp.wait_ge(m_route, 1)
            n = sp.value_load(nblk[0:1, 0:1], min_val=1, max_val=2)
            with sp.Fori(1, n * NE) as i:
                expert = sp.snap(sp.to_reg(i & (NE - 1)))
                for k in range(NLOAD_E):
                    if k < NS:
                        c, kind = (k + NLOAD_E - NS) // 3, (k + NLOAD_E - NS) % 3
                        done, base = ((m_g, 0), (s_gu, B_M), (m_dn, 0))[kind]
                        sp.wait_ge(done, 7 * i + (base + c + 1 - 7))
                    else:
                        used(k - NS, i)
                    expert_load(expert, k)
            out_v = out[0].rearrange("(t p) d -> p t d", p=P)
            for t in range(TT):
                sp.wait_ge(s_x, 15 + t)
                sp.dma_start(out_v[:, t, :], X[:, t, :]).then_inc(s_out, 16)
            sp.wait_ge(s_out, 16 * TT)

        @block.gpsimd
        def _(pool):
            step = Steps(pool, pool_step)
            bias = a["attn_rel_bias"]
            pool.dma_start(gpost[:, :], a["norm_mix_post"][0].partition_broadcast(P)).then_inc(gpost_in, 16)
            pool.dma_start(A_bias, bass.AP(tensor=bias.tensor, offset=1,
                                           ap=[[1, P], [2 * REL_CLIP + 1, N_HEADS_A], [1, KEYS]])).then_inc(side_in, 16)
            for i, name in enumerate(lam_names):
                pool.dma_start(lamv[:, i, :], a[name][0].partition_broadcast(P)).then_inc(side_in, 16)
            pool.dma_start(wrouter[:, :, :], a["moe_w_router_2"][0].rearrange("(k p) e -> p k e", p=P)).then_inc(side_in, 16)
            setup_gpsimd(pool, step)
            posts = ["norm_mix_post", "norm_ffn_post"]
            for k in range(8):
                norm_gpsimd(pool, step, k)
                if k < 4:
                    postnorm_gpsimd(pool, step, k)
                    if k < 3:
                        pool.wait_ge(s_x, 2 * k + 2)
                        pool.dma_start(gpost[:, :], a[posts[(k + 1) % 2]][(k + 1) // 2].partition_broadcast(P))\
                            .then_inc(gpost_in, 16)

        @block.scalar
        def _(act):
            step = Steps(act, act_step)
            setup_loads(act)
            A_scalar(act, step)
            F_scalar(act, 0)
            R_scalar(act, step)
            F_scalar(act, 1)
            E_scalar(act, step)
            F_scalar(act, 2)
            G_scalar(act, step)
            M_scalar(act, step)

        @block.vector
        def _(dve):
            step = Steps(dve, dve_step)
            setup_vector(dve, step)
            A_vector(dve, step)
            F_vector(dve, step, 0)
            R_vector(dve, step)
            F_vector(dve, step, 1)
            E_vector(dve, step)
            F_vector(dve, step, 2)
            G_vector(dve, step)
            M_vector(dve, step)

        @block.tensor
        def _(pe):
            setup_tensor(pe)
            A_tensor(pe)
            F_tensor(pe, 0)
            R_tensor(pe)
            F_tensor(pe, 1)
            E_tensor(pe)
            F_tensor(pe, 2)
            G_tensor(pe)
            M_tensor(pe)


def kernel(**inputs):
    import numpy as _np
    import concourse.bacc as _bacc
    from concourse import mybir as _mybir
    from concourse.bass_utils import run_bass_kernel_spmd as _run

    nc = _bacc.Bacc("TRN2", target_bir_lowering=False, num_devices=1)
    arrays, args = {}, {}
    for name in inputs:
        v = _np.ascontiguousarray(inputs[name])
        arrays[f"in_{name}"] = v
        args[name] = nc.dram_tensor(f"in_{name}", v.shape, _mybir.dt.from_np(v.dtype), kind="ExternalInput").ap()
    out = nc.dram_tensor("out", (1, SEQ, D), F32, kind="ExternalOutput").ap()
    build(nc, args, out)
    return _run(nc, [arrays], core_ids=[0]).results[0]["out"]
```

```python
from contextlib import ExitStack

import concourse.bass as bass
from concourse import mybir

P = 128
D = 1024
SEQ = 256
KT = D // P
TT = SEQ // P
HD = 64
KEYS = P + SEQ
N_HEADS_A = 8
N_HEADS_B = 8
CHUNK = 64
REL_CLIP = 256
D_FF = 2816
FT_FF = D_FF // P
GROUPS_FF = FT_FF // 4
CONV_WIDTH = 4
LRU_BLOCKS = 4
LRU_C = 8.0
N_DIL = 12
N_DIFF = 4
DIL_WINDOW = (128, 512, 2048)
DIL_STEP = (1, 4, 16)
LAM_INIT = 0.8 - 0.6
HG = 8
NE = 8
FE = 3584
CE = FE // 512
NLOAD_E = 3 * CE
CAP = P
EPS = 1e-6
MASKED = 1e30

NS = 7
NS_EARLY = 5
SLOT = 4096

F32 = mybir.dt.float32
F32R = mybir.dt.float32r
I32 = mybir.dt.int32
U32 = mybir.dt.uint32
ALU = mybir.AluOpType
ACT = mybir.ActivationFunctionType
AX = mybir.AxisListType


def build(nc, a, out):
    ctx = ExitStack()
    with ctx:
        def sb(name, shape, dt=F32):
            return ctx.enter_context(nc.sbuf_tensor(name, shape, dt))

        def sem(name):
            return ctx.enter_context(nc.semaphore(name))

        aligned = lambda at: (at + 31) // 32 * 32
        ring_at = aligned(nc.sbuf_base)
        ring = sb("ring", [P, NS, SLOT])
        arena_at = aligned(nc.sbuf_base)
        arena = sb("arena", [P, 8, 2048])
        ring_r = [[nc.alloc_sbuf_tensor_at(f"ring_r{s}_{h}", [P, 2048], F32R, offset=ring_at + (2 * s + h) * 8192)
                   for h in range(2)] for s in range(NS)]
        arena_r = [nc.alloc_sbuf_tensor_at(f"arena_r{i}", [P, 2048], F32R, offset=arena_at + i * 8192) for i in range(8)]
        ps = ctx.enter_context(nc.psum_tensor("ps", [P, 8, 512], F32))

        def page(i, n=1):
            if i >= 8:
                flat = ring[:, NS_EARLY:NS, :].rearrange("p s n -> p (s n)")
                return flat[:, (i - 8) * 2048:(i - 8 + n) * 2048]
            return arena[:, i:i + n, :].rearrange("p s n -> p (s n)")

        def page_r(i):
            return arena_r[i][:, :] if i < 8 else ring_r[NS_EARLY + (i - 8) // 2][i % 2][:, :]

        X = page(0).rearrange("p (t d) -> p t d", t=TT)
        HT = page(1).rearrange("p (k t) -> p k t", k=KT)
        XN = page(2).rearrange("p (t d) -> p t d", t=TT)
        junk = sb("junk", [P, D])
        gpost = sb("gpost", [P, D])
        rows = sb("rows", [P, 2, P])
        cols = sb("cols", [P, 160])
        ident = sb("ident", [P, P])
        ones128 = sb("ones128", [P, P])
        ones64 = sb("ones64", [P, P])
        ones32 = sb("ones32", [P, P])
        before = sb("before", [P, P])
        stickmask = sb("stickmask", [P, KEYS])
        disti = sb("disti", [P, KEYS], I32)
        distm = sb("distm", [P, KEYS], I32)
        dist = sb("dist", [P, 4, KEYS])
        causal = sb("causal", [P, 2, CHUNK])
        restart = sb("restart", [P, SEQ])
        scores_T = sb("scores_T", [P, 2, TT, P])
        halves = sb("halves", [P, 4])
        epscol = sb("epscol", [P, 2])
        sumsq = sb("sumsq", [P, 32])
        rstd = sb("rstd", [P, 32])
        neg_max = sb("neg_max", [P, 2, 16])
        sums = sb("sums", [P, 2, 16])
        small = sb("small", [P, 256])
        iota_j = sb("iota_j", [P, 3 * CAP])
        wrouter = sb("wrouter", [P, KT, NE])
        rt = sb("rt", [P, 16, 16])
        rti = sb("rti", [P, 2, 8], U32)
        nblk = sb("nblk", [1, 1], I32)
        lamv = sb("lamv", [P, 4, 32])

        col = {}
        row_loads = []
        at = [0, 0]

        def rows_of(name, tile, src):
            n = src.shape[0]
            row_loads.append((rows[at[tile]:at[tile] + n, tile, :], src))
            col[name] = at[tile] + P * tile
            at[tile] += n

        def row_repeated(name, src, width):
            again = bass.AP(tensor=src.tensor, offset=src.offset, ap=[[width, 1], [0, P // width], [1, width]])
            row_loads.append((rows[at[1]:at[1] + 1, 1, :].rearrange("o (r n) -> o r n", n=width), again))
            col[name] = at[1] + P
            at[1] += 1

        split = lambda ap: ap.rearrange("l (k p) -> (l k) p", p=P)
        rows_of("norm_mix_pre", 0, split(a["norm_mix_pre"]))
        rows_of("norm_ffn_pre", 0, split(a["norm_ffn_pre"]))
        rows_of("attn_norm", 0, split(a["attn_norm_2"]))
        rows_of("ffn_norm", 0, split(a["ffn_norm_2"]))
        rows_of("hgrn_norm", 0, split(a["hgrn_norm_2"]))
        rows_of("moe_norm", 0, split(a["moe_norm_2"]))
        rows_of("conv_w", 0, a["rg_conv_w"].rearrange("a w b (f p) -> (a w b f) p", p=P))
        rows_of("conv_b", 0, split(a["rg_conv_b"]))
        rows_of("b_a", 0, a["rg_b_a"].rearrange("a n (j p) -> (a n j) p", p=P))
        rows_of("b_i", 0, a["rg_b_i"].rearrange("a n (j p) -> (a n j) p", p=P))
        rows_of("lambda", 0, split(a["rg_lambda"]))
        rows_of("lb", 1, split(a["hgrn_lb_logits_2"]))
        rows_of("hgrn_out_gain", 1, a["hgrn_out_gain_2"])
        row_repeated("dil_q_gain", a["dil_q_gain_2"], HD)
        row_repeated("dil_k_gain", a["dil_k_gain_2"], HD)
        row_repeated("diff_q_gain", a["diff_q_gain_2"], HD // 2)
        row_repeated("diff_k_gain", a["diff_k_gain_2"], HD // 2)
        row_repeated("diff_out_gain", a["diff_out_gain_2"], HD)
        NROW1 = at[1]
        lam_names = ("diff_lambda_q1_2", "diff_lambda_k1_2", "diff_lambda_q2_2", "diff_lambda_k2_2")

        def column(name, i=0, n=1):
            return cols[:, col[name] + i:col[name] + i + n]

        landed = [sem(f"landed{s}") for s in range(NS)]
        landed_half = sem("landed_half")
        x_in = sem("x_in")
        rows_in = sem("rows_in")
        small_in = sem("small_in")
        side_in = sem("side_in")
        gpost_in = sem("gpost_in")
        s_out = sem("s_out")
        const_ok = sem("const_ok")
        ident_ok = sem("ident_ok")
        dist_ok = sem("dist_ok")
        rows_t = sem("rows_t")
        params_ok = sem("params_ok")
        exp_par = sem("exp_par")
        pool_step = sem("pool_step")
        dve_step = sem("dve_step")
        act_step = sem("act_step")
        s_ss = sem("s_ss")
        s_rstd = sem("s_rstd")
        s_xn = sem("s_xn")
        s_tr = sem("s_tr")
        s_ht = sem("s_ht")
        s_hth = sem("s_hth")
        s_htl = sem("s_htl")
        s_unit = sem("s_unit")
        s_evac = sem("s_evac")
        s_y = sem("s_y")
        s_yss = sem("s_yss")
        s_yrstd = sem("s_yrstd")
        s_x = sem("s_x")
        s_gu = sem("s_gu")
        s_sg = sem("s_sg")
        s_v = sem("s_v")
        s_hh = sem("s_hh")
        s_h = sem("s_h")
        s_dn = sem("s_dn")
        w_hi = sem("w_hi")
        w_lo = sem("w_lo")

        stream = []
        count = [0] * NS
        freed = [None] * NS
        nxt = [0]

        def next_slot():
            s = nxt[0]
            nxt[0] = (s + 1) % NS_EARLY
            return s

        def load(pairs, used):
            s = next_slot()
            stream.append((s, pairs(s), freed[s]))
            count[s] += 16 * len(pairs(s))
            freed[s] = used
            return s, count[s]

        def slot_k(s):
            return ring[:, s, :].rearrange("p (k n) -> p k n", k=KT)

        def columns_of(w, c0, n=512):
            return lambda s: [(slot_k(s)[:, :, 0:n], w.rearrange("(k p) n -> p k n", p=P)[:, :, c0:c0 + n])]

        units = [0]

        def project(w, parts):
            plan = []
            for c0, kinds in parts:
                units_before = units[0]
                units[0] += len(kinds)
                s, n = load(columns_of(w, c0), (s_unit, units[0]))
                off = 0
                tt = 0
                for j, kind in enumerate(kinds):
                    plan.append((kind, s, n, off, tt, units_before + j))
                    if kind in "FH":
                        off += 256
                    else:
                        tt += 1
            return plan

        y_n = [0]

        def project_out(w):
            y_n[0] += 2
            return [load(columns_of(w, c * 512), (s_y, y_n[0])) for c in range(2)] + [y_n[0] - 2]

        ffn_tiles = [0]
        half_n = [0]

        LOWS_FF = 6 * GROUPS_FF + 3

        def plan_ffn(wg, wu, wd):
            y_n[0] += 2
            i = ffn_tiles[0] // FT_FF
            base, lo = ffn_tiles[0], LOWS_FF * i
            ffn_tiles[0] += FT_FF
            g0, g1, low0, low1, dn = slots = [next_slot() for _ in range(5)]
            gate, up = (w.rearrange("(k p) (f n) -> f p k n", p=P, n=256) for w in (wg, wu))
            down = wd.rearrange("(f r p) n -> f p r n", r=2, p=P)
            f = dict(base=base, lo=lo, y=y_n[0] - 2, g0=g0, g1=g1, dn=dn, low0=low0, low1=low1, gate=gate, up=up, down=down,
                     n={s: count[s] for s in slots}, half=half_n[0], freed={s: freed[s] for s in slots})
            count[g0] += 32 * (GROUPS_FF + 1)
            count[g1] += 32 * GROUPS_FF
            count[dn] += 16 * (GROUPS_FF + 1)
            half_n[0] += 16 * GROUPS_FF
            freed[g0] = (w_lo, lo + LOWS_FF - 2)
            freed[g1] = (w_lo, lo + LOWS_FF - 5)
            freed[low0] = (s_gu, base + FT_FF)
            freed[low1] = (s_gu, base + 4 * GROUPS_FF)
            freed[dn] = (s_y, y_n[0])
            spare, late = (page_r(9), page_r(6)) if i != 1 else (page_r(6), page_r(9))
            f["high"] = dict(g0=(page_r(10), page_r(11)), g1=(page_r(7), page_r(8)), dn=(page_r(5), spare))
            f["HTh"] = late.rearrange("p (k t) -> p k t", k=KT)
            stream.append(f)
            return f

        A_w_in = a["attn_w_in"][0]
        R_w_in = a["rg_w_in"][0]
        E_w_in = a["attn_w_in_2"][0]
        G_w_in = a["hgrn_w_in_2"][0]
        A_plan = project(A_w_in, [(0, "FF"), (512, "FF"), (1024, "TT"), (1536, "FF"), (2048, "FF"), (2560, "TT")])
        A_out = project_out(a["attn_w_out"][0])
        FFN = [plan_ffn(a["ffn_w_gate"][0], a["ffn_w_up"][0], a["ffn_w_down"][0])]
        R_plan = project(R_w_in, [(1024, "FF"), (1536, "FF")])
        r_gates = sem("r_gates")

        def gate_weights(s):
            v = ring[:, s, :].rearrange("p (w k n) -> p w k n", w=2, k=KT)
            return [(v[:, i], a[n][0].rearrange("n (k p) j -> p (n k) j", p=P)) for i, n in enumerate(("rg_w_a", "rg_w_i"))]

        R_gate_w = load(gate_weights, (r_gates, KT))
        R_plan += project(R_w_in, [(0, "FF"), (512, "FF")])
        R_out = project_out(a["rg_w_out"][0])
        FFN.append(plan_ffn(a["ffn_w_gate"][1], a["ffn_w_up"][1], a["ffn_w_down"][1]))
        E_plan = project(E_w_in, [(0, "FF"), (512, "FF"), (1024, "FF"), (1536, "TT"), (2048, "HF"), (2560, "FH")])
        E_out = project_out(a["attn_w_out_2"][0])
        FFN.append(plan_ffn(a["ffn_w_gate_2"][0], a["ffn_w_up_2"][0], a["ffn_w_down_2"][0]))
        G_plan = project(G_w_in, [(1024, "FF"), (1536, "FF"), (0, "FF"), (512, "FF"), (2048, "TT"), (2560, "TT"),
                                  (3072, "FF"), (3584, "FF")])
        G_out = project_out(a["hgrn_w_out_2"][0])

        block = ctx.enter_context(nc.Block())

        class Steps:

            def __init__(self, eng, s):
                self.eng, self.s, self.n = eng, s, 0

            def link(self, ins):
                self.n += 1
                ins.then_inc(self.s, 1)
                self.eng.wait_ge(self.s, self.n)

        gain_of = [("norm_mix_pre", 0), ("norm_ffn_pre", 0), ("norm_mix_pre", 8), ("norm_ffn_pre", 8),
                   ("attn_norm", 0), ("ffn_norm", 0), ("hgrn_norm", 0), ("moe_norm", 0)]

        def norm_steps(k):
            if k == 0:
                return [("norm", 0), ("norm", 1)]
            if k % 2:
                return [("residual", 0), ("norm", 0), ("residual", 1), ("norm", 1)]
            return [("residual", 0), ("residual", 1), ("norm", 0), ("norm", 1)]

        def norm_scalar(act, k):
            for what, t in norm_steps(k):
                if what == "residual":
                    if k <= 4:
                        postnorm_scalar(act, k - 1, t)
                    continue
                if k == 0:
                    act.wait_ge(x_in, 16)
                else:
                    act.wait_ge(s_x, 2 * (k - 1) + t + 1)
                nc.scalar.activation(XN[:, t, :], X[:, t, :], ACT.Square,
                                     accum_out=sumsq[:, 2 * k + t:2 * k + t + 1]).then_inc(s_ss, 1)

        def norm_gpsimd(pool, step, k):
            for what, t in norm_steps(k):
                if what == "residual":
                    if k <= 4:
                        postnorm_gpsimd(pool, step, k - 1, t)
                    continue
                c = slice(2 * k + t, 2 * k + t + 1)
                pool.wait_ge(s_ss, 2 * k + t + 1)
                step.link(nc.gpsimd.tensor_scalar(sumsq[:, c], sumsq[:, c], D * EPS, None, ALU.add))
                nc.gpsimd.tensor_tensor(rstd[:, c], sumsq[:, c], halves[:, 0:1], ALU.pow).then_inc(s_rstd, 1)

        def norm_vector(dve, step, k, f=None, between=None):
            name, i = gain_of[k]

            def turned(t, h):
                dve.wait_ge(s_tr, 4 * k + 2 * t + h + 1)
                g = column(name, i + 4 * h, 4).rearrange("p (k o) -> p k o", o=1).to_broadcast([P, 4, P])
                nc.vector.tensor_tensor(HT[:, 4 * h:4 * h + 4, t * P:(t + 1) * P],
                                        ps[:, 2 * t + h, :].rearrange("p (k t) -> p k t", k=4), g,
                                        ALU.mult).then_inc(s_ht, 1)

            for what, t in norm_steps(k):
                if what == "residual":
                    if k <= 4:
                        postnorm_vector(dve, step, k - 1, t)
                    else:
                        residual_vector(dve, k - 1, t)
                    continue
                if k % 2 and t == 1:
                    turned(0, 0)
                    turned(0, 1)
                dve.wait_ge(s_rstd, 2 * k + t + 1)
                nc.vector.tensor_scalar(XN[:, t, :], X[:, t, :], rstd[:, 2 * k + t:2 * k + t + 1], float(D) ** 0.5,
                                        ALU.mult, ALU.mult).then_inc(s_xn, 1)
            if between:
                between()
            if k % 2 == 0:
                turned(0, 0)
                turned(0, 1)
            if f:
                ffn_norm_vector(dve, f, 0)
                ffn_norm_vector(dve, f, 1)
            turned(1, 0)
            turned(1, 1)
            if f:
                ffn_norm_vector(dve, f, 2)
                ffn_norm_vector(dve, f, 3)

        def norm_tensor(pe, k, f=None, between=None):
            for t in range(TT):
                pe.wait_ge(s_xn, 2 * k + t + 1)
                for h in range(2):
                    for kt in range(4 * h, 4 * h + 4):
                        mm = nc.tensor.transpose(ps[:, 2 * t + h, (kt % 4) * P:(kt % 4 + 1) * P],
                                                 XN[:, t, kt * P:(kt + 1) * P], ident[:, :])
                    mm.then_inc(s_tr, 1)
            if between:
                between()
            if f:
                pe.wait_ge(s_htl, 4 * (f["base"] // FT_FF) + 4)
            else:
                pe.wait_ge(s_ht, 4 * k + 4)

        def unit_tensor(pe, plan, j, nbanks):
            kind, s, n, off, tt, u = plan[j]
            pe.wait_ge(landed[s], n)
            if j >= nbanks:
                pe.wait_ge(s_evac, u - nbanks + 1)
            bank = ps[:, j % nbanks, :]
            w = slot_k(s)
            if kind == "F":
                for f in range(2):
                    for kt in range(KT):
                        mm = nc.tensor.matmul(bank[:, f * SEQ:(f + 1) * SEQ], w[:, kt, off + f * P:off + (f + 1) * P],
                                              HT[:, kt, :], start=(kt == 0), stop=(kt == KT - 1))
            elif kind == "T":
                for kt in range(KT):
                    mm = nc.tensor.matmul(bank, HT[:, kt, tt * P:(tt + 1) * P], w[:, kt, :],
                                          start=(kt == 0), stop=(kt == KT - 1))
            else:
                for t in range(TT):
                    for kt in range(KT):
                        mm = nc.tensor.matmul(bank[:, t * 256:(t + 1) * 256], HT[:, kt, t * P:(t + 1) * P],
                                              w[:, kt, off:off + 256], start=(kt == 0), stop=(kt == KT - 1))
            mm.then_inc(s_unit, 1)

        def unit_scalar(act, plan, j, nbanks, dst, func=ACT.Copy, scale=1.0):
            u = plan[j][5]
            act.wait_ge(s_unit, u + 1)
            nc.scalar.activation(dst, ps[:, j % nbanks, :], func, scale=scale).then_inc(s_evac, 1)

        Y = ps[:, 4:8, :].rearrange("p (t h) n -> p t (h n)", t=TT)

        def out_tensor(pe, plan, actT):
            for c in range(2):
                pe.wait_ge(landed[plan[c][0]], plan[c][1])
            for t in range(TT):
                for c in range(2):
                    for kt in range(KT):
                        mm = nc.tensor.matmul(Y[:, t, c * 512:(c + 1) * 512], actT[:, kt, t * P:(t + 1) * P],
                                              slot_k(plan[c][0])[:, kt, :], start=(kt == 0), stop=(kt == KT - 1))
                mm.then_inc(s_y, 1)

        def postnorm_scalar(act, m, t):
            act.wait_ge(s_y, 2 * m + t + 1)
            nc.scalar.activation(XN[:, 1, :] if t else junk[:, :], Y[:, t, :], ACT.Square,
                                 accum_out=sumsq[:, 16 + 2 * m + t:17 + 2 * m + t]).then_inc(s_yss, 1)

        def postnorm_gpsimd(pool, step, m, t):
            c = slice(16 + 2 * m + t, 17 + 2 * m + t)
            pool.wait_ge(s_yss, 2 * m + t + 1)
            step.link(nc.gpsimd.tensor_scalar(sumsq[:, c], sumsq[:, c], D * EPS, None, ALU.add))
            nc.gpsimd.tensor_tensor(rstd[:, c], sumsq[:, c], halves[:, 0:1], ALU.pow).then_inc(s_yrstd, 1)

        def postnorm_vector(dve, step, m, t):
            dve.wait_ge(gpost_in, 16 * (m + 1))
            dve.wait_ge(s_yrstd, 2 * m + t + 1)
            step.link(nc.vector.scalar_tensor_tensor(XN[:, t, :], Y[:, t, :],
                                                     rstd[:, 16 + 2 * m + t:17 + 2 * m + t], gpost[:, :],
                                                     ALU.mult, ALU.mult))
            nc.vector.scalar_tensor_tensor(X[:, t, :], XN[:, t, :], float(D) ** 0.5, X[:, t, :],
                                           ALU.mult, ALU.add).then_inc(s_x, 1)

        def residual_vector(dve, m, t):
            dve.wait_ge(s_y, 2 * m + t + 1)
            nc.vector.tensor_tensor(X[:, t, :], X[:, t, :], Y[:, t, :], ALU.add).then_inc(s_x, 1)

        hidden = page_r(3).rearrange("p (v f t) -> p v f t", v=2, f=4)
        silu = page(4)[:, 0:1024].rearrange("p (f t) -> p f t", f=4)
        whole = page(4)[:, 1024:2048].rearrange("p (f t) -> p f t", f=4)
        HTl = page_r(1).rearrange("p (k t) -> p k t", k=KT)

        def ffn_norm_scalar(act, f, k):
            for q in range(4):
                c = (slice(None), slice(q % 2 * 4, q % 2 * 4 + 4), slice(q // 2 * P, (q // 2 + 1) * P))
                act.wait_ge(s_ht, 4 * k + q + 1)
                nc.scalar.activation(f["HTh"][c], HT[c], ACT.Copy).then_inc(s_hth, 1)

        def ffn_norm_vector(dve, f, q):
            c = (slice(None), slice(q % 2 * 4, q % 2 * 4 + 4), slice(q // 2 * P, (q // 2 + 1) * P))
            dve.wait_ge(s_hth, 4 * (f["base"] // FT_FF) + q + 1)
            nc.vector.tensor_tensor(HTl[c], HT[c], f["HTh"][c], ALU.subtract).then_inc(s_htl, 1)

        def ffn_halves(f, name):
            w = ring[:, f[name], :].rearrange("p (v n) -> p v n", v=2)
            low = [v[:, :] for v in ring_r[f[{"g0": "low0", "g1": "low1", "dn": "dn"}[name]]]]
            return w, f["high"][name], low

        def ffn_high(act, f, name, h, landed_at, s=None):
            act.wait_ge(landed[f[name]] if s is None else s, landed_at)
            w, high, low = ffn_halves(f, name)
            nc.scalar.activation(high[h], w[:, h, :], ACT.Copy).then_inc(w_hi, 1)

        def ffn_low(dve, f, name, h, n):
            dve.wait_ge(w_hi, n)
            w, high, low = ffn_halves(f, name)
            nc.vector.tensor_tensor(low[h], w[:, h, :], high[h],
                                    ALU.subtract).then_inc(w_lo, 1)

        def first_split_scalar(act, f):
            for h in range(2):
                ffn_high(act, f, "g0", h, f["n"][f["g0"]] + 32)

        def first_split_vector(dve, f):
            dve.wait_ge(*f["freed"][f["low0"]])
            for h in range(2):
                ffn_low(dve, f, "g0", h, f["lo"] + h + 1)

        def gate_up(pe, f, f4, freed_h):
            if freed_h is not None:
                pe.wait_ge(s_h, freed_h)
            w, high, low = ffn_halves(f, "g0" if f4 < 2 else "g1")
            c = slice(f4 % 2 * P, f4 % 2 * P + P)
            for i in range(2):
                wh = high[i].rearrange("p (k n) -> p k n", k=KT)
                wl = low[i].rearrange("p (k n) -> p k n", k=KT)
                out_ = ps[:, f4, i * SEQ:(i + 1) * SEQ]
                for kt in range(KT):
                    nc.tensor.matmul(out_, wh[:, kt, c], f["HTh"][:, kt, :], start=(kt == 0), stop=False)
                    nc.tensor.matmul(out_, wh[:, kt, c], HTl[:, kt, :], start=False, stop=False)
                    mm = nc.tensor.matmul(out_, wl[:, kt, c], f["HTh"][:, kt, :], start=False, stop=(kt == KT - 1))
            mm.then_inc(s_gu, 1)

        def down(pe, f, f4, ready_h, first=False, last=False, tail=False):
            pe.wait_ge(s_h, ready_h)
            w, high, low = ffn_halves(f, "dn")
            wh = high[f4 // 2].rearrange("p (r n) -> p r n", n=D)
            wl = low[f4 // 2].rearrange("p (r n) -> p r n", n=D)
            for t in range(TT):
                x = [hidden[:, v, f4, t * P:(t + 1) * P] for v in range(2)]
                for c in range(2):
                    out_, n = Y[:, t, c * 512:(c + 1) * 512], slice(c * 512, (c + 1) * 512)
                    nc.tensor.matmul(out_, x[0], wh[:, f4 % 2, n], start=first, stop=False)
                    nc.tensor.matmul(out_, x[0], wl[:, f4 % 2, n], start=False, stop=False)
                    mm = nc.tensor.matmul(out_, x[1], wh[:, f4 % 2, n], start=False, stop=last)
                if last:
                    mm.then_inc(s_y, 1)
            if not last:
                mm.then_inc(s_dn, 1)

        def ffn_tensor(pe, f):
            b, lo = f["base"], f["lo"]
            pe.wait_ge(w_lo, lo + 2)
            gate_up(pe, f, 0, None)
            gate_up(pe, f, 1, None)
            pe.wait_ge(w_lo, lo + 4)
            gate_up(pe, f, 2, None)
            pe.wait_ge(w_lo, lo + 5)
            down(pe, f, 0, b + 1, first=True)
            gate_up(pe, f, 3, None)
            down(pe, f, 1, b + 2)
            with pe.Fori(1, GROUPS_FF) as i:
                pe.wait_ge(w_lo, 6 * i + (lo + 1))
                gate_up(pe, f, 0, 4 * i + (b - 3))
                pe.wait_ge(w_lo, 6 * i + (lo + 2))
                down(pe, f, 2, 4 * i + (b - 1))
                gate_up(pe, f, 1, 4 * i + (b - 2))
                down(pe, f, 3, 4 * i + b)
                pe.wait_ge(w_lo, 6 * i + (lo + 4))
                gate_up(pe, f, 2, 4 * i + (b - 1))
                pe.wait_ge(w_lo, 6 * i + (lo + 5))
                down(pe, f, 0, 4 * i + (b + 1))
                gate_up(pe, f, 3, 4 * i + b)
                down(pe, f, 1, 4 * i + (b + 2))
            t0 = 4 * GROUPS_FF
            pe.wait_ge(w_lo, lo + LOWS_FF - 2)
            gate_up(pe, f, 0, b + t0 - 3)
            pe.wait_ge(w_lo, lo + LOWS_FF - 1)
            down(pe, f, 2, b + t0 - 1)
            gate_up(pe, f, 1, b + t0 - 2)
            down(pe, f, 3, b + t0)
            pe.wait_ge(w_lo, lo + LOWS_FF)
            down(pe, f, 0, b + t0 + 1)
            down(pe, f, 1, b + t0 + 2, last=True)

        def ffn_scalar(act, f):
            b, n = f["base"], f["n"]
            k = (FT_FF - 1) * (b // FT_FF)

            def act_tile(f4, gu):
                act.wait_ge(s_gu, gu)
                nc.scalar.activation(silu[:, f4, :], ps[:, f4, 0:SEQ], ACT.Silu).then_inc(s_sg, 1)

            def high_tile(f4, v, dn_used):
                act.wait_ge(s_v, v)
                if dn_used is not None:
                    act.wait_ge(s_dn, dn_used)
                nc.scalar.activation(hidden[:, 0, f4, :], whole[:, f4, :], ACT.Copy).then_inc(s_hh, 1)

            def group(i, first=False):
                for h in range(2):
                    ffn_high(act, f, "g1", h, 32 * i + (n[f["g1"]] + 32))
                for f4 in range(4):
                    used = None if first else 4 * i + (k + f4 - 3)
                    act_tile(f4, 4 * i + (b + f4 + 1))
                    if f4 == 0:
                        ffn_high(act, f, "dn", 0, 16 * i + (n[f["dn"]] + 16))
                    elif f4 == 1:
                        ffn_high(act, f, "g0", 0, 32 * i + (n[f["g0"]] + 64))
                    elif f4 == 2:
                        ffn_high(act, f, "dn", 1, 16 * i + (f["half"] + 16), landed_half)
                    high_tile(f4, 4 * i + (b + f4 + 1), used)
                    if f4 == 1:
                        ffn_high(act, f, "g0", 1, 32 * i + (n[f["g0"]] + 64))

            group(0, first=True)
            with act.Fori(1, GROUPS_FF) as i:
                group(i)
            t0 = 4 * GROUPS_FF
            act_tile(0, b + t0 + 1)
            ffn_high(act, f, "dn", 0, n[f["dn"]] + 16 * (GROUPS_FF + 1))
            high_tile(0, b + t0 + 1, k + t0 - 3)
            act_tile(1, b + t0 + 2)
            high_tile(1, b + t0 + 2, k + t0 - 2)

        def ffn_vector(dve, f):
            b, lo = f["base"], f["lo"]

            def tile(f4, at):
                dve.wait_ge(s_sg, at)
                nc.vector.tensor_tensor(whole[:, f4, :], silu[:, f4, :], ps[:, f4, SEQ:2 * SEQ], ALU.mult).then_inc(s_v, 1)

            def low_tile(f4, at):
                dve.wait_ge(s_hh, at)
                nc.vector.tensor_tensor(hidden[:, 1, f4, :], whole[:, f4, :], hidden[:, 0, f4, :],
                                        ALU.subtract).then_inc(s_h, 1)

            def group(i):
                for h in range(2):
                    ffn_low(dve, f, "g1", h, 6 * i + (lo + 3 + h))
                for f4 in range(4):
                    at = 4 * i + (b + f4 + 1)
                    tile(f4, at)
                    if f4 == 0:
                        ffn_low(dve, f, "dn", 0, 6 * i + (lo + 5))
                    elif f4 == 1:
                        ffn_low(dve, f, "g0", 0, 6 * i + (lo + 6))
                    elif f4 == 2:
                        ffn_low(dve, f, "dn", 1, 6 * i + (lo + 8))
                    low_tile(f4, at)
                    if f4 == 1:
                        ffn_low(dve, f, "g0", 1, 6 * i + (lo + 7))

            if f["freed"][f["low1"]]:
                dve.wait_ge(*f["freed"][f["low1"]])
            group(0)
            with dve.Fori(1, GROUPS_FF) as i:
                group(i)
            t0 = 4 * GROUPS_FF
            tile(0, b + t0 + 1)
            ffn_low(dve, f, "dn", 0, lo + LOWS_FF)
            low_tile(0, b + t0 + 1)
            tile(1, b + t0 + 2)
            low_tile(1, b + t0 + 2)

        def ffn_sync(sp, f):
            b, lo, fr = f["base"], f["lo"], f["freed"]
            k = (FT_FF - 1) * (b // FT_FF)
            slot_pair = lambda name: ring[:, f[name], :].rearrange("p (w k n) -> p w k n", w=2, k=KT)
            dn = ring[:, f["dn"], :].rearrange("p (r n) -> p r n", n=D)
            g0, g1 = slot_pair("g0"), slot_pair("g1")

            def pair(name, v, j):
                at = (lambda w: w[j]) if isinstance(j, int) else (lambda w: w[bass.ds(j, 1)].rearrange("o p k n -> p (o k) n"))
                sp.dma_start(v[:, 0], at(f["gate"])).then_inc(landed[f[name]], 16)
                sp.dma_start(v[:, 1], at(f["up"])).then_inc(landed[f[name]], 16)

            def half(j, r):
                src = f["down"][j] if isinstance(j, int) else f["down"][bass.ds(j, 1)].rearrange("o p k n -> p (o k) n")
                sp.dma_start(dn[:, 2 * r:2 * r + 2, :], src).then_inc(landed_half if r else landed[f["dn"]], 16)

            for name, v, j in (("g0", g0, 0), ("g1", g1, 1)):
                if fr[f[name]]:
                    sp.wait_ge(*fr[f[name]])
                pair(name, v, j)
            sp.wait_ge(*fr[f["dn"]])
            half(0, 0)
            half(1, 1)
            sp.wait_ge(w_lo, lo + 2)
            pair("g0", g0, 2)
            with sp.Fori(1, GROUPS_FF) as i:
                sp.wait_ge(w_lo, 6 * i + (lo - 2))
                pair("g1", g1, 2 * i + 1)
                sp.wait_ge(s_dn, 4 * i + (k - 2))
                half(2 * i, 0)
                sp.wait_ge(w_lo, 6 * i + (lo + 2))
                pair("g0", g0, 2 * i + 2)
                sp.wait_ge(s_dn, 4 * i + k)
                half(2 * i + 1, 1)
            sp.wait_ge(s_dn, 4 * GROUPS_FF + (k - 2))
            half(2 * GROUPS_FF, 0)

        def setup_gpsimd_first(pool, step):
            step.link(nc.gpsimd.memset(halves[:, :], -0.5))
            nc.gpsimd.memset(epscol[:, :], EPS)
            step.link(nc.gpsimd.memset(ident[:, :], 0.0))
            nc.gpsimd.affine_select(out=ident[:, :], in_=ident[:, :], compare_op=ALU.not_equal, fill=1.0,
                                    base=0, pattern=[[-1, P]], channel_multiplier=1).then_inc(ident_ok, 1)

        def setup_gpsimd(pool, step):
            nc.gpsimd.iota(disti[:, 0:P], [[-1, P]], base=0, channel_multiplier=1)
            nc.gpsimd.iota(disti[:, P:], [[-1, SEQ]], base=P, channel_multiplier=1)
            nc.gpsimd.iota(distm[:, :], [[1, 3 * CAP]], base=0, channel_multiplier=0)
            nc.gpsimd.memset(ones128[:, :], 1.0)
            nc.gpsimd.memset(stickmask[:, :], 0.0)
            nc.gpsimd.memset(causal[:, :, :], 1.0)
            nc.gpsimd.memset(restart[:, :], 1.0)
            step.link(nc.gpsimd.memset(scores_T[:, :, :, :], 0.0))
            nc.gpsimd.tensor_copy(iota_j[:, :], distm[:, :]).then_inc(const_ok, 1)
            pool.wait_ge(const_ok, 1)
            for q in range(2):
                step.link(nc.gpsimd.affine_select(out=causal[64 * q:64 * q + 64], in_=causal[64 * q:64 * q + 64],
                                                  compare_op=ALU.is_ge, fill=0.0, base=0, pattern=[[0, 2], [1, CHUNK]],
                                                  channel_multiplier=-1))
            nc.gpsimd.memset(restart[:, :].rearrange("p (c t) -> p c t", t=CHUNK)[:, :, 0:1], 0.0)
            nc.gpsimd.affine_select(out=before[:, :], in_=ones128[:, :], compare_op=ALU.is_gt, fill=0.0, base=0,
                                    pattern=[[1, P]], channel_multiplier=-1)
            step.link(keys_select(stickmask, ALU.is_gt, 0, 1, -MASKED))
            pool.wait_ge(dist_ok, 1)
            for g in range(4):
                step.link(keys_select(dist[:, g, :], ALU.is_ge, 0, 1, MASKED))
            keys_select(dist[:, 0, :], ALU.is_ge, DIL_WINDOW[0], -1, MASKED).then_inc(const_ok, 1)

        def keys_select(m, op, base, sign, fill):
            nc.gpsimd.affine_select(out=m[:, 0:P], in_=m[:, 0:P], compare_op=op, fill=fill, base=base,
                                    pattern=[[-sign, P]], channel_multiplier=sign)
            return nc.gpsimd.affine_select(out=m[:, P:KEYS], in_=m[:, P:KEYS], compare_op=op, fill=fill,
                                           base=base + sign * P, pattern=[[-sign, SEQ]], channel_multiplier=sign)

        EARLY_ROWS = 6

        def setup_loads(act, pairs):
            for dst, src in pairs:
                act.dma_start(dst, src).then_inc(rows_in, 16)

        z24, e24, sp24 = small[:, 0:24], small[:, 24:48], small[:, 48:72]
        decay_scale, decay_neg = small[:, 72:80], small[:, 80:88]
        ln_lb, ln_1lb, ln_dif = small[:, 88:96], small[:, 96:104], small[:, 104:112]
        gains = small[:, 112:116]
        lam2, elam, neg_lam = small[:, 116:118], small[:, 118:120], small[:, 120:121]
        lam_prod = small[:, 128:192].rearrange("p (a d) -> p a d", a=2)

        def setup_tensor(pe):
            pe.wait_ge(rows_in, 16 * len(row_loads))
            nc.tensor.transpose(ps[:, 7, 0:P], rows[:, 0, :], ident[:, :])
            nc.tensor.transpose(ps[:, 7, P:P + NROW1], rows[0:NROW1, 1, :], ident[0:NROW1, 0:NROW1]).then_inc(rows_t, 1)

        def setup_vector(dve, step):
            nc.vector.memset(ones64[:, :], 0.0)
            step.link(nc.vector.memset(ones32[:, :], 0.0))
            for q in range(4):
                nc.vector.memset(ones32[32 * q:32 * q + 32, 32 * q:32 * q + 32], 1.0)
            for q in range(2):
                nc.vector.memset(ones64[64 * q:64 * q + 64, 64 * q:64 * q + 64], 1.0)

        def columns_vector(dve, step):
            dve.wait_ge(rows_t, 1)
            step.link(nc.vector.tensor_copy(cols[:, 0:P + NROW1], ps[:, 7, 0:P + NROW1]))

        def distances_vector(dve, step):
            dve.wait_ge(const_ok, 1)
            nc.vector.tensor_copy(dist[:, 0, :], disti[:, :])
            nc.vector.tensor_copy(dist[:, 3, :], disti[:, :])
            step.link(nc.vector.tensor_scalar(distm[:, :], disti[:, :], DIL_STEP[1] - 1, None, ALU.bitwise_and))
            step.link(nc.vector.scalar_tensor_tensor(dist[:, 1, :], distm[:, :], MASKED, disti[:, :], ALU.mult, ALU.add))
            step.link(nc.vector.tensor_scalar(distm[:, :], disti[:, :], DIL_STEP[2] - 1, None, ALU.bitwise_and))
            nc.vector.scalar_tensor_tensor(dist[:, 2, :], distm[:, :], MASKED, disti[:, :], ALU.mult, ALU.add)\
                .then_inc(dist_ok, 1)

        def params_vector(dve, step):
            nc.vector.tensor_scalar(z24[:, 0:8], column("lambda", 0, 8), -1.0, None, ALU.mult)
            nc.vector.tensor_tensor(z24[:, 8:16], column("lb", 0, 8), column("lb", 8, 8), ALU.subtract)
            nc.vector.tensor_tensor(z24[:, 16:24], column("lb", 8, 8), column("lb", 0, 8), ALU.subtract)
            nc.vector.tensor_scalar(gains[:, 0:1], column("dil_q_gain"), HD ** -0.5, None, ALU.mult)
            nc.vector.tensor_scalar(gains[:, 1:2], column("diff_q_gain"), (HD // 2) ** -0.5, None, ALU.mult)
            nc.vector.tensor_scalar(gains[:, 2:3], column("diff_out_gain"), 1.0 - LAM_INIT, None, ALU.mult)
            dve.wait_ge(small_in, 16 * 5)
            nc.vector.tensor_tensor(lam_prod[:, 0], lamv[:, 0], lamv[:, 1], ALU.mult)
            step.link(nc.vector.tensor_tensor(lam_prod[:, 1], lamv[:, 2], lamv[:, 3], ALU.mult))
            nc.vector.tensor_reduce(lam2, lam_prod, AX.X, ALU.add)
            nc.vector.scalar_tensor_tensor(e24, z24, -1.0, z24, ALU.mult, ALU.min).then_inc(params_ok, 1)
            dve.wait_ge(exp_par, 3)
            step.link(nc.vector.scalar_tensor_tensor(sp24, z24, 0.0, e24, ALU.max, ALU.add))
            nc.vector.tensor_scalar(decay_scale, sp24[:, 0:8], -LRU_C, None, ALU.mult)
            nc.vector.tensor_scalar(decay_neg, sp24[:, 0:8], LRU_C, None, ALU.mult)
            nc.vector.tensor_scalar(ln_lb, sp24[:, 8:16], -1.0, None, ALU.mult)
            nc.vector.tensor_scalar(ln_1lb, sp24[:, 16:24], -1.0, None, ALU.mult)
            nc.vector.tensor_tensor(ln_dif, sp24[:, 8:16], sp24[:, 16:24], ALU.subtract)
            step.link(nc.vector.tensor_tensor(neg_lam, elam[:, 1:2], elam[:, 0:1], ALU.subtract))
            nc.vector.tensor_scalar(neg_lam, neg_lam, -LAM_INIT, None, ALU.add).then_inc(params_ok, 1)

        def setup_scalar(act):
            act.wait_ge(params_ok, 1)
            nc.scalar.activation(e24, e24, ACT.Exp).then_inc(exp_par, 1)
            nc.scalar.activation(elam, lam2, ACT.Exp).then_inc(exp_par, 1)
            act.wait_ge(exp_par, 2)
            nc.scalar.activation(e24, e24, ACT.Ln, bias=1.0).then_inc(exp_par, 1)

        QK = page(3, 2).rearrange("p (f t) -> p f t", t=SEQ)
        V = page(5).rearrange("p (t d) -> p t d", t=TT)
        OT = page(6).rearrange("p (f t) -> p f t", t=SEQ)
        four = lambda pg: pg[:, 0:4 * KEYS].rearrange("p (h k) -> p h k", h=4)
        A_sc = [four(page(2)), four(page(7))]
        A_w = [four(page(10)), four(page(11))]
        A_na = four(page(8))
        A_bias = page(8, 2)[:, 0:8 * KEYS].rearrange("p (h k) -> p h k", h=8)
        A_pt = page(8, 2)[:, 8 * KEYS:10 * KEYS].rearrange("p (h k) -> p h k", h=2)
        a_s, a_sc, a_mx, a_e, a_pn = (sem("a_" + n) for n in ("s", "sc", "mx", "e", "pn"))
        a_na, a_ln, a_d, a_w = (sem("a_" + n) for n in ("na", "ln", "d", "w"))
        a_t, a_pt, a_pv, a_ot = (sem("a_" + n) for n in ("t", "pt", "pv", "ot"))

        def A_tensor(pe):
            pe.wait_ge(ident_ok, 1)
            norm_tensor(pe, 0, between=lambda: setup_tensor(pe))

            def gemm(*js):
                for j in js:
                    unit_tensor(pe, A_plan, j, 2)

            def scores(b):
                pe.wait_ge(s_evac, 4 if b < 2 else 10)
                for g in range(4 * b, 4 * b + 4):
                    if g >= 2:
                        pe.wait_ge(a_sc, g - 1)
                    fq = g // 2 if g < 8 else 8 + (g - 8) // 2
                    r = slice(HD * (g % 2), HD * (g % 2) + HD)
                    nc.tensor.matmul(ps[:, 4 + g % 2, 0:P], QK[r, fq, 0:P], QK[r, fq + 4, 0:P], start=True, stop=True)
                    nc.tensor.matmul(ps[:, 4 + g % 2, P:KEYS], QK[r, fq, P:SEQ], QK[r, fq + 4, :], start=True,
                                     stop=True).then_inc(a_s, 1)

            def turn(g):
                if g >= 2:
                    pe.wait_ge(a_pt, g - 1)
                for c in range(3):
                    mm = nc.tensor.transpose(ps[:, 6 + g % 2, c * P:(c + 1) * P],
                                             A_w[g // 4 % 2][:, g % 4, c * P:(c + 1) * P], ident[:, :])
                mm.then_inc(a_t, 1)

            def values(g):
                pe.wait_ge(a_pt, g + 1)
                if g >= 4 and g % 2 == 0:
                    pe.wait_ge(a_ot, g // 2 - 1)
                o = ps[HD * (g % 2):HD * (g % 2) + HD, 2 + g // 2 % 2, :]
                nc.tensor.matmul(o[:, 0:SEQ], V[:, 0, g * HD:(g + 1) * HD], A_pt[:, g % 2, 0:SEQ], start=True, stop=False)
                nc.tensor.matmul(o[:, P:SEQ], V[:, 1, g * HD:(g + 1) * HD], A_pt[:, g % 2, SEQ:KEYS], start=False,
                                 stop=True).then_inc(a_pv, 1)

            def attend(b):
                if b < 2:
                    pe.wait_ge(a_pn, b + 1)
                else:
                    pe.wait_ge(a_w, b - 1)
                turn(4 * b)
                for g in range(4 * b, 4 * b + 4):
                    if g % 4 < 3:
                        turn(g + 1)
                    values(g)

            gemm(0, 1, 2, 3, 4, 5)
            scores(0)
            gemm(6, 7)
            scores(1)
            gemm(8, 9)
            attend(0)
            scores(2)
            gemm(10, 11)
            scores(3)
            attend(1)
            attend(2)
            attend(3)
            pe.wait_ge(a_ot, 8)
            out_tensor(pe, A_out, OT)

        def A_scalar(act, step):
            norm_scalar(act, 0)
            setup_loads(act, row_loads[EARLY_ROWS:])
            for i, name in enumerate(lam_names):
                act.dma_start(lamv[:, i, :], a[name][0].partition_broadcast(P)).then_inc(small_in, 16)
            act.dma_start(wrouter[:, :, :], a["moe_w_router_2"][0].rearrange("(k p) e -> p k e", p=P)).then_inc(small_in, 16)
            setup_scalar(act)

            def evac(j):
                c = A_plan[j]
                if c[0] == "T":
                    unit_scalar(act, A_plan, j, 2, V[:, c[4], (0 if j < 6 else 512):(512 if j < 6 else D)])
                else:
                    f = 2 * (j if j < 4 else j - 2)
                    unit_scalar(act, A_plan, j, 2, QK[:, f:f + 2, :], scale=HD ** -0.5 if f // 4 in (0, 2) else 1.0)

            def exps(b):
                act.wait_ge(a_mx, b + 1)
                for i in range(4):
                    for t, c in enumerate((slice(0, P), slice(P, KEYS))):
                        ins = nc.scalar.activation(A_w[b % 2][:, i, c], A_sc[b % 2][:, i, c], ACT.Exp,
                                                   bias=neg_max[:, t, 4 * b + i:4 * b + i + 1],
                                                   accum_out=sums[:, t, 4 * b + i:4 * b + i + 1])
                ins.then_inc(a_e, 1)

            def softplus(b):
                act.wait_ge(a_na, b - 1)
                step.link(nc.scalar.activation(A_na, A_na, ACT.Exp))
                nc.scalar.activation(A_na, A_na, ACT.Ln, bias=1.0).then_inc(a_ln, 1)

            def weights(b):
                act.wait_ge(a_d, b - 1)
                nc.scalar.activation(A_w[b % 2], A_sc[b % 2], ACT.Exp).then_inc(a_w, 1)

            def copies(b):
                for g in range(4 * b, 4 * b + 5):
                    if g < 4 * b + 4:
                        act.wait_ge(a_t, g + 1)
                        if g >= 2:
                            act.wait_ge(a_pv, g - 1)
                        nc.scalar.activation(A_pt[:, g % 2, :], ps[:, 6 + g % 2, 0:KEYS], ACT.Copy).then_inc(a_pt, 1)
                    if g % 2 == 0 and g > 4 * b:
                        act.wait_ge(a_pv, g)
                        nc.scalar.activation(OT[:, g // 2 - 1, :], ps[:, 2 + (g // 2 - 1) % 2, 0:SEQ],
                                             ACT.Copy).then_inc(a_ot, 1)

            for j in range(6):
                evac(j)
            exps(0)
            evac(6), evac(7)
            exps(1)
            evac(8), evac(9)
            copies(0)
            softplus(2)
            evac(10), evac(11)
            weights(2)
            softplus(3)
            copies(1)
            copies(2)
            weights(3)
            copies(3)
            first_split_scalar(act, FFN[0])

        def A_vector(dve, step):
            norm_vector(dve, step, 0, between=lambda: columns_vector(dve, step))
            distances_vector(dve, step)
            params_vector(dve, step)
            dve.wait_ge(side_in, 16)
            step.link(nc.vector.memset(A_bias[0:CHUNK, :, P:P + CHUNK], -MASKED))

            def biased(b):
                sc = A_sc[b]
                for i in range(4):
                    g = 4 * b + i
                    dve.wait_ge(a_s, g + 1)
                    nc.vector.tensor_tensor(sc[:, i, 0:P], ps[:, 4 + g % 2, 0:P], A_bias[:, g, P:SEQ][:, ::-1], ALU.add)
                    nc.vector.tensor_tensor(sc[:, i, P:KEYS], ps[:, 4 + g % 2, P:KEYS], A_bias[:, g, P:KEYS][:, ::-1],
                                            ALU.add).then_inc(a_sc, 1)
                dve.wait_ge(a_sc, 4 * b + 4)
                nc.vector.tensor_reduce(neg_max[:, 0, 4 * b:4 * b + 4], sc[:, :, 0:P], AX.X, ALU.max, negate=True)
                nc.vector.tensor_reduce(neg_max[:, 1, 4 * b:4 * b + 4], sc[:, :, P:KEYS], AX.X, ALU.max,
                                        negate=True).then_inc(a_mx, 1)

            def normalised(b):
                dve.wait_ge(a_e, b + 1)
                r = sums[:, :, 4 * b:4 * b + 4]
                step.link(nc.vector.reciprocal(r, r))
                for i in range(4):
                    for t, c in enumerate((slice(0, P), slice(P, KEYS))):
                        w = A_w[b][:, i, c]
                        ins = nc.vector.tensor_scalar(w, w, sums[:, t, 4 * b + i:4 * b + i + 1], None, ALU.mult)
                ins.then_inc(a_pn, 1)

            def stick_scores(b):
                sc = A_sc[b % 2]
                for i in range(4):
                    g = 4 * b + i
                    dve.wait_ge(a_s, g + 1)
                    nc.vector.tensor_tensor(sc[:, i, :], ps[:, 4 + g % 2, 0:KEYS], stickmask[:, :],
                                            ALU.add).then_inc(a_sc, 1)
                dve.wait_ge(a_sc, 4 * b + 4)
                nc.vector.scalar_tensor_tensor(A_na, sc, -1.0, sc, ALU.mult, ALU.min).then_inc(a_na, 1)

            def stick_sums(b):
                sc, w = A_sc[b % 2], A_w[b % 2]
                dve.wait_ge(a_ln, b - 1)
                dve.wait_ge(a_t, 4 * (b - 1))
                step.link(nc.vector.scalar_tensor_tensor(w, sc, 0.0, A_na, ALU.max, ALU.add))
                for i in range(4):
                    for c in (slice(0, P), slice(P, KEYS)):
                        v = w[:, i, c][:, ::-1]
                        ins = nc.vector.tensor_tensor_scan(A_na[:, i, c][:, ::-1], v, v, 0.0, ALU.add, ALU.bypass)
                step.link(ins)
                nc.vector.tensor_tensor(sc, sc, A_na, ALU.subtract).then_inc(a_d, 1)

            biased(0)
            normalised(0)
            biased(1)
            normalised(1)
            stick_scores(2)
            stick_sums(2)
            stick_scores(3)
            stick_sums(3)
            first_split_vector(dve, FFN[0])

        norm_at_ffn = (1, 3, 5)

        def F_tensor(pe, i):
            norm_tensor(pe, norm_at_ffn[i], FFN[i])
            ffn_tensor(pe, FFN[i])

        def F_scalar(act, i):
            norm_scalar(act, norm_at_ffn[i])
            ffn_norm_scalar(act, FFN[i], norm_at_ffn[i])
            ffn_scalar(act, FFN[i])

        def F_vector(dve, step, i):
            norm_vector(dve, step, norm_at_ffn[i], FFN[i])
            ffn_vector(dve, FFN[i])

        TAPS = CONV_WIDTH - 1
        R_x = page(3, 2)[:, 0:KT * (TAPS + SEQ)].rearrange("p (f t) -> p f t", f=KT)
        tiles = lambda i: page(i).rearrange("p (f t) -> p f t", f=KT)
        R_xc, R_r, R_i, R_gate, R_tau, R_a, R_u, R_y = (tiles(i) for i in (5, 6, 7, 8, 9, 10, 11, 9))
        R_h = page(3).rearrange("p (f t) -> p f t", f=KT)
        r_pad, r_xc, r_sig, r_tau, r_inv, r_exp, r_v, r_mult, r_out = (
            sem("r_" + n) for n in ("pad", "xc", "sig", "tau", "inv", "exp", "v", "mult", "out"))

        def R_tensor(pe):
            norm_tensor(pe, 2)
            for j in range(5):
                unit_tensor(pe, R_plan, j, 2)
            s, n = R_gate_w
            pe.wait_ge(landed[s], n)
            w = ring[:, s, :].rearrange("p (w k n) -> p w k n", w=2, k=KT)
            for j in range(KT):
                pe.wait_ge(r_xc, j // 2 + 1)
                if j >= 2:
                    pe.wait_ge(r_sig, j - 1)
                for i in range(2):
                    for kt in range(2):
                        f = j // 2 * 2 + kt
                        mm = nc.tensor.matmul(ps[:, 2 + j % 2, i * SEQ:(i + 1) * SEQ],
                                              w[:, i, f, j % 2 * P:(j % 2 + 1) * P], R_xc[:, f, :],
                                              start=(kt == 0), stop=(kt == 1))
                mm.then_inc(r_gates, 1)
            for j in range(5, 8):
                unit_tensor(pe, R_plan, j, 2)
            pe.wait_ge(r_out, 4)
            out_tensor(pe, R_out, R_y)

        def R_scalar(act, step):
            norm_scalar(act, 2)
            act.wait_ge(r_pad, 1)
            for j in range(4):
                unit_scalar(act, R_plan, j, 2, R_x[:, 2 * j:2 * j + 2, TAPS:])
            gate = lambda j: unit_scalar(act, R_plan, j, 2, R_gate[:, 2 * (j - 4):2 * (j - 4) + 2, :], ACT.Gelu_apprx_tanh)
            gate(4)
            for j in range(KT):
                act.wait_ge(r_gates, j + 1)
                bank = ps[:, 2 + j % 2, :]
                nc.scalar.activation(R_r[:, j, :], bank[:, 0:SEQ], ACT.Sigmoid, bias=column("b_a", j))
                nc.scalar.activation(R_i[:, j, :], bank[:, SEQ:], ACT.Sigmoid, bias=column("b_i", j)).then_inc(r_sig, 1)
            act.wait_ge(r_sig, KT)
            for j in range(KT):
                ins = nc.scalar.activation(R_tau[:, j, :], R_r[:, j, :], ACT.Tanh, scale=decay_neg[:, j:j + 1])
            ins.then_inc(r_tau, 1)
            act.wait_ge(r_tau, 1)
            step.link(nc.scalar.activation(R_u, R_tau, ACT.Ln, bias=1.0))
            nc.scalar.activation(R_u, R_u, ACT.Exp, scale=-1.0).then_inc(r_inv, 1)
            for j in range(KT):
                ins = nc.scalar.activation(R_a[:, j, :], R_r[:, j, :], ACT.Exp, scale=decay_scale[:, j:j + 1])
            ins.then_inc(r_exp, 1)
            gate(5)
            act.wait_ge(r_v, 1)
            nc.scalar.activation(R_u, R_u, ACT.Sqrt, scale=2.0).then_inc(r_mult, 1)
            gate(6)
            gate(7)
            act.wait_ge(r_out, 4)
            first_split_scalar(act, FFN[1])

        def R_vector(dve, step):
            norm_vector(dve, step, 2)
            nc.vector.memset(R_x[:, :, 0:TAPS], 0.0).then_inc(r_pad, 1)
            for u in range(4):
                dve.wait_ge(s_evac, R_plan[u][5] + 1)
                for k in range(CONV_WIDTH):
                    for f in (2 * u, 2 * u + 1):
                        w = column("conv_w", k * KT + f)
                        v = R_x[:, f, k:k + SEQ]
                        if k == 0:
                            ins = nc.vector.tensor_scalar(R_xc[:, f, :], v, w, column("conv_b", f), ALU.mult, ALU.add)
                        else:
                            ins = nc.vector.scalar_tensor_tensor(R_xc[:, f, :], v, w, R_xc[:, f, :], ALU.mult, ALU.add)
                    if k < CONV_WIDTH - 1:
                        step.link(ins)
                ins.then_inc(r_xc, 1)
            dve.wait_ge(r_xc, 4)
            dve.wait_ge(r_sig, KT)
            step.link(nc.vector.tensor_tensor(R_i, R_i, R_xc, ALU.mult))
            dve.wait_ge(r_inv, 1)
            nc.vector.tensor_tensor(R_u, R_u, R_tau, ALU.mult).then_inc(r_v, 1)
            dve.wait_ge(r_mult, 1)
            step.link(nc.vector.tensor_tensor(R_u, R_u, R_i, ALU.mult))
            dve.wait_ge(r_exp, 1)
            for f in range(KT):
                ins = nc.vector.tensor_tensor_scan(R_h[:, f, :], R_a[:, f, :], R_u[:, f, :], 0.0, ALU.mult, ALU.add)
            step.link(ins)
            for u in range(4):
                dve.wait_ge(s_evac, R_plan[4 + u][5] + 1)
                nc.vector.tensor_tensor(R_y[:, 2 * u:2 * u + 2, :], R_h[:, 2 * u:2 * u + 2, :],
                                        R_gate[:, 2 * u:2 * u + 2, :], ALU.mult).then_inc(r_out, 1)
            first_split_vector(dve, FFN[1])

        E_sc = [page(i)[:, 0:3 * KEYS].rearrange("p (n k) -> p n k", n=3) for i in (7, 8, 2)]
        E_pt = page(9)[:, 0:2 * KEYS].rearrange("p (n k) -> p n k", n=2)
        E_sq = page(10).rearrange("p (n k) -> p n k", k=512)
        E_rs = page(11).rearrange("p (n k) -> p n k", k=512)
        e_sq, e_nn, e_rt, e_qn, e_s, e_sc, e_mx, e_e, e_pn, e_t, e_pt, e_pv, e_ot = (
            sem("e_" + n) for n in ("sq", "nn", "rt", "qn", "s", "sc", "mx", "e", "pn", "t", "pt", "pv", "ot"))
        E_F = [j for j, u in enumerate(E_plan) if u[0] == "F"]
        NG = 8
        maps_of = lambda g: 3 if g < 4 else 2
        heads_of = lambda g: [g, 4 + g, 8 + g] if g < 4 else [8 + g]
        maps_before = lambda g: sum(maps_of(x) for x in range(g))
        heads_before = lambda g: sum(len(heads_of(x)) for x in range(g))
        E_gain = [gains[:, 0:1]] * 3 + [column("dil_k_gain")] * 3 + [gains[:, 1:2], column("diff_k_gain"), gains[:, 2:3]]
        slope_of = lambda head: 2.0 ** (-8.0 * (head + 1) / (N_DIL + N_DIFF))
        tile_cols = (slice(0, P), slice(P, KEYS))

        def E_rows(i):
            return QK[:, 2 * i:2 * i + 2, :] if i < 8 else OT[:, 6:8, :]

        def E_tensor(pe):
            norm_tensor(pe, 4)

            def sum_squares(i):
                pe.wait_ge(e_sq, i + 1)
                if i >= 2:
                    pe.wait_ge(e_rt, i - 1)
                nc.tensor.matmul(ps[:, 2 + i % 2, :], (ones32 if i in (6, 7) else ones64)[:, :], E_sq[:, i % 2, :],
                                 start=True, stop=True).then_inc(e_nn, 1)

            pe.wait_ge(const_ok, 2)
            for j in range(12):
                unit_tensor(pe, E_plan, j, 2)
                if j - 1 in E_F:
                    sum_squares(E_F.index(j - 1))

            def scores(g):
                for n in range(maps_of(g)):
                    c = maps_before(g) + n
                    if g < 4:
                        head = g + 4 * n
                        fq, fk, r0, width = head // 2, 6 + head // 2, head % 2 * HD, HD
                    else:
                        i = g - 4
                        fq, fk, r0, width = 12 + i // 2, 14 + i // 2, i % 2 * HD + n * HD // 2, HD // 2
                    if c >= 2:
                        pe.wait_ge(e_sc, c - 1)
                    r = slice(r0, r0 + width)
                    nc.tensor.matmul(ps[:, 4 + c % 2, 0:P], QK[r, fq, 0:P], QK[r, fk, 0:P], start=True, stop=True,
                                     tile_position=(r0, 0))
                    nc.tensor.matmul(ps[:, 4 + c % 2, P:KEYS], QK[r, fq, P:SEQ], QK[r, fk, :], start=True, stop=True,
                                     tile_position=(r0, 0)).then_inc(e_s, 1)

            def turn(g, n, c):
                if c >= 2:
                    pe.wait_ge(e_pt, c - 1)
                for b in range(3):
                    mm = nc.tensor.transpose(ps[:, 6 + c % 2, b * P:(b + 1) * P], E_sc[g % 3][:, n, b * P:(b + 1) * P],
                                             ident[:, :])
                mm.then_inc(e_t, 1)

            def values(head, c):
                pe.wait_ge(e_pt, c + 1)
                if c >= 2:
                    pe.wait_ge(e_ot, c - 1)
                o = ps[HD * (head % 2):HD * (head % 2) + HD, 2 + c % 2, :]
                nc.tensor.matmul(o[:, 0:SEQ], V[:, 0, head * HD:(head + 1) * HD], E_pt[:, c % 2, 0:SEQ],
                                 start=True, stop=False)
                nc.tensor.matmul(o[:, P:SEQ], V[:, 1, head * HD:(head + 1) * HD], E_pt[:, c % 2, SEQ:KEYS],
                                 start=False, stop=True).then_inc(e_pv, 1)

            def attend(g):
                pe.wait_ge(e_pn, g + 1)
                hs, c0 = heads_of(g), heads_before(g)
                turn(g, 0, c0)
                for n, head in enumerate(hs):
                    if n + 1 < len(hs):
                        turn(g, n + 1, c0 + n + 1)
                    values(head, c0 + n)

            pe.wait_ge(e_qn, 8)
            scores(0)
            scores(1)
            for g in range(NG):
                if g + 2 < NG:
                    scores(g + 2)
                attend(g)
            sum_squares(8)
            pe.wait_ge(e_qn, 9)
            out_tensor(pe, E_out, OT)

        def E_scalar(act, step):
            norm_scalar(act, 4)

            def squares(i):
                if i >= 2:
                    act.wait_ge(e_nn, i - 1)
                nc.scalar.activation(E_sq[:, i % 2, :], E_rows(i).rearrange("p f t -> p (f t)"), ACT.Square).then_inc(e_sq, 1)

            def root(i):
                act.wait_ge(e_nn, i + 1)
                if i >= 2:
                    act.wait_ge(e_qn, i - 1)
                nc.scalar.activation(E_rs[:, i % 2, :], ps[:, 2 + i % 2, :], ACT.Sqrt, bias=epscol[:, 0:1],
                                     scale=1.0 / (HD // 2 if i in (6, 7) else HD)).then_inc(e_rt, 1)

            for j in range(12):
                kind, tt = E_plan[j][0], E_plan[j][4]
                if kind == "F":
                    i = E_F.index(j)
                    unit_scalar(act, E_plan, j, 2, QK[:, 2 * i:2 * i + 2, :])
                    act.wait_ge(s_evac, E_plan[j][5] + 1)
                    squares(i)
                elif kind == "T":
                    unit_scalar(act, E_plan, j, 2, V[:, tt, 0:512])
                else:
                    c0 = 512 if j == 8 else 768
                    unit_scalar(act, E_plan, j, 2, V[:, :, c0:c0 + 256])
                if j - 1 in E_F:
                    root(E_F.index(j - 1))

            def exps(g):
                act.wait_ge(e_mx, g + 1)
                sc = E_sc[g % 3]
                for t, c in enumerate(tile_cols):
                    for m in range(1 if g < 4 else 2):
                        v = sc[:, 0:3, c] if g < 4 else sc[:, m, c]
                        k = 2 * g + m
                        ins = nc.scalar.activation(v, v, ACT.Exp, bias=neg_max[:, t, k:k + 1], accum_out=sums[:, t, k:k + 1])
                ins.then_inc(e_e, 1)

            def copies(g):
                c0, hs = heads_before(g), heads_of(g)
                for c in range(c0, c0 + len(hs) + 1):
                    if c < c0 + len(hs):
                        act.wait_ge(e_t, c + 1)
                        if c >= 2:
                            act.wait_ge(e_pv, c - 1)
                        nc.scalar.activation(E_pt[:, c % 2, :], ps[:, 6 + c % 2, 0:KEYS], ACT.Copy).then_inc(e_pt, 1)
                    if c > c0:
                        head = hs[c - 1 - c0]
                        r = slice(HD * (head % 2), HD * (head % 2) + HD)
                        act.wait_ge(e_pv, c)
                        nc.scalar.activation(OT[r, head // 2, :], ps[r, 2 + (c - 1) % 2, 0:SEQ], ACT.Copy).then_inc(e_ot, 1)

            exps(0)
            for g in range(NG):
                if g + 1 < NG:
                    exps(g + 1)
                copies(g)
            act.wait_ge(e_ot, 16)
            squares(8)
            root(8)
            act.wait_ge(e_qn, 9)
            first_split_scalar(act, FFN[2])

        def E_vector(dve, step):
            norm_vector(dve, step, 4)

            def normalise(i):
                dve.wait_ge(e_rt, i + 1)
                step.link(nc.vector.reciprocal(E_rs[:, i % 2, :], E_rs[:, i % 2, :]))
                v = E_rows(i).rearrange("p f t -> p (f t)")
                nc.vector.scalar_tensor_tensor(v, v, E_gain[i], E_rs[:, i % 2, :], ALU.mult, ALU.mult).then_inc(e_qn, 1)

            for i in range(8):
                normalise(i)
            dve.wait_ge(const_ok, 2)

            def biased(g):
                sc = E_sc[g % 3]
                if g >= 3:
                    dve.wait_ge(e_t, heads_before(g - 2))
                for n in range(maps_of(g)):
                    c = maps_before(g) + n
                    head, d = (g + 4 * n, n) if g < 4 else (8 + g, 3)
                    dve.wait_ge(e_s, c + 1)
                    nc.vector.scalar_tensor_tensor(sc[:, n, :], dist[:, d, :], -slope_of(head), ps[:, 4 + c % 2, 0:KEYS],
                                                   ALU.mult, ALU.add).then_inc(e_sc, 1)
                dve.wait_ge(e_sc, maps_before(g + 1))
                for t, c in enumerate(tile_cols):
                    if g < 4:
                        ins = nc.vector.tensor_reduce(neg_max[:, t, 2 * g:2 * g + 1], sc[:, :, c], AX.XY, ALU.max, negate=True)
                    else:
                        ins = nc.vector.tensor_reduce(neg_max[:, t, 2 * g:2 * g + 2], sc[:, 0:2, c], AX.X, ALU.max, negate=True)
                ins.then_inc(e_mx, 1)

            def normalised(g):
                sc = E_sc[g % 3]
                dve.wait_ge(e_e, g + 1)
                k = 2 * g
                if g < 4:
                    step.link(nc.vector.reciprocal(sums[:, :, k:k + 1], sums[:, :, k:k + 1]))
                    for t, c in enumerate(tile_cols):
                        ins = nc.vector.tensor_scalar(sc[:, :, c], sc[:, :, c], sums[:, t, k:k + 1], None, ALU.mult)
                else:
                    step.link(nc.vector.reciprocal(sums[:, :, k:k + 2], sums[:, :, k:k + 2]))
                    step.link(nc.vector.tensor_scalar(sums[:, :, k + 1:k + 2], sums[:, :, k + 1:k + 2], neg_lam, None, ALU.mult))
                    for t, c in enumerate(tile_cols):
                        ins = nc.vector.tensor_scalar(sc[:, 0, c], sc[:, 0, c], sums[:, t, k:k + 1], None, ALU.mult)
                    step.link(ins)
                    for t, c in enumerate(tile_cols):
                        ins = nc.vector.scalar_tensor_tensor(sc[:, 0, c], sc[:, 1, c], sums[:, t, k + 1:k + 2], sc[:, 0, c],
                                                             ALU.mult, ALU.add)
                ins.then_inc(e_pn, 1)

            biased(0)
            biased(1)
            for g in range(NG):
                normalised(g)
                if g + 2 < NG:
                    biased(g + 2)
            normalise(8)
            first_split_vector(dve, FFN[2])

        G_q, G_k, G_b, G_g, G_o = (tiles(i) for i in (3, 4, 5, 7, 8))
        G_v = page(6).rearrange("p (t d) -> p t d", t=TT)
        G_ls, G_mx, G_ad = (page(i).rearrange("p (u n) -> p u n", u=4) for i in (9, 10, 11))
        G_sq = page(5).rearrange("p (u n) -> p u n", u=4)
        G_pr = page(9, 2).rearrange("p (r n t) -> p r n t", r=4, n=4)
        G_e = page(11).rearrange("p (r n t) -> p r n t", r=2, n=4)
        G_tmp = page(2)
        G_st = G_tmp[:, 0:2 * 3 * P].rearrange("p (r c v) -> p r c v", r=2, c=3)
        G_ks = G_tmp[:, 768:768 + 2 * SEQ].rearrange("p (r t k) -> p r t k", r=2, t=TT)
        G_dec = G_tmp[:, 1280:1280 + HG * 4].rearrange("p (h c) -> p h c", h=HG)
        g_na, g_ln, g_kk, g_k, g_b, g_d, g_ex, g_pr, g_t, g_ks, g_s, g_at, g_kv, g_st, g_o, g_oc, g_sq, g_nn, g_rt, g_y = (
            sem("g_" + n) for n in ("na", "ln", "kk", "k", "b", "d", "ex", "pr", "t", "ks", "s", "at", "kv", "st", "o",
                                    "oc", "sq", "nn", "rt", "y"))
        G_evac = lambda j: G_plan[j][5] + 1

        def G_tensor(pe):
            norm_tensor(pe, 6)
            for j in range(13):
                unit_tensor(pe, G_plan, j, 4)

            def scores(h):
                pe.wait_ge(g_pr, h + 1)
                if h >= 1:
                    pe.wait_ge(g_ks, h)
                for t in range(TT):
                    mm = nc.tensor.transpose(ps[:, 5, t * P:(t + 1) * P], G_pr[:, h % 4, 3, t * P:(t + 1) * P], ident[:, :])
                mm.then_inc(g_t, 1)
                if h >= 1:
                    pe.wait_ge(g_at, h)
                for t in range(TT):
                    for q in range(4):
                        c0 = t * P + q // 2 * CHUNK
                        first = q % 2 * 32
                        mm = nc.tensor.matmul(ps[32 * q:32 * q + 32, 4, t * CHUNK + first:(t + 1) * CHUNK],
                                              G_pr[:, h % 4, 1, c0 + first:c0 + first + 32],
                                              G_pr[:, h % 4, 0, c0 + first:c0 + CHUNK], start=True, stop=True)
                mm.then_inc(g_s, 1)

            def states(h):
                pe.wait_ge(g_ks, h + 1)
                if h >= 1:
                    pe.wait_ge(g_st, h)
                else:
                    pe.wait_ge(s_evac, G_evac(12))
                for c in range(3):
                    r = slice(c % 2 * CHUNK, c % 2 * CHUNK + CHUNK)
                    mm = nc.tensor.matmul(ps[:, c % 2 * -6 + 6, c * P:(c + 1) * P], G_ks[r, h % 2, c // 2, :],
                                          G_v[r, c // 2, h * P:(h + 1) * P], start=True, stop=True)
                mm.then_inc(g_kv, 1)

            def outputs(h):
                pe.wait_ge(g_at, h + 1)
                if h >= 1:
                    pe.wait_ge(g_oc, h)
                for t in range(TT):
                    nc.tensor.matmul(ps[:, 7, t * P:(t + 1) * P], G_v[:, t, h * P:(h + 1) * P], scores_T[:, h % 2, t, :],
                                     start=(t == 0), stop=False, skip_group_check=True)
                pe.wait_ge(g_st, h + 1)
                for c in range(1, 4):
                    mm = nc.tensor.matmul(ps[:, 7, c * CHUNK:(c + 1) * CHUNK], G_st[:, h % 2, c - 1, :],
                                          G_pr[:, h % 4, 2, c * CHUNK:(c + 1) * CHUNK], start=False, stop=(c == 3),
                                          skip_group_check=True)
                mm.then_inc(g_o, 1)

            def sum_squares(u):
                pe.wait_ge(g_sq, u + 1)
                nc.tensor.matmul(ps[:, (u + 1) % 4, :], ones128[:, :], G_sq[:, u, :], start=True, stop=True).then_inc(g_nn, 1)

            pe.wait_ge(s_evac, G_evac(11))
            scores(0)
            for h in range(HG):
                if h < 3:
                    unit_tensor(pe, G_plan, 13 + h, 4)
                states(h)
                if h + 1 < HG:
                    scores(h + 1)
                outputs(h)
                if h >= 2 and h % 2 == 0:
                    sum_squares(h // 2 - 1)
            sum_squares(3)
            pe.wait_ge(g_y, 4)
            out_tensor(pe, G_out, G_o)

        def G_scalar(act, step):
            norm_scalar(act, 6)
            for u in range(4):
                unit_scalar(act, G_plan, u, 4, G_b[:, 2 * u:2 * u + 2, :])
                act.wait_ge(g_na, u + 1)
                step.link(nc.scalar.activation(G_ls[:, u, :], G_ls[:, u, :], ACT.Exp))
                nc.scalar.activation(G_ls[:, u, :], G_ls[:, u, :], ACT.Ln, bias=1.0).then_inc(g_ln, 1)
                act.wait_ge(g_kk, u + 1)
                step.link(nc.scalar.activation(G_ad[:, u, :], G_ad[:, u, :], ACT.Exp))
                nc.scalar.activation(G_ad[:, u, :], G_ad[:, u, :], ACT.Ln, bias=1.0)
                for f in (2 * u, 2 * u + 1):
                    ins = nc.scalar.activation(G_k[:, f, :], G_ls[:, u, (f % 2) * SEQ:(f % 2 + 1) * SEQ], ACT.Exp,
                                               bias=ln_1lb[:, f:f + 1])
                ins.then_inc(g_k, 1)
            for u in range(4):
                unit_scalar(act, G_plan, 4 + u, 4, G_q[:, 2 * u:2 * u + 2, :], ACT.Silu)

            def exps(h):
                act.wait_ge(g_d, h + 1)
                if h >= 2:
                    act.wait_ge(g_pr, h - 1)
                e = G_e[:, h % 2]
                nc.scalar.activation(e[:, 1], e[:, 0], ACT.Exp, scale=-1.0)
                nc.scalar.activation(e[:, 3], G_b[:, h, :], ACT.Exp)
                step.link(nc.scalar.activation(e[:, 2], e[:, 2], ACT.Exp))
                nc.scalar.activation(e[:, 0], e[:, 0], ACT.Exp).then_inc(g_ex, 1)

            def keys(h):
                act.wait_ge(g_t, h + 1)
                if h >= 2:
                    act.wait_ge(g_kv, h - 1)
                nc.scalar.activation(G_ks[:, h % 2], ps[:, 5, 0:SEQ].rearrange("p (t k) -> p t k", t=TT), ACT.Copy)\
                    .then_inc(g_ks, 1)

            def output(h):
                act.wait_ge(g_o, h + 1)
                nc.scalar.activation(G_o[:, h, :], ps[:, 7, 0:SEQ], ACT.Copy).then_inc(g_oc, 1)

            for i in range(4):
                unit_scalar(act, G_plan, 8 + i, 4, G_v[:, i % 2, i // 2 * 512:(i // 2 + 1) * 512])
                exps(i)
            gate = lambda u: unit_scalar(act, G_plan, 12 + u, 4, G_g[:, 2 * u:2 * u + 2, :], ACT.Sigmoid)
            gate(0)
            keys(0)
            for h in range(HG):
                if h < 3:
                    gate(h + 1)
                if h + 4 < HG:
                    exps(h + 4)
                if h + 1 < HG:
                    keys(h + 1)
                output(h)
                if h % 2:
                    u = h // 2
                    act.wait_ge(g_oc, 2 * u + 2)
                    nc.scalar.activation(G_sq[:, u, :], G_o[:, 2 * u:2 * u + 2, :].rearrange("p f t -> p (f t)"), ACT.Square)\
                        .then_inc(g_sq, 1)
            for u in range(4):
                act.wait_ge(g_nn, u + 1)
                ins = nc.scalar.activation(G_ad[:, u, :], ps[:, (u + 1) % 4, :], ACT.Ln, bias=epscol[:, 0:1], scale=1.0 / P)
            step.link(ins)
            for u in range(4):
                nc.scalar.activation(G_ad[:, u, :], G_ad[:, u, :], ACT.Exp, scale=-0.5).then_inc(g_rt, 1)

        def G_vector(dve, step):
            norm_vector(dve, step, 6)
            for u in range(4):
                f2 = G_b[:, 2 * u:2 * u + 2, :].rearrange("p f t -> p (f t)")
                ls, mx, ad = G_ls[:, u, :], G_mx[:, u, :], G_ad[:, u, :]
                dve.wait_ge(s_evac, G_evac(u))
                nc.vector.scalar_tensor_tensor(ls, f2, -1.0, f2, ALU.mult, ALU.min).then_inc(g_na, 1)
                dve.wait_ge(g_ln, u + 1)
                step.link(nc.vector.scalar_tensor_tensor(ls, f2, 0.0, ls, ALU.min, ALU.subtract))
                for f in (2 * u, 2 * u + 1):
                    c = slice(f % 2 * SEQ, (f % 2 + 1) * SEQ)
                    nc.vector.tensor_scalar(mx[:, c], ls[:, c], ln_1lb[:, f:f + 1], ln_lb[:, f:f + 1], ALU.add, ALU.max)
                    ins = nc.vector.tensor_scalar(ad[:, c], ls[:, c], ln_dif[:, f:f + 1], None, ALU.add)
                step.link(ins)
                step.link(nc.vector.scalar_tensor_tensor(ad, ad, -1.0, ad, ALU.mult, ALU.min))
                nc.vector.tensor_tensor(ls, ls, f2, ALU.subtract).then_inc(g_kk, 1)
                dve.wait_ge(g_k, u + 1)
                step.link(nc.vector.tensor_tensor(mx, mx, ad, ALU.add))
                for f in (2 * u, 2 * u + 1):
                    ins = nc.vector.tensor_tensor_scan(G_b[:, f, :], restart[:, :], mx[:, f % 2 * SEQ:(f % 2 + 1) * SEQ], 0.0,
                                                       ALU.mult, ALU.add)
                ins.then_inc(g_b, 1)

            chunks = lambda v: v.rearrange("p (c t) -> p c t", t=CHUNK)

            def exponents(h):
                dve.wait_ge(g_b, h // 2 + 1)
                if h >= 2:
                    dve.wait_ge(g_pr, h - 1)
                b, e = chunks(G_b[:, h, :]), G_e[:, h % 2]
                if h < 2:
                    dve.wait_ge(g_b, 4)
                nc.vector.tensor_tensor(chunks(e[:, 0]), b, b[:, :, CHUNK // 2:CHUNK // 2 + 1].to_broadcast([P, 4, CHUNK]),
                                        ALU.subtract)
                nc.vector.tensor_tensor(chunks(e[:, 2]), b[:, :, CHUNK - 1:CHUNK].to_broadcast([P, 4, CHUNK]), b,
                                        ALU.subtract).then_inc(g_d, 1)

            def products(h):
                dve.wait_ge(g_ex, h + 1)
                dve.wait_ge(s_evac, G_evac(4 + h // 2))
                if h >= 4:
                    dve.wait_ge(g_o, h - 3)
                e, pr = G_e[:, h % 2], G_pr[:, h % 4]
                nc.vector.tensor_copy(G_dec[:, h, :], chunks(e[:, 3])[:, :, CHUNK - 1])
                for n, (x, y) in enumerate(((G_q, 0), (G_k, 1), (G_q, 3), (G_k, 2))):
                    ins = nc.vector.tensor_tensor(pr[:, n], x[:, h, :], e[:, y], ALU.mult)
                ins.then_inc(g_pr, 1)

            def seen(h):
                dve.wait_ge(g_s, h + 1)
                if h >= 2:
                    dve.wait_ge(g_o, h - 1)
                for q in range(4):
                    r, first = slice(32 * q, 32 * q + 32), q % 2 * 32
                    c0 = q // 2 * CHUNK
                    ins = nc.vector.copy_predicated(scores_T[r, h % 2, :, c0 + first:c0 + CHUNK],
                                                    causal[r, :, first:CHUNK].bitcast(I32),
                                                    ps[r, 4, 0:P].rearrange("p (t c) -> p t c", t=TT)[:, :, first:CHUNK])
                ins.then_inc(g_at, 1)

            def states(h):
                dve.wait_ge(g_kv, h + 1)
                st = G_st[:, h % 2]
                step.link(nc.vector.tensor_copy(st[:, 0], ps[:, 6, 0:P]))
                step.link(nc.vector.scalar_tensor_tensor(st[:, 1], st[:, 0], G_dec[:, h, 1:2], ps[:, 0, P:2 * P],
                                                         ALU.mult, ALU.add))
                nc.vector.scalar_tensor_tensor(st[:, 2], st[:, 1], G_dec[:, h, 2:3], ps[:, 6, 2 * P:3 * P],
                                               ALU.mult, ALU.add).then_inc(g_st, 1)

            exponents(0)
            for h in range(4):
                if h < 3:
                    exponents(h + 1)
                products(h)
            for h in range(HG):
                if h + 4 < HG:
                    exponents(h + 4)
                seen(h)
                states(h)
                if h + 4 < HG:
                    products(h + 4)
            for u in range(4):
                o = G_o[:, 2 * u:2 * u + 2, :].rearrange("p f t -> p (f t)")
                dve.wait_ge(g_rt, u + 1)
                step.link(nc.vector.scalar_tensor_tensor(o, o, column("hgrn_out_gain"), G_ad[:, u, :], ALU.mult, ALU.mult))
                dve.wait_ge(s_evac, G_evac(12 + u))
                nc.vector.tensor_tensor(o, o, G_g[:, 2 * u:2 * u + 2, :].rearrange("p f t -> p (f t)"), ALU.mult)\
                    .then_inc(g_y, 1)

        LOGIT, OH0, OH1, MASK, GATE, POS, TMP, CUM = (rt[:, n, :].rearrange("p (t e) -> p t e", t=TT) for n in range(8))
        M_top = rt[:, 8, 0:4].rearrange("p (n t o) -> p n t o", n=2, t=TT)
        M_w = rt[:, 9, 0:4].rearrange("p (n t o) -> p n t o", n=2, t=TT)
        M_cnt = rt[:, 10, :]
        XTE = page_r(1).rearrange("p (v k j) -> p v k j", v=2, k=KT)
        M_sg = page(3)[:, 0:1024].rearrange("p (r n) -> p r n", r=2)
        M_h = page(3)[:, 1024:2048].rearrange("p (r n) -> p r n", r=2)
        M_hT = page_r(4).rearrange("p (r v f j) -> p r v f j", r=2, v=2, f=4)
        M_y = page(5)[:, 0:D]
        M_v = page(5)[:, D:2 * D].rearrange("p (k j) -> p k j", k=KT)
        M_sel = page(6)[:, 0:TT * CAP].rearrange("p (t j) -> p t j", t=TT)
        M_selg = page(6)[:, 256:256 + TT * CAP].rearrange("p (t j) -> p t j", t=TT)
        M_selT = page(6)[:, 512:512 + SEQ]
        m_lg, m_top, m_ex, m_mask, m_pos, m_route = (sem("m_" + n) for n in ("lg", "top", "ex", "mask", "pos", "route"))
        m_g, m_half, m_tt, m_hh, m_ht, m_dn, m_sel, m_ga, m_v, m_xh, m_xt, m_tr, m_st, m_sct, m_sc, m_yc, m_hi, m_lo = (
            sem("m_" + n) for n in ("g", "half", "tt", "hh", "ht", "dn", "sel", "ga", "v", "xh", "xt", "tr", "st", "sct",
                                    "sc", "yc", "hi", "lo"))
        B_M = 3 * FT_FF
        M_n0 = list(count)

        M_loads = [(0, 0), (1, 0)]
        for c_ in range(1, CE):
            M_loads += [(0, c_), (1, c_), (2, c_ - 1)]
        M_loads.append((2, CE - 1))
        NU = 2 * len(M_loads)
        M_per_slot = NU // NS
        M_order = [(nxt[0] + j) % NS_EARLY for j in range(NS_EARLY)] + list(range(NS_EARLY, NS))
        slot_of = lambda k: M_order[k % NS]
        unit_of = {(kind, c, h): 2 * q + h for q, (kind, c) in enumerate(M_loads) for h in range(2)}

        def unit_parts(k):
            return ring_r[slot_of(k)][1][:, :], ring_r[slot_of(k)][0][:, :]

        def split_high(act, i, k):
            act.wait_ge(landed[slot_of(k)], 16 * M_per_slot * i + (M_n0[slot_of(k)] + 16 * (k // NS + 1)))
            nc.scalar.activation(unit_parts(k)[0], ring[:, slot_of(k), 0:2048], ACT.Copy).then_inc(m_hi, 1)

        def split_low(dve, i, k):
            dve.wait_ge(m_hi, NU * i + (k + 1))
            high, low = unit_parts(k)
            nc.vector.tensor_tensor(low, ring[:, slot_of(k), 0:2048], high, ALU.subtract).then_inc(m_lo, 1)

        def product(pe, out_, x, f, w, first, last):
            nc.tensor.matmul(out_, x[:, 0, f, :], w[0], start=first, stop=False)
            nc.tensor.matmul(out_, x[:, 1, f, :], w[0], start=False, stop=False)
            return nc.tensor.matmul(out_, x[:, 0, f, :], w[1], start=False, stop=last)

        def gather(pe, half):
            for kt in range(4):
                for t in range(TT):
                    f = (4 * half + kt) * P
                    mm = nc.tensor.matmul(ps[:, 7, kt * CAP:(kt + 1) * CAP], XN[:, t, f:f + P], M_sel[:, t, :],
                                          start=(t == 0), stop=(t == TT - 1))
            mm.then_inc(m_ga, 1)

        def scatter(r, bank):
            return nc.tensor.matmul(ps[:, bank, :], M_selT[:, r // 2 * P:(r // 2 + 1) * P],
                                    M_y[:, r % 2 * 512:(r % 2 + 1) * 512], start=True, stop=True)

        def M_tensor(pe):
            norm_tensor(pe, 7)
            pe.wait_ge(small_in, 16 * 5)
            for t in range(TT):
                for kt in range(KT):
                    mm = nc.tensor.matmul(ps[:, 4, t * NE:(t + 1) * NE], HT[:, kt, t * P:(t + 1) * P], wrouter[:, kt, :],
                                          start=(kt == 0), stop=(kt == KT - 1))
                mm.then_inc(m_lg if t else m_dn, 1)
            pe.wait_ge(m_mask, 1)
            nc.tensor.matmul(ps[:, 5, 0:NE], before[:, :], MASK[:, 0, :], start=True, stop=True)
            nc.tensor.matmul(ps[:, 5, NE:2 * NE], ones128[:, :], MASK[:, 0, :], start=True, stop=False)
            nc.tensor.matmul(ps[:, 5, NE:2 * NE], before[:, :], MASK[:, 1, :], start=False, stop=True)
            for t in range(TT):
                mm = nc.tensor.matmul(ps[:, 5, 2 * NE:3 * NE], ones128[:, :], MASK[:, t, :], start=(t == 0), stop=(t == TT - 1))
            mm.then_inc(m_pos, 1)
            pe.wait_ge(m_route, 1)
            n = pe.value_load(nblk[0:1, 0:1], min_val=1, max_val=2)
            pe.wait_ge(m_sel, 1)
            gather(pe, 0)
            pe.wait_ge(m_v, 1)
            gather(pe, 1)

            def turn(i, c):
                pe.wait_ge(s_h, 7 * i + (B_M + c + 1))
                pe.wait_ge(m_ht, 7 * i + (c + 1))
                for f in range(4):
                    mm = nc.tensor.transpose(ps[:, 4, f * CAP:(f + 1) * CAP], M_h[:, c % 2, f * P:(f + 1) * P], ident[:, :])
                mm.then_inc(m_tt, 1)

            def down_chunk(i, c):
                pe.wait_ge(m_ht, 7 * i + (c + 2))
                if c == 0:
                    pe.wait_ge(m_yc, i + 1)
                for half in range(2):
                    k = unit_of[2, c, half]
                    pe.wait_ge(m_lo, NU * i + (k + 1))
                    w = [v.rearrange("p (r n) -> p r n", n=D) for v in unit_parts(k)]
                    for r in range(2):
                        for h in range(2):
                            mm = product(pe, ps[:, 5 + h, :], M_hT[:, c % 2], 2 * half + r,
                                         [v[:, r, h * 512:(h + 1) * 512] for v in w],
                                         c == 0 and half == 0 and r == 0, c == CE - 1 and half == 1 and r == 1)
                    mm.then_inc(m_dn if half else m_half, 1)

            with pe.Fori(0, n * NE) as i:
                pe.wait_ge(m_xt, i + 1)
                for c in range(CE):
                    for u, (bank, read, done) in enumerate(((c % 2, s_sg, m_g), (2 + c % 2, s_h, s_gu))):
                        pe.wait_ge(read, 7 * i + (B_M + c - (c > 0)) if c != 1 else 7 * i + (B_M - 1))
                        for half in range(2):
                            k = unit_of[u, c, half]
                            pe.wait_ge(m_lo, NU * i + (k + 1))
                            w = [v.rearrange("p (k n) -> p k n", n=512) for v in unit_parts(k)]
                            for kt in range(4):
                                mm = product(pe, ps[:, bank, :], XTE, 4 * half + kt, [v[:, kt, :] for v in w],
                                             half == 0 and kt == 0, half == 1 and kt == 3)
                            mm.then_inc(done if half else m_half, 1)
                        if u == 0 and c >= 1:
                            turn(i, c - 1)
                    if c >= 1:
                        down_chunk(i, c - 1)
                    if c == 0:
                        pe.wait_ge(m_yc, i + 1)
                        scatter(0, 7).then_inc(m_sct, 1)
                    elif c < 4:
                        pe.wait_ge(m_sc, 4 * i + c)
                        scatter(c, 7).then_inc(m_sct, 1)
                    elif c == 4:
                        pe.wait_ge(m_sc, 4 * i + 4)
                        pe.wait_ge(m_sel, i + 1)
                        for t in range(TT):
                            mm = nc.tensor.transpose(ps[:, 7, t * P:(t + 1) * P], M_selg[:, t, :], ident[:, :])
                        mm.then_inc(m_tr, 1)
                    elif c == 5:
                        pe.wait_ge(m_st, i + 1)
                        pe.wait_ge(m_sel, i + 2)
                        gather(pe, 0)
                turn(i, CE - 1)
                pe.wait_ge(m_v, 2 * i + 3)
                gather(pe, 1)
                down_chunk(i, CE - 1)
            pe.wait_ge(m_v, n * (2 * NE) + 2)
            pe.wait_ge(m_yc, n * NE + 1)
            for r, bank in enumerate((7, 0, 1, 2)):
                scatter(r, bank).then_inc(m_sct, 1)

        def M_scalar(act, step):
            for k in range(2):
                split_high(act, 0, unit_of[0, 0, k])
            norm_scalar(act, 7)
            act.wait_ge(m_top, 1)
            nc.scalar.activation(M_w[:, 1], M_w[:, 1], ACT.Exp).then_inc(m_ex, 1)
            act.wait_ge(m_route, 1)
            n = act.value_load(nblk[0:1, 0:1], min_val=1, max_val=2)

            def turned_high(i, c):
                act.wait_ge(m_tt, 7 * i + (c + 1))
                nc.scalar.activation(M_hT[:, c % 2, 0].rearrange("p f j -> p (f j)"), ps[:, 4, :], ACT.Copy).then_inc(m_hh, 1)

            def tokens_high():
                nc.scalar.activation(XTE[:, 0], M_v, ACT.Copy).then_inc(m_xh, 1)

            def result():
                nc.scalar.activation(M_y.rearrange("p (h n) -> p h n", h=2), ps[:, 5:7, :], ACT.Copy).then_inc(m_yc, 1)

            act.wait_ge(m_v, 2)
            tokens_high()
            with act.Fori(0, n * NE) as i:
                act.wait_ge(m_dn, 7 * i + 1)
                result()
                for c in range(CE):
                    ahead = [unit_of[1, c, 0], unit_of[1, c, 1]]
                    if c >= 1:
                        ahead.append(unit_of[2, c - 1, 0])
                    for k in ahead:
                        split_high(act, i, k)
                    if c == 5:
                        act.wait_ge(m_tr, i + 1)
                        nc.scalar.activation(M_selT, ps[:, 7, 0:SEQ], ACT.Copy).then_inc(m_st, 1)
                    if c >= 1:
                        turned_high(i, c - 1)
                        split_high(act, i, unit_of[2, c - 1, 1])
                    if c + 1 < CE:
                        split_high(act, i, unit_of[0, c + 1, 0])
                    act.wait_ge(m_g, 7 * i + (c + 1))
                    act.wait_ge(s_h, 7 * i + (B_M + c - (c > 0)) if c != 1 else 7 * i + (B_M - 1))
                    nc.scalar.activation(M_sg[:, c % 2, :], ps[:, c % 2, :], ACT.Silu).then_inc(s_sg, 1)
                    if c + 1 < CE:
                        split_high(act, i, unit_of[0, c + 1, 1])
                for k in range(2):
                    split_high(act, i, unit_of[2, CE - 1, k])
                turned_high(i, CE - 1)
                for k in range(2):
                    split_high(act, i, NU + unit_of[0, 0, k])
                act.wait_ge(m_v, 2 * i + 4)
                act.wait_ge(s_gu, 7 * i + (B_M + 7))
                tokens_high()
            act.wait_ge(m_dn, n * (7 * NE) + 1)
            result()

        def M_vector(dve, step):
            for k in range(2):
                split_low(dve, 0, unit_of[0, 0, k])
            norm_vector(dve, step, 7)
            nc.vector.memset(M_selT, 0.0).then_inc(m_ht, 1)
            dve.wait_ge(m_lg, 1)
            step.link(nc.vector.tensor_copy(LOGIT, ps[:, 4, 0:TT * NE].rearrange("p (t e) -> p t e", t=TT)))
            src = LOGIT
            for k, onehot in enumerate((OH0, OH1)):
                step.link(nc.vector.tensor_reduce(M_top[:, k], src, AX.X, ALU.max))
                if k == 1:
                    nc.vector.tensor_tensor(M_w[:, 1], M_top[:, 1], M_top[:, 0], ALU.subtract).then_inc(m_top, 1)
                step.link(nc.vector.tensor_tensor(onehot, src, M_top[:, k].to_broadcast([P, TT, NE]), ALU.is_equal))
                for t in range(TT):
                    ins = nc.vector.tensor_tensor_scan(CUM[:, t, :], onehot[:, t, :], onehot[:, t, :], 0.0, ALU.add, ALU.bypass)
                step.link(ins)
                step.link(nc.vector.scalar_tensor_tensor(onehot, CUM, 1.0, onehot, ALU.is_equal, ALU.mult))
                if k == 0:
                    step.link(nc.vector.scalar_tensor_tensor(TMP, OH0, -MASKED, LOGIT, ALU.mult, ALU.add))
                    src = TMP
            nc.vector.tensor_tensor(MASK, OH0, OH1, ALU.add).then_inc(m_mask, 1)
            dve.wait_ge(m_ex, 1)
            step.link(nc.vector.tensor_scalar(M_w[:, 0], M_w[:, 1], 1.0, None, ALU.add))
            step.link(nc.vector.reciprocal(M_w[:, 0], M_w[:, 0]))
            step.link(nc.vector.tensor_tensor(M_w[:, 1], M_w[:, 1], M_w[:, 0], ALU.mult))
            for k, onehot in enumerate((OH0, OH1)):
                ins = nc.vector.tensor_tensor(onehot, onehot, M_w[:, k].to_broadcast([P, TT, NE]), ALU.mult)
            step.link(ins)
            step.link(nc.vector.tensor_tensor(GATE, OH0, OH1, ALU.add))
            dve.wait_ge(m_pos, 1)
            step.link(nc.vector.tensor_reduce(M_cnt[0:1, 0:1], ps[0:1, 5, 2 * NE:3 * NE], AX.X, ALU.max))
            step.link(nc.vector.tensor_scalar(nblk[0:1, 0:1], M_cnt[0:1, 0:1], float(CAP), 1.0, ALU.is_gt, ALU.add))
            nc.vector.scalar_tensor_tensor(POS, ps[:, 5, 0:2 * NE].rearrange("p (t e) -> p t e", t=TT), 1.0, MASK,
                                           ALU.add, ALU.mult).then_inc(m_route, 1)
            dve.wait_ge(m_route, 1)
            step.link(nc.vector.tensor_scalar(POS, POS, -1.0, None, ALU.add))
            n = dve.value_load(nblk[0:1, 0:1], min_val=1, max_val=2)

            def select(e, b):
                for v, scale in ((M_selg, True), (M_sel, False)):
                    for t in range(TT):
                        ins = nc.vector.tensor_scalar(v[:, t, :], iota_j[:, bass.ds(b * CAP, CAP)] if not isinstance(b, int) else
                                                      iota_j[:, b * CAP:(b + 1) * CAP],
                                                      POS[:, t, bass.ds(e, 1)], GATE[:, t, bass.ds(e, 1)] if scale else None,
                                                      ALU.is_equal, *((ALU.mult,) if scale else ()))
                ins.then_inc(m_sel, 1)

            def gathered(half):
                g = column("moe_norm", 4 * half, 4).rearrange("p (k o) -> p k o", o=1).to_broadcast([P, 4, CAP])
                nc.vector.tensor_tensor(M_v[:, 4 * half:4 * half + 4, :], ps[:, 7, :].rearrange("p (k j) -> p k j", k=4), g,
                                        ALU.mult).then_inc(m_v, 1)

            def tokens_low():
                nc.vector.tensor_tensor(XTE[:, 1], M_v, XTE[:, 0], ALU.subtract).then_inc(m_xt, 1)

            def turned_low(i, c):
                dve.wait_ge(m_hh, 7 * i + (c + 1))
                high = M_hT[:, c % 2, 0].rearrange("p f j -> p (f j)")
                nc.vector.tensor_tensor(M_hT[:, c % 2, 1].rearrange("p f j -> p (f j)"), ps[:, 4, :], high, ALU.subtract)\
                    .then_inc(m_ht, 1)

            def scattered(r, bank, done):
                x = X[:, r // 2, r % 2 * 512:(r % 2 + 1) * 512]
                nc.vector.tensor_tensor(x, x, ps[:, bank, :], ALU.add).then_inc(done, 1)

            select(0, 0)
            for half in range(2):
                dve.wait_ge(m_ga, half + 1)
                gathered(half)
            dve.wait_ge(m_xh, 1)
            tokens_low()
            with dve.Fori(0, n * NE) as i:
                for c in range(CE):
                    for k in range(2):
                        split_low(dve, i, unit_of[1, c, k])
                    if 1 <= c < 5:
                        dve.wait_ge(m_sct, 4 * i + c)
                        scattered(c - 1, 7, m_sc)
                    elif c == 5:
                        dve.wait_ge(m_tr, i + 1)
                        select((i + 1) & (NE - 1), (i + 1) >> 3)
                    elif c == 6:
                        dve.wait_ge(m_ga, 2 * i + 3)
                        gathered(0)
                    if c >= 1:
                        split_low(dve, i, unit_of[2, c - 1, 0])
                        turned_low(i, c - 1)
                        split_low(dve, i, unit_of[2, c - 1, 1])
                    if c + 1 < CE:
                        for k in range(2):
                            split_low(dve, i, unit_of[0, c + 1, k])
                    else:
                        split_low(dve, i, unit_of[2, CE - 1, 0])
                    dve.wait_ge(s_gu, 7 * i + (B_M + c + 1))
                    dve.wait_ge(s_sg, 7 * i + (B_M + c + 1))
                    nc.vector.tensor_tensor(M_h[:, c % 2, :], M_sg[:, c % 2, :], ps[:, 2 + c % 2, :], ALU.mult).then_inc(s_h, 1)
                split_low(dve, i, unit_of[2, CE - 1, 1])
                turned_low(i, CE - 1)
                split_low(dve, i, NU + unit_of[0, 0, 0])
                dve.wait_ge(m_ga, 2 * i + 4)
                gathered(1)
                split_low(dve, i, NU + unit_of[0, 0, 1])
                dve.wait_ge(m_xh, i + 2)
                tokens_low()
            for r, bank in enumerate((7, 0, 1, 2)):
                dve.wait_ge(m_sct, n * (4 * NE) + (r + 1))
                scattered(r, bank, s_x if r % 2 else m_sc)


        @block.sync
        def _(sp):
            sp.dma_start(X, a["x"][0].rearrange("(t p) d -> p t d", p=P)).then_inc(x_in, 16)
            for j, item in enumerate(stream):
                if j == 1:
                    sp.wait_ge(rows_in, 16 * len(row_loads))
                if isinstance(item, dict):
                    ffn_sync(sp, item)
                    continue
                s, pairs, used = item
                if used:
                    sp.wait_ge(*used)
                for dst, src in pairs:
                    sp.dma_start(dst, src).then_inc(landed[s], 16)
            def expert_load(e, k):
                (kind, c), half = M_loads[k // 2], k % 2
                one = lambda w: w[0][bass.ds(e, 1)] if not isinstance(e, int) else w[0][e:e + 1]
                dst = ring[:, slot_of(k), 0:2048]
                if kind < 2:
                    w = one(a[("moe_w_gate_2", "moe_w_up_2")[kind]])
                    src = w.rearrange("o (k p) n -> p (o k) n", p=P)[:, 4 * half:4 * half + 4, c * 512:(c + 1) * 512]
                    dst = dst.rearrange("p (k n) -> p k n", n=512)
                else:
                    r = 4 * c + 2 * half
                    src = one(a["moe_w_down_2"]).rearrange("o (r p) n -> p (o r) n", p=P)[:, r:r + 2, :]
                    dst = dst.rearrange("p (r n) -> p r n", n=D)
                sp.dma_start(dst, src).then_inc(landed[slot_of(k)], 16)

            def used(k, i, items_back=0):
                kind, c = M_loads[k // 2]
                if k % 2 == 0:
                    sp.wait_ge(m_half, (NU // 2) * i + (k // 2 + 1 - items_back * NU // 2))
                else:
                    done, base = ((m_g, 0), (s_gu, B_M), (m_dn, 1))[kind]
                    sp.wait_ge(done, 7 * i + (base + c + 1 - 7 * items_back))

            for k in range(NU):
                if k < NS_EARLY:
                    sp.wait_ge(*freed[slot_of(k)])
                elif k < NS:
                    sp.wait_ge(s_y, 14)
                else:
                    used(k - NS, 0)
                expert_load(0, k)
            for k in range(2):
                used(k + NU - NS, 0)
                expert_load(1, k)
            sp.wait_ge(m_route, 1)
            n = sp.value_load(nblk[0:1, 0:1], min_val=1, max_val=2)
            with sp.Fori(1, n * NE) as i:
                expert = sp.snap(sp.to_reg(i & (NE - 1)))
                expert_next = sp.snap(sp.to_reg((i + 1) & (NE - 1)))
                for k in range(2, NU):
                    if k < NS:
                        used(k + NU - NS, i, 1)
                    else:
                        used(k - NS, i)
                    expert_load(expert, k)
                for k in range(2):
                    used(k + NU - NS, i)
                    expert_load(expert_next, k)
            out_v = out[0].rearrange("(t p) d -> p t d", p=P)
            for t in range(TT):
                sp.wait_ge(s_x, 15 + t)
                sp.dma_start(out_v[:, t, :], X[:, t, :]).then_inc(s_out, 16)
            sp.wait_ge(s_out, 16 * TT)

        @block.gpsimd
        def _(pool):
            step = Steps(pool, pool_step)
            bias = a["attn_rel_bias"]
            setup_gpsimd_first(pool, step)
            norm_gpsimd(pool, step, 0)
            setup_gpsimd(pool, step)
            pool.dma_start(gpost[:, :], a["norm_mix_post"][0].partition_broadcast(P)).then_inc(gpost_in, 16)
            pool.dma_start(A_bias, bass.AP(tensor=bias.tensor, offset=1,
                                           ap=[[1, P], [2 * REL_CLIP + 1, N_HEADS_A], [1, KEYS]])).then_inc(side_in, 16)
            posts = ["norm_mix_post", "norm_ffn_post"]
            for k in range(1, 8):
                norm_gpsimd(pool, step, k)
                if k <= 3:
                    pool.dma_start(gpost[:, :], a[posts[k % 2]][k // 2].partition_broadcast(P)).then_inc(gpost_in, 16)

        @block.scalar
        def _(act):
            step = Steps(act, act_step)
            setup_loads(act, row_loads[:EARLY_ROWS])
            A_scalar(act, step)
            F_scalar(act, 0)
            R_scalar(act, step)
            F_scalar(act, 1)
            E_scalar(act, step)
            F_scalar(act, 2)
            G_scalar(act, step)
            M_scalar(act, step)

        @block.vector
        def _(dve):
            step = Steps(dve, dve_step)
            setup_vector(dve, step)
            A_vector(dve, step)
            F_vector(dve, step, 0)
            R_vector(dve, step)
            F_vector(dve, step, 1)
            E_vector(dve, step)
            F_vector(dve, step, 2)
            G_vector(dve, step)
            M_vector(dve, step)

        @block.tensor
        def _(pe):
            A_tensor(pe)
            F_tensor(pe, 0)
            R_tensor(pe)
            F_tensor(pe, 1)
            E_tensor(pe)
            F_tensor(pe, 2)
            G_tensor(pe)
            M_tensor(pe)


def kernel(**inputs):
    import numpy as _np
    import concourse.bacc as _bacc
    from concourse import mybir as _mybir
    from concourse.bass_utils import run_bass_kernel_spmd as _run

    nc = _bacc.Bacc("TRN2", target_bir_lowering=False, num_devices=1)
    arrays, args = {}, {}
    for name in inputs:
        v = _np.ascontiguousarray(inputs[name])
        arrays[f"in_{name}"] = v
        args[name] = nc.dram_tensor(f"in_{name}", v.shape, _mybir.dt.from_np(v.dtype), kind="ExternalInput").ap()
    out = nc.dram_tensor("out", (1, SEQ, D), F32, kind="ExternalOutput").ap()
    build(nc, args, out)
    return _run(nc, [arrays], core_ids=[0]).results[0]["out"]
```
